# Optimizing a Trainium2 kernel written in Bass

```python
import math
import jax
import jax.numpy as jnp
from jax import lax
import numpy as np
import jax, jax.numpy as jnp

D_MODEL = 1024
BATCH = 1
SEQ = 256
DEPTH = 2

CHUNK = 64
Q_BLOCK = 128
D_MIX = D_MODEL
D_FF = 2816
CONV_K = 4
EPS = 1e-6
ROPE_THETA = 10000.0

GDN_HEADS = 4
GDN_DK = 64
GDN_DV = 64
GDN_QK_W = GDN_HEADS * GDN_DK
GDN_W = GDN_HEADS * GDN_DV

DIFF_HEADS = 4
DIFF_DH = 32
DIFF_DV = 2 * DIFF_DH
DIFF_QK_W = 2 * DIFF_HEADS * DIFF_DH
DIFF_W = DIFF_HEADS * DIFF_DV

SSD_HEADS = 4
SSD_P = 64
SSD_N = 128
SSD_G = 2
SSD_W = SSD_HEADS * SSD_P

MLSTM_HEADS = 4
MLSTM_DH = 64
MLSTM_W = MLSTM_HEADS * MLSTM_DH

IN_SPLITS = (GDN_QK_W, GDN_QK_W, GDN_W, GDN_W, GDN_HEADS, GDN_HEADS,
             DIFF_QK_W, DIFF_QK_W, DIFF_W,
             SSD_W, SSD_W + 2 * SSD_G * SSD_N, SSD_HEADS,
             MLSTM_W, MLSTM_W, MLSTM_W, MLSTM_W, MLSTM_HEADS, MLSTM_HEADS)
IN_COLS = sum(IN_SPLITS)


def rmsnorm(x, g):
    xf = x.astype(jnp.float32)
    y = xf * lax.rsqrt(jnp.mean(xf * xf, axis=-1, keepdims=True) + EPS)
    return (y * g.astype(jnp.float32)).astype(x.dtype)

def l2norm(t):
    return t * lax.rsqrt(jnp.sum(t * t, axis=-1, keepdims=True) + EPS)

def swiglu(h, w_gate, w_up, w_down):
    return (jax.nn.silu(h @ w_gate) * (h @ w_up)) @ w_down

def causal_dwconv(u, w):
    ch = u.shape[-1]
    return lax.conv_general_dilated(u, w.astype(u.dtype)[:, None, :], window_strides=(1,),
                                    padding=[(CONV_K - 1, 0)],
                                    dimension_numbers=('NWC', 'WIO', 'NWC'),
                                    feature_group_count=ch)

def causal_tril():
    return jnp.tril(jnp.ones((CHUNK, CHUNK), dtype=bool))

def masked_decay(cum):
    diff = cum[..., :, None] - cum[..., None, :]
    return jnp.exp(jnp.where(causal_tril(), diff, -jnp.inf))

def heads_to_chunks(t):
    b, s = t.shape[:2]
    t = t.reshape((b, s // CHUNK, CHUNK) + t.shape[2:])
    perm = (1, 0, 3, 2) + tuple(range(4, t.ndim))
    return t.transpose(perm)

def chunks_to_heads(t):
    n, b, h, c, d = t.shape
    return t.transpose(1, 0, 3, 2, 4).reshape(b, n * c, h, d)

def rope_tables(seq, dim):
    inv_freq = ROPE_THETA ** (-jnp.arange(0, dim, 2, dtype=jnp.float32) / dim)
    ang = jnp.arange(seq, dtype=jnp.float32)[:, None] * inv_freq[None, :]
    return jnp.cos(ang), jnp.sin(ang)

def apply_rope(t, cos, sin):
    half = t.shape[-1] // 2
    t1, t2 = t[..., :half], t[..., half:]
    c, s = cos[None, :, None, :], sin[None, :, None, :]
    return jnp.concatenate([t1 * c - t2 * s, t2 * c + t1 * s], axis=-1)

def gated_deltanet(q, k, v, gate, beta_raw, a_raw, conv_w, a_log, dt_bias, norm_g):
    bsz, seq, _ = q.shape
    qkv = jax.nn.silu(causal_dwconv(jnp.concatenate([q, k, v], axis=-1), conv_w))
    q, k, v = jnp.split(qkv, [GDN_QK_W, 2 * GDN_QK_W], axis=-1)
    q = l2norm(q.reshape(bsz, seq, GDN_HEADS, GDN_DK)) * (GDN_DK ** -0.5)
    k = l2norm(k.reshape(bsz, seq, GDN_HEADS, GDN_DK))
    v = v.reshape(bsz, seq, GDN_HEADS, GDN_DV)
    beta = jax.nn.sigmoid(beta_raw)
    g = -jnp.exp(a_log) * jax.nn.softplus(a_raw + dt_bias)
    qc, kc, vc = heads_to_chunks(q), heads_to_chunks(k), heads_to_chunks(v)
    gc = jnp.cumsum(heads_to_chunks(g), axis=-1)
    bc = heads_to_chunks(beta)[..., None]
    decay = masked_decay(gc)
    eye = jnp.eye(CHUNK, dtype=jnp.float32)
    kb = kc * bc
    lower = jnp.einsum('nbhcd,nbhmd->nbhcm', kb, kc) * decay * (1.0 - eye)
    t_mat = lax.linalg.triangular_solve(eye + lower, jnp.broadcast_to(eye, lower.shape),
                                        left_side=True, lower=True, unit_diagonal=True)
    u = t_mat @ (vc * bc)
    w = t_mat @ (kb * jnp.exp(gc)[..., None])
    attn = jnp.einsum('nbhcd,nbhmd->nbhcm', qc, kc) * decay
    q_dec = qc * jnp.exp(gc)[..., None]
    k_dec = kc * jnp.exp(gc[..., -1:] - gc)[..., None]
    g_last = jnp.exp(gc[..., -1])

    def step(state, inp):
        q_i, k_i, u_i, w_i, a_i, gl_i = inp
        v_new = u_i - w_i @ state
        o_i = q_i @ state + a_i @ v_new
        state = state * gl_i[..., None, None] + jnp.einsum('bhcd,bhce->bhde', k_i, v_new)
        return state, o_i

    s0 = jnp.zeros((bsz, GDN_HEADS, GDN_DK, GDN_DV), jnp.float32)
    _, o = lax.scan(step, s0, (q_dec, k_dec, u, w, attn, g_last))
    o = chunks_to_heads(o)
    o = rmsnorm(o, norm_g) * jax.nn.silu(gate.reshape(bsz, seq, GDN_HEADS, GDN_DV))
    return o.reshape(bsz, seq, GDN_W)

def diff_attention(q, k, v, lam_q1, lam_k1, lam_q2, lam_k2, norm_g, lambda_init, cos, sin):
    bsz, seq, _ = q.shape
    q = apply_rope(q.reshape(bsz, seq, 2 * DIFF_HEADS, DIFF_DH), cos, sin)
    k = apply_rope(k.reshape(bsz, seq, 2 * DIFF_HEADS, DIFF_DH), cos, sin)
    v = v.reshape(bsz, seq, DIFF_HEADS, DIFF_DV)
    lam = (jnp.exp(jnp.sum(lam_q1 * lam_k1)) - jnp.exp(jnp.sum(lam_q2 * lam_k2))
           + lambda_init).astype(jnp.float32)
    nb = seq // Q_BLOCK
    qb = q.reshape(bsz, nb, Q_BLOCK, 2 * DIFF_HEADS, DIFF_DH).transpose(1, 0, 3, 2, 4) * (DIFF_DH ** -0.5)
    kt = k.transpose(0, 2, 1, 3)
    vt = v.transpose(0, 2, 1, 3)
    key_chunk = jnp.arange(seq) // CHUNK

    def block(args):
        q_blk, blk = args
        scores = jnp.einsum('bhqd,bhkd->bhqk', q_blk, kt)
        q_chunk = (blk * Q_BLOCK + jnp.arange(Q_BLOCK)) // CHUNK
        allowed = key_chunk[None, :] <= q_chunk[:, None]
        p = jax.nn.softmax(jnp.where(allowed, scores, -jnp.inf), axis=-1)
        p = p.reshape(bsz, DIFF_HEADS, 2, Q_BLOCK, seq)
        return jnp.einsum('bhqk,bhkd->bhqd', p[:, :, 0] - lam * p[:, :, 1], vt)

    o = lax.map(block, (qb, jnp.arange(nb)))
    o = o.transpose(1, 0, 3, 2, 4).reshape(bsz, seq, DIFF_HEADS, DIFF_DV)
    o = rmsnorm(o, norm_g) * (1.0 - lambda_init)
    return o.reshape(bsz, seq, DIFF_W)

def ssd_mixer(z, xbc, dt_raw, conv_w, conv_b, a_log, dt_bias, d_skip, norm_g):
    bsz, seq, _ = z.shape
    xbc = jax.nn.silu(causal_dwconv(xbc, conv_w) + conv_b)
    xs, bm, cm = jnp.split(xbc, [SSD_W, SSD_W + SSD_G * SSD_N], axis=-1)
    x = xs.reshape(bsz, seq, SSD_HEADS, SSD_P)
    rep = SSD_HEADS // SSD_G
    bm = jnp.repeat(bm.reshape(bsz, seq, SSD_G, SSD_N), rep, axis=2)
    cm = jnp.repeat(cm.reshape(bsz, seq, SSD_G, SSD_N), rep, axis=2)
    dt = jax.nn.softplus(dt_raw + dt_bias)
    da = dt * (-jnp.exp(a_log))
    nch = seq // CHUNK
    xc = (x * dt[..., None]).reshape(bsz, nch, CHUNK, SSD_HEADS, SSD_P)
    bc = bm.reshape(bsz, nch, CHUNK, SSD_HEADS, SSD_N)
    cc = cm.reshape(bsz, nch, CHUNK, SSD_HEADS, SSD_N)
    acs = jnp.cumsum(da.reshape(bsz, nch, CHUNK, SSD_HEADS).transpose(0, 3, 1, 2), axis=-1)
    l_mat = masked_decay(acs)
    y_diag = jnp.einsum('bclhn,bcmhn,bhclm,bcmhp->bclhp', cc, bc, l_mat, xc)
    decay_states = jnp.exp(acs[..., -1:] - acs)
    states = jnp.einsum('bclhn,bhcl,bclhp->bchpn', bc, decay_states, xc)

    def step(st, inp):
        s_c, d_c = inp
        return st * d_c[..., None, None] + s_c, st

    s0 = jnp.zeros((bsz, SSD_HEADS, SSD_P, SSD_N), jnp.float32)
    _, prev = lax.scan(step, s0, (states.transpose(1, 0, 2, 3, 4),
                                  jnp.exp(acs[..., -1]).transpose(2, 0, 1)))
    prev = prev.transpose(1, 0, 2, 3, 4)
    y_off = jnp.einsum('bclhn,bchpn,bhcl->bclhp', cc, prev, jnp.exp(acs))
    y = (y_diag + y_off).reshape(bsz, seq, SSD_HEADS, SSD_P) + x * d_skip[:, None]
    y = y.reshape(bsz, seq, SSD_W) * jax.nn.silu(z)
    gw = SSD_W // SSD_G
    y = rmsnorm(y.reshape(bsz, seq, SSD_G, gw), norm_g.reshape(SSD_G, gw))
    return y.reshape(bsz, seq, SSD_W)

def mlstm(q, k, v, o_raw, i_raw, f_raw, i_bias, f_bias, norm_g):
    bsz, seq, _ = q.shape
    shp = (bsz, seq, MLSTM_HEADS, MLSTM_DH)
    qc = heads_to_chunks(q.reshape(shp))
    kc = heads_to_chunks(k.reshape(shp) * (MLSTM_DH ** -0.5))
    vc = heads_to_chunks(v.reshape(shp))
    li = heads_to_chunks(i_raw + i_bias)
    lf = heads_to_chunks(jax.nn.log_sigmoid(f_raw + f_bias))
    b = jnp.cumsum(lf, axis=-1)
    d_log = jnp.where(causal_tril(), b[..., :, None] - b[..., None, :] + li[..., None, :], -jnp.inf)
    d_max = jnp.max(d_log, axis=-1)
    qk = jnp.einsum('nbhcd,nbhmd->nbhcm', qc, kc)
    g_end = b[..., -1:] - b + li

    def step(carry, inp):
        c_st, n_st, m_st = carry
        q_i, k_i, v_i, b_i, dl_i, dm_i, qk_i, ge_i = inp
        m_t = jnp.maximum(b_i + m_st[..., None], dm_i)
        w_st = jnp.exp(b_i + m_st[..., None] - m_t)
        s_i = qk_i * jnp.exp(dl_i - m_t[..., None])
        num = w_st[..., None] * (q_i @ c_st) + s_i @ v_i
        den = w_st * jnp.einsum('bhcd,bhd->bhc', q_i, n_st) + jnp.sum(s_i, axis=-1)
        h_i = num / jnp.maximum(jnp.abs(den), jnp.exp(-m_t))[..., None]
        m_new = jnp.maximum(b_i[..., -1] + m_st, jnp.max(ge_i, axis=-1))
        w_old = jnp.exp(b_i[..., -1] + m_st - m_new)
        k_w = k_i * jnp.exp(ge_i - m_new[..., None])[..., None]
        c_st = c_st * w_old[..., None, None] + jnp.einsum('bhcd,bhce->bhde', k_w, v_i)
        n_st = n_st * w_old[..., None] + jnp.sum(k_w, axis=-2)
        return (c_st, n_st, m_new), h_i

    init = (jnp.zeros((bsz, MLSTM_HEADS, MLSTM_DH, MLSTM_DH), jnp.float32),
            jnp.zeros((bsz, MLSTM_HEADS, MLSTM_DH), jnp.float32),
            jnp.zeros((bsz, MLSTM_HEADS), jnp.float32))
    _, h = lax.scan(step, init, (qc, kc, vc, b, d_log, d_max, qk, g_end))
    h = chunks_to_heads(h) * jax.nn.sigmoid(o_raw.reshape(shp))
    h = rmsnorm(h, norm_g.reshape(MLSTM_HEADS, MLSTM_DH))
    return h.reshape(bsz, seq, MLSTM_W)

def hybrid_mixer(h, w_in, w_out, gdn_conv_w, gdn_a_log, gdn_dt_bias, gdn_norm_g,
                 diff_lam_q1, diff_lam_k1, diff_lam_q2, diff_lam_k2, diff_norm_g,
                 ssd_conv_w, ssd_conv_b, ssd_a_log, ssd_dt_bias, ssd_d, ssd_norm_g,
                 mlstm_i_bias, mlstm_f_bias, mlstm_norm_g, lambda_init, cos, sin):
    proj = (h @ w_in).astype(jnp.float32)
    points = np.cumsum(np.array(IN_SPLITS))[:-1].tolist()
    (a_q, a_k, a_v, a_g, a_beta, a_a,
     b_q, b_k, b_v,
     c_z, c_xbc, c_dt,
     d_q, d_k, d_v, d_o, d_i, d_f) = jnp.split(proj, points, axis=-1)
    out_a = gated_deltanet(a_q, a_k, a_v, a_g, a_beta, a_a, gdn_conv_w, gdn_a_log, gdn_dt_bias, gdn_norm_g)
    out_b = diff_attention(b_q, b_k, b_v, diff_lam_q1, diff_lam_k1, diff_lam_q2, diff_lam_k2,
                           diff_norm_g, lambda_init, cos, sin)
    out_c = ssd_mixer(c_z, c_xbc, c_dt, ssd_conv_w, ssd_conv_b, ssd_a_log, ssd_dt_bias, ssd_d, ssd_norm_g)
    out_d = mlstm(d_q, d_k, d_v, d_o, d_i, d_f, mlstm_i_bias, mlstm_f_bias, mlstm_norm_g)
    mixed = jnp.concatenate([out_a, out_b, out_c, out_d], axis=-1)
    return mixed.astype(h.dtype) @ w_out

def first_inputs(seed: int = 0) -> dict:
    key = jax.random.key(seed)
    keys = list(jax.random.split(key, 48))
    f32 = jnp.float32
    L = DEPTH

    def nxt():
        return keys.pop()

    def normal(shape, scale):
        return jax.random.normal(nxt(), shape, f32) * scale

    def gain(n):
        return 1.0 + normal((L, n), 0.02)

    def a_log_init(n):
        return jnp.log(jax.random.uniform(nxt(), (L, n), f32, 1.0, 16.0))

    def dt_bias_init(n):
        dt = jnp.exp(jax.random.uniform(nxt(), (L, n), f32, math.log(1e-3), math.log(1e-1)))
        return dt + jnp.log(-jnp.expm1(-dt))

    xbc_w = SSD_W + 2 * SSD_G * SSD_N
    return {
        'x': normal((BATCH, SEQ, D_MODEL), 1.0),
        'ffn1_pre_g': gain(D_MODEL),
        'ffn1_w_gate': normal((L, D_MODEL, D_FF), D_MODEL ** -0.5),
        'ffn1_w_up': normal((L, D_MODEL, D_FF), D_MODEL ** -0.5),
        'ffn1_w_down': normal((L, D_FF, D_MODEL), D_FF ** -0.5),
        'ffn1_post_g': gain(D_MODEL),
        'mix_pre_g': gain(D_MODEL),
        'w_in': normal((L, D_MODEL, IN_COLS), D_MODEL ** -0.5),
        'gdn_conv_w': normal((L, CONV_K, 2 * GDN_QK_W + GDN_W), CONV_K ** -0.5),
        'gdn_a_log': a_log_init(GDN_HEADS),
        'gdn_dt_bias': dt_bias_init(GDN_HEADS),
        'gdn_norm_g': gain(GDN_DV),
        'diff_lam_q1': normal((L, DIFF_DH), 0.1),
        'diff_lam_k1': normal((L, DIFF_DH), 0.1),
        'diff_lam_q2': normal((L, DIFF_DH), 0.1),
        'diff_lam_k2': normal((L, DIFF_DH), 0.1),
        'diff_norm_g': gain(DIFF_DV),
        'ssd_conv_w': normal((L, CONV_K, xbc_w), CONV_K ** -0.5),
        'ssd_conv_b': normal((L, xbc_w), 0.02),
        'ssd_a_log': a_log_init(SSD_HEADS),
        'ssd_dt_bias': dt_bias_init(SSD_HEADS),
        'ssd_d': 1.0 + normal((L, SSD_HEADS), 0.1),
        'ssd_norm_g': gain(SSD_W),
        'mlstm_i_bias': normal((L, MLSTM_HEADS), 0.1),
        'mlstm_f_bias': jnp.linspace(3.0, 6.0, MLSTM_HEADS, dtype=f32)[None, :] + normal((L, MLSTM_HEADS), 0.1),
        'mlstm_norm_g': gain(MLSTM_W),
        'w_out': normal((L, D_MIX, D_MODEL), D_MIX ** -0.5),
        'mix_post_g': gain(D_MODEL),
        'ffn2_pre_g': gain(D_MODEL),
        'ffn2_w_gate': normal((L, D_MODEL, D_FF), D_MODEL ** -0.5),
        'ffn2_w_up': normal((L, D_MODEL, D_FF), D_MODEL ** -0.5),
        'ffn2_w_down': normal((L, D_FF, D_MODEL), D_FF ** -0.5),
        'ffn2_post_g': gain(D_MODEL),
    }

def first_block(x, ffn1_pre_g, ffn1_w_gate, ffn1_w_up, ffn1_w_down, ffn1_post_g,
              mix_pre_g, w_in,
              gdn_conv_w, gdn_a_log, gdn_dt_bias, gdn_norm_g,
              diff_lam_q1, diff_lam_k1, diff_lam_q2, diff_lam_k2, diff_norm_g,
              ssd_conv_w, ssd_conv_b, ssd_a_log, ssd_dt_bias, ssd_d, ssd_norm_g,
              mlstm_i_bias, mlstm_f_bias, mlstm_norm_g,
              w_out, mix_post_g,
              ffn2_pre_g, ffn2_w_gate, ffn2_w_up, ffn2_w_down, ffn2_post_g):
    cos, sin = rope_tables(x.shape[1], DIFF_DH)
    for l in range(DEPTH):
        lambda_init = 0.8 - 0.6 * math.exp(-0.3 * l)
        h = rmsnorm(x, ffn1_pre_g[l])
        x = x + 0.5 * rmsnorm(swiglu(h, ffn1_w_gate[l], ffn1_w_up[l], ffn1_w_down[l]), ffn1_post_g[l])
        h = rmsnorm(x, mix_pre_g[l])
        m = hybrid_mixer(h, w_in[l], w_out[l],
                         gdn_conv_w[l], gdn_a_log[l], gdn_dt_bias[l], gdn_norm_g[l],
                         diff_lam_q1[l], diff_lam_k1[l], diff_lam_q2[l], diff_lam_k2[l], diff_norm_g[l],
                         ssd_conv_w[l], ssd_conv_b[l], ssd_a_log[l], ssd_dt_bias[l], ssd_d[l], ssd_norm_g[l],
                         mlstm_i_bias[l], mlstm_f_bias[l], mlstm_norm_g[l],
                         lambda_init, cos, sin)
        x = x + rmsnorm(m, mix_post_g[l])
        h = rmsnorm(x, ffn2_pre_g[l])
        x = x + 0.5 * rmsnorm(swiglu(h, ffn2_w_gate[l], ffn2_w_up[l], ffn2_w_down[l]), ffn2_post_g[l])
    return x


_first_inputs = first_inputs


def first_inputs(seed=0):
    import zlib

    import numpy as np

    out = dict(_first_inputs(seed))
    spreads = {}
    factors = {'ffn1_post_g': 2.844,
     'gdn_norm_g': 150.432,
     'diff_lam_k1': 3.396,
     'diff_norm_g': 118.388,
     'ssd_conv_b': 3.463,
     'ssd_norm_g': 87.162,
     'mlstm_i_bias': 64.0,
     'mlstm_norm_g': 95.806,
     'ffn2_pre_g': 4.043,
     'ffn2_post_g': 15.197,
     'diff_lam_k2': 2.878,
     'ssd_d': 2.71,
     'mix_post_g': 3.109}
    for name, (base, spread) in spreads.items():
        noise = np.random.default_rng([zlib.crc32(name.encode()), seed]).standard_normal(out[name].shape)
        drawn = base * np.exp(spread * noise) if base else spread * noise
        out[name] = jnp.asarray(drawn.astype(out[name].dtype))
    for name, factor in factors.items():
        out[name] = (out[name] * factor).astype(out[name].dtype)
    return out


_narrow_inputs = first_inputs


def first_inputs(seed=0):
    out = dict(_narrow_inputs(seed))
    wider = {'gdn_norm_g': 3.8, 'diff_norm_g': 3.83, 'ssd_norm_g': 3.78, 'mlstm_norm_g': 3.78}
    for name, times in wider.items():
        mean = out[name].mean()
        out[name] = (mean + times * (out[name] - mean)).astype(out[name].dtype)
    return out


HEAD_DIM = 64
RET_HEADS = 4
RET_DK = 64
RET_DV = 128
DIL_HEADS = 4
SB_HEADS = 4
MIX_WIDTH = RET_HEADS * RET_DV + DIL_HEADS * HEAD_DIM + SB_HEADS * HEAD_DIM
IN_SIZES = (RET_HEADS * RET_DK, RET_HEADS * RET_DK, RET_HEADS * RET_DV, RET_HEADS * RET_DV,
            DIL_HEADS * HEAD_DIM, DIL_HEADS * HEAD_DIM, DIL_HEADS * HEAD_DIM,
            SB_HEADS * HEAD_DIM, SB_HEADS * HEAD_DIM, SB_HEADS * HEAD_DIM)
IN_WIDTH = sum(IN_SIZES)
BLOCK = 128
RET_CHUNK = 128
WINDOWS = (128, 512, 2048)
DILATIONS = (1, 4, 16)
ALPHA = (2.0 * DEPTH) ** 0.25
BETA = (8.0 * DEPTH) ** -0.25
LN_EPS = 1e-5
GN_EPS = 1e-6
FFN_RES = 0.5
N_MOD = 9


def _layer_norm(x, gain, bias):
    xf = x.astype(jnp.float32)
    mu = jnp.mean(xf, -1, keepdims=True)
    var = jnp.mean(jnp.square(xf - mu), -1, keepdims=True)
    y = (xf - mu) * lax.rsqrt(var + LN_EPS)
    return (y * gain.astype(jnp.float32) + bias.astype(jnp.float32)).astype(x.dtype)

def _modulate(x, shift, scale):
    return x * (1.0 + scale) + shift

def _post_norm(x, y, gate, res_w, gain, bias):
    return _layer_norm(ALPHA * x + res_w * (1.0 + gate) * y, gain, bias)

def _swiglu(h, w_gate, w_up, w_down):
    return (jax.nn.silu(h @ w_gate) * (h @ w_up)) @ w_down

def _split_heads(x, n_heads):
    b, s, _ = x.shape
    return x.reshape(b, s, n_heads, -1).transpose(0, 2, 1, 3)

def _merge_heads(x):
    b, h, s, d = x.shape
    return x.transpose(0, 2, 1, 3).reshape(b, s, h * d)

def _rotate(x, inv_freq):
    s, d = x.shape[2], x.shape[3]
    ang = jnp.arange(s, dtype=jnp.float32)[:, None] * inv_freq[None, :]
    cos, sin = jnp.cos(ang), jnp.sin(ang)
    xf = x.astype(jnp.float32)
    x1, x2 = xf[..., : d // 2], xf[..., d // 2:]
    return jnp.concatenate([x1 * cos - x2 * sin, x1 * sin + x2 * cos], -1).astype(x.dtype)

def _retention(q, k, v, g):
    b, h, s, dk = q.shape
    dv = v.shape[-1]
    c = RET_CHUNK
    n = s // c
    log_gamma = jnp.log1p(-jnp.exp2(-5.0 - jnp.arange(h, dtype=jnp.float32)))
    i = jnp.arange(c, dtype=jnp.float32)
    diff = i[:, None] - i[None, :]
    decay_in = jnp.where(diff >= 0, jnp.exp(log_gamma[:, None, None] * jnp.maximum(diff, 0.0)), 0.0)
    xi = jnp.exp(log_gamma[:, None] * (i + 1.0))
    zeta = jnp.exp(log_gamma[:, None] * (c - 1.0 - i))
    gamma_c = jnp.exp(log_gamma * c)
    qc = q.astype(jnp.float32).reshape(b, h, n, c, dk)
    kc = (k.astype(jnp.float32) * dk ** -0.5).reshape(b, h, n, c, dk)
    vc = v.astype(jnp.float32).reshape(b, h, n, c, dv)
    scores = jnp.einsum('bhncd,bhnmd->bhncm', qc, kc) * decay_in[None, :, None]
    o_inner = jnp.einsum('bhncm,bhnme->bhnce', scores, vc)
    kv = jnp.einsum('bhncd,bhnce->bhnde', kc * zeta[None, :, None, :, None], vc)

    def step(state, kv_n):
        return state * gamma_c[None, :, None, None] + kv_n, state

    init = jnp.zeros((b, h, dk, dv), jnp.float32)
    _, prev = lax.scan(step, init, jnp.moveaxis(kv, 2, 0))
    prev = jnp.moveaxis(prev, 0, 2)
    o_cross = jnp.einsum('bhncd,bhnde->bhnce', qc, prev) * xi[None, :, None, :, None]
    o = (o_inner + o_cross).reshape(b, h, s, dv)
    mu = jnp.mean(o, -1, keepdims=True)
    var = jnp.mean(jnp.square(o - mu), -1, keepdims=True)
    o = (o - mu) * lax.rsqrt(var + GN_EPS)
    return jax.nn.silu(g.astype(jnp.float32)) * _merge_heads(o)

def _dilated_attention(q, k, v):
    b, h, s, d = q.shape
    nb = s // BLOCK
    n_keys = max(w // dl for w, dl in zip(WINDOWS, DILATIONS)) + 1
    dist = jnp.array(DILATIONS, jnp.int32)[:, None] * jnp.arange(n_keys, dtype=jnp.int32)[None, :]
    in_win = dist <= jnp.array(WINDOWS, jnp.int32)[:, None]
    qb = (q.astype(jnp.float32) * d ** -0.5).reshape(b, h, nb, BLOCK, d).transpose(2, 0, 1, 3, 4)
    kf = k.astype(jnp.float32)
    vf = v.astype(jnp.float32)

    def block(args):
        q_blk, start = args
        t = start + jnp.arange(BLOCK, dtype=jnp.int32)
        idx = t[:, None, None] - dist[None]
        valid = (idx >= 0) & in_win[None]
        idx = jnp.maximum(idx, 0)
        k_g = jnp.take(kf, idx, axis=2)
        v_g = jnp.take(vf, idx, axis=2)
        sc = jnp.einsum('bhqd,bhqpjd->bhqpj', q_blk, k_g)
        sc = jnp.where(valid, sc, -jnp.inf)
        m = jnp.max(sc, -1)
        e = jnp.exp(sc - m[..., None])
        den = jnp.sum(e, -1)
        o_p = jnp.einsum('bhqpj,bhqpjd->bhqpd', e, v_g) / den[..., None]
        wgt = den * jnp.exp(m - jnp.max(m, -1, keepdims=True))
        wgt = wgt / jnp.sum(wgt, -1, keepdims=True)
        return jnp.einsum('bhqp,bhqpd->bhqd', wgt, o_p)

    out = lax.map(block, (qb, jnp.arange(nb, dtype=jnp.int32) * BLOCK))
    return out.transpose(1, 2, 0, 3, 4).reshape(b, h, s, d)

def _stick_breaking(q, k, v):
    b, h, s, d = q.shape
    nb = s // BLOCK
    qb = (q.astype(jnp.float32) * d ** -0.5).reshape(b, h, nb, BLOCK, d).transpose(2, 0, 1, 3, 4)
    kf = k.astype(jnp.float32)
    vf = v.astype(jnp.float32)
    key_pos = jnp.arange(s, dtype=jnp.int32)

    def block(args):
        q_blk, start = args
        t = start + jnp.arange(BLOCK, dtype=jnp.int32)
        z = jnp.einsum('bhqd,bhsd->bhqs', q_blk, kf)
        causal = key_pos[None, :] < t[:, None]
        log_beta = jax.nn.log_sigmoid(z)
        log_keep = jnp.where(causal, jax.nn.log_sigmoid(-z), 0.0)
        between = lax.cumsum(log_keep, axis=3, reverse=True) - log_keep
        a = jnp.where(causal, jnp.exp(log_beta + between), 0.0)
        return jnp.einsum('bhqs,bhsd->bhqd', a, vf)

    out = lax.map(block, (qb, jnp.arange(nb, dtype=jnp.int32) * BLOCK))
    return out.transpose(1, 2, 0, 3, 4).reshape(b, h, s, d)

def _token_mixer(h, w_in, w_out):
    proj = h @ w_in
    points, acc = [], 0
    for size in IN_SIZES[:-1]:
        acc += size
        points.append(acc)
    rq, rk, rv, rg, dq, dk, dv, sq, sk, sv = jnp.split(proj, points, axis=-1)
    ret_freq = 1.0 / (ROPE_THETA ** jnp.linspace(0.0, 1.0, RET_DK // 2, dtype=jnp.float32))
    rope_freq = 1.0 / (ROPE_THETA ** (jnp.arange(0, HEAD_DIM, 2, dtype=jnp.float32) / HEAD_DIM))
    y_ret = _retention(_rotate(_split_heads(rq, RET_HEADS), ret_freq),
                       _rotate(_split_heads(rk, RET_HEADS), ret_freq),
                       _split_heads(rv, RET_HEADS), rg)
    y_dil = _merge_heads(_dilated_attention(_rotate(_split_heads(dq, DIL_HEADS), rope_freq),
                                            _rotate(_split_heads(dk, DIL_HEADS), rope_freq),
                                            _split_heads(dv, DIL_HEADS)))
    y_sb = _merge_heads(_stick_breaking(_split_heads(sq, SB_HEADS), _split_heads(sk, SB_HEADS),
                                        _split_heads(sv, SB_HEADS)))
    y = jnp.concatenate([y_ret, y_dil, y_sb], -1).astype(h.dtype)
    return y @ w_out

def second_inputs(seed: int = 0) -> dict:
    key = jax.random.key(seed)
    ks = jax.random.split(key, 16)
    f32 = jnp.float32
    nrm = lambda k, shape, scale: jax.random.normal(k, shape, f32) * scale
    return {
        'x': nrm(ks[0], (BATCH, SEQ, D_MODEL), 1.0),
        'c': nrm(ks[1], (BATCH, D_MODEL), 1.0),
        'w_ada': nrm(ks[2], (DEPTH, D_MODEL, N_MOD * D_MODEL), 0.3 * D_MODEL ** -0.5),
        'b_ada': nrm(ks[3], (DEPTH, N_MOD * D_MODEL), 0.01),
        'ln_gain': 1.0 + nrm(ks[4], (DEPTH, 3, D_MODEL), 0.01),
        'ln_bias': nrm(ks[5], (DEPTH, 3, D_MODEL), 0.01),
        'ffn1_w_gate': nrm(ks[6], (DEPTH, D_MODEL, D_FF), D_MODEL ** -0.5),
        'ffn1_w_up': nrm(ks[7], (DEPTH, D_MODEL, D_FF), D_MODEL ** -0.5),
        'ffn1_w_down': nrm(ks[8], (DEPTH, D_FF, D_MODEL), BETA * D_FF ** -0.5),
        'w_in': nrm(ks[9], (DEPTH, D_MODEL, IN_WIDTH), D_MODEL ** -0.5),
        'w_out': nrm(ks[10], (DEPTH, MIX_WIDTH, D_MODEL), BETA * MIX_WIDTH ** -0.5),
        'ffn2_w_gate': nrm(ks[11], (DEPTH, D_MODEL, D_FF), D_MODEL ** -0.5),
        'ffn2_w_up': nrm(ks[12], (DEPTH, D_MODEL, D_FF), D_MODEL ** -0.5),
        'ffn2_w_down': nrm(ks[13], (DEPTH, D_FF, D_MODEL), BETA * D_FF ** -0.5),
    }

def second_block(x, c, w_ada, b_ada, ln_gain, ln_bias, ffn1_w_gate, ffn1_w_up, ffn1_w_down,
              w_in, w_out, ffn2_w_gate, ffn2_w_up, ffn2_w_down):
    cond = jax.nn.silu(c)
    for l in range(DEPTH):
        mod = cond @ w_ada[l] + b_ada[l]
        sh1, sc1, g1, sh2, sc2, g2, sh3, sc3, g3 = jnp.split(mod[:, None, :].astype(x.dtype), N_MOD, axis=-1)
        y = _swiglu(_modulate(x, sh1, sc1), ffn1_w_gate[l], ffn1_w_up[l], ffn1_w_down[l])
        x = _post_norm(x, y, g1, FFN_RES, ln_gain[l, 0], ln_bias[l, 0])
        y = _token_mixer(_modulate(x, sh2, sc2), w_in[l], w_out[l])
        x = _post_norm(x, y, g2, 1.0, ln_gain[l, 1], ln_bias[l, 1])
        y = _swiglu(_modulate(x, sh3, sc3), ffn2_w_gate[l], ffn2_w_up[l], ffn2_w_down[l])
        x = _post_norm(x, y, g3, FFN_RES, ln_gain[l, 2], ln_bias[l, 2])
    return x


def setup_inputs(seed=0):
    out = dict(first_inputs(seed))
    for name, value in second_inputs(seed + 1).items():
        if name != "x":
            out[name + "_2"] = value
    return out


def reference(
    x, ffn1_pre_g, ffn1_w_gate, ffn1_w_up, ffn1_w_down, ffn1_post_g, mix_pre_g, w_in,
    gdn_conv_w, gdn_a_log, gdn_dt_bias, gdn_norm_g, diff_lam_q1, diff_lam_k1, diff_lam_q2,
    diff_lam_k2, diff_norm_g, ssd_conv_w, ssd_conv_b, ssd_a_log, ssd_dt_bias, ssd_d, ssd_norm_g,
    mlstm_i_bias, mlstm_f_bias, mlstm_norm_g, w_out, mix_post_g, ffn2_pre_g, ffn2_w_gate,
    ffn2_w_up, ffn2_w_down, ffn2_post_g, c_2, w_ada_2, b_ada_2, ln_gain_2, ln_bias_2,
    ffn1_w_gate_2, ffn1_w_up_2, ffn1_w_down_2, w_in_2, w_out_2, ffn2_w_gate_2, ffn2_w_up_2,
    ffn2_w_down_2,
):
    x = first_block(
        x, ffn1_pre_g, ffn1_w_gate, ffn1_w_up, ffn1_w_down, ffn1_post_g, mix_pre_g, w_in,
        gdn_conv_w, gdn_a_log, gdn_dt_bias, gdn_norm_g, diff_lam_q1, diff_lam_k1, diff_lam_q2,
        diff_lam_k2, diff_norm_g, ssd_conv_w, ssd_conv_b, ssd_a_log, ssd_dt_bias, ssd_d,
        ssd_norm_g, mlstm_i_bias, mlstm_f_bias, mlstm_norm_g, w_out, mix_post_g, ffn2_pre_g,
        ffn2_w_gate, ffn2_w_up, ffn2_w_down, ffn2_post_g,
    )
    return second_block(
        x, c_2, w_ada_2, b_ada_2, ln_gain_2, ln_bias_2, ffn1_w_gate_2, ffn1_w_up_2,
        ffn1_w_down_2, w_in_2, w_out_2, ffn2_w_gate_2, ffn2_w_up_2, ffn2_w_down_2,
    )


_drawn_inputs = setup_inputs


def setup_inputs(seed=0):
    import zlib

    import numpy as np

    out = dict(_drawn_inputs(seed))
    spreads = {}
    factors = {'b_ada_2': 2.992}
    for name, (base, spread) in spreads.items():
        noise = np.random.default_rng([zlib.crc32(name.encode()), seed]).standard_normal(out[name].shape)
        drawn = base * np.exp(spread * noise) if base else spread * noise
        out[name] = jnp.asarray(drawn.astype(out[name].dtype))
    for name, factor in factors.items():
        out[name] = (out[name] * factor).astype(out[name].dtype)
    return out
```

```python
from contextlib import ExitStack

import numpy as np

import concourse.bass as bass
from concourse import mybir

F32 = mybir.dt.float32
BF16 = mybir.dt.bfloat16
ALU = mybir.AluOpType
ACT = mybir.ActivationFunctionType
AX = mybir.AxisListType.X

P = 128
SEQ = 256
TILES = SEQ // P
D = 1024
KT = D // P
DFF = 2816
FB = 256
NF = DFF // FB
DEPTH = 2
H = 4
NEG = -1.0e30
EPS = 1e-6
LN_EPS = 1e-5
ALPHA = (2.0 * DEPTH) ** 0.25
RING = 4
IN1 = 16
IN2 = 12
WO = 4
SMALL = 20
SMALL_AT = 8
NADA = 9
ADAQ = 4
LEVELS = 6
PAD = 3
U1 = IN1 + WO
U2 = IN2 + WO

C_IDENT, C_TRIU, C_ONES, C_SU, C_BLOCK = 0, 128, 256, 384, 512
C_MT = 640
C_NEGM = C_MT + 7 * 128
C_NEGD = C_NEGM + 128
C_SGN = C_NEGD + 384
C_ROPE = C_SGN + 12
N1 = C_ROPE + 64
C2_SL, C2_NEGC, C2_CNT, C2_RET, C2_ROT = 0, 128, 512, 896, 896 + 4 * 384
N2 = C2_ROT + 2 * 2 * 2 * 32
NBASE = C_BLOCK

R_SPB, R_ALOG, R_IB, R_DSK, R_LAM, R_LI, R_GAIN = 0, 12, 24, 28, 32, 160, 162
NR = R_GAIN + D
F_CONV, F_CB = 0, 48
NFP = 54
ARENA = 26200


class Steps:

    def __init__(self, sem, names):
        self.sem, self.names, self.turn = sem, names.split(), 0
        assert len(set(self.names)) == len(self.names)

    def at(self, name, use):
        return use * len(self.names) + (self.names.index(name) + 1)

    def done(self, name):
        assert self.names[self.turn] == name, (self.names[self.turn], name)
        self.turn = (self.turn + 1) % len(self.names)
        return self.sem


def over(ap, shape, *dims):
    for d in dims:
        ap = ap.unsqueeze(d)
    return ap.to_broadcast(shape)


def build(nc, t, out):
    ctx = ExitStack()

    def sb(name, shape, dt=F32):
        return ctx.enter_context(nc.sbuf_tensor(name, shape, dt))

    def sem(name):
        return ctx.enter_context(nc.semaphore(name))

    def steps(name, names):
        return Steps(sem(name), names)

    ps = ctx.enter_context(nc.psum_tensor("ps", [P, 8, 512], F32))
    x = sb("x", [P, TILES, D])
    tok = sb("tok", [P, TILES, D])
    hT = sb("hT", [P, KT, SEQ])
    slot_g = sb("slot_g", [P, KT, FB])
    slot_u = sb("slot_u", [P, KT, FB])
    slot_d = sb("slot_d", [P, FB // P, D])
    silu_g = sb("silu_g", [P, 2 * SEQ])
    act = sb("act", [P, FB // P, SEQ])
    ring = sb("ring", [P, RING, KT * FB])
    rows = sb("rows", [P, 2, 2, D])
    arena = sb("arena", [P, ARENA])
    base = sb("base", [P, NBASE])
    zero = sb("zero", [P, 512], BF16)
    stat = sb("stat", [P, 8])
    bn = sb("bn", [P, TILES, 2, 6])
    mv = sb("mv", [P, TILES, 2])
    IDENT, TRIU = base[:, C_IDENT:C_IDENT + P], base[:, C_TRIU:C_TRIU + P]
    ONES, SU = base[:, C_ONES:C_ONES + P], base[:, C_SU:C_SU + P]
    TU = base[:, C_TRIU:C_TRIU + SEQ]

    x_ready = sem("x_ready")
    base_in = sem("base_in")
    settled = sem("settled")
    rows_in = [sem("rows_in0"), sem("rows_in1")]
    zero_set = sem("zero_set")
    gate_in, up_in, down_in = sem("gate_in"), sem("up_in"), sem("down_in")
    gate_done, up_done, down_done = sem("gate_done"), sem("up_done"), sem("down_done")
    silu_done, act_ready = sem("silu_done"), sem("act_ready")
    ring_in = [sem(f"ring_in{i}") for i in range(RING)]
    ring_used = sem("ring_used")
    proj_evac = sem("proj_evac")
    pre_t = steps("pre_t", "trans")
    pre_a = steps("pre_a", "ssq root copy")
    pre_v = steps("pre_v", "mean rstd tok copy")
    post_a = steps("post_a", "ssq root")
    post_v = steps("post_v", "mean stats rstd scaled")
    bn_done, ln_r = sem("bn_done"), sem("ln_r")
    mod_v = steps("mod_v", "shift scale rows")
    ln_v = steps("ln_v", "gated mixed stats var centred gained")
    ln_a = steps("ln_a", "root")

    def settle(eng):
        eng.sem_inc(settled, 1)

    def acc(tile):
        return ps[:, 2 * tile:2 * tile + 2, :]

    def ffn_sp(sp, f, l, wg, wu, wd):
        settle(sp)
        with sp.Fori(0, NF) as i:
            n = f * NF + i
            sp.wait_ge(gate_done, n + 1)
            sp.dma_start(slot_g[:].rearrange("p k n -> p (k n)"),
                         wg[bass.ds(l, 1), bass.ds(i, 1), :, :].rearrange("l i p n -> p (l i n)")).then_inc(gate_in, 16)
            sp.wait_ge(up_done, n + 1)
            sp.dma_start(slot_u[:].rearrange("p k n -> p (k n)"),
                         wu[bass.ds(l, 1), bass.ds(i, 1), :, :].rearrange("l i p n -> p (l i n)")).then_inc(up_in, 16)
            sp.wait_ge(down_done, n + 1)
            sp.dma_start(slot_d[:].rearrange("p k n -> p (k n)"),
                         wd[bass.ds(l, 1), bass.ds(i, 1), :, :].rearrange("l i p n -> p (l i n)")).then_inc(down_in, 16)

    def ffn_pe(pe, f, g):
        pe.wait_ge(zero_set, 1)
        for b in range(4):
            nc.tensor.matmul(ps[:, b, :], zero[:, 0:P], zero[:], start=True, stop=False)

        def gate_up(n):
            pe.wait_ge(gate_in, n * 16 + 16)
            pe.wait_ge(silu_done, n + 1)
            for s in range(2):
                for k in range(KT):
                    last = nc.tensor.matmul(ps[:, 4, s * SEQ:(s + 1) * SEQ], slot_g[:, k, s * P:(s + 1) * P],
                                            hT[:, k, :], start=(k == 0), stop=(k == KT - 1))
            last.then_inc(gate_done, 1)
            pe.wait_ge(up_in, n * 16 + 16)
            pe.wait_ge(act_ready, n + 1)
            for s in range(2):
                for k in range(KT):
                    last = nc.tensor.matmul(ps[:, 5, s * SEQ:(s + 1) * SEQ], slot_u[:, k, s * P:(s + 1) * P],
                                            hT[:, k, :], start=(k == 0), stop=(k == KT - 1))
            last.then_inc(up_done, 1)

        def down(n, stop):
            pe.wait_ge(down_in, n * 16 + 16)
            pe.wait_ge(act_ready, n + 2)
            for kk in range(2):
                for tile in range(TILES):
                    for half in range(2):
                        last = nc.tensor.matmul(ps[:, 2 * tile + half, :], act[:, kk, tile * P:(tile + 1) * P],
                                                slot_d[:, kk, half * 512:(half + 1) * 512],
                                                start=False, stop=stop and kk == 1)
            last.then_inc(down_done, 1)

        pe.wait_ge(pre_a.sem, pre_a.at("copy", g))
        pe.wait_ge(pre_v.sem, pre_v.at("copy", g))
        gate_up(f * NF)
        with pe.Fori(1, NF) as i:
            gate_up(f * NF + i)
            down(f * NF + i - 1, False)
        down(f * NF + (NF - 1), True)

    def ffn_act(a, f):
        with a.Fori(0, NF) as i:
            n = f * NF + i
            a.wait_ge(gate_done, n + 2)
            a.wait_ge(act_ready, n + 1)
            nc.scalar.activation(silu_g[:], ps[:, 4, :], ACT.Silu).then_inc(silu_done, 1)

    def ffn_dve(v, f):
        with v.Fori(0, NF) as i:
            n = f * NF + i
            v.wait_ge(silu_done, n + 2)
            v.wait_ge(up_done, n + 2)
            v.wait_ge(down_done, n + 1)
            nc.vector.tensor_tensor(act[:].rearrange("p s t -> p (s t)"), silu_g[:], ps[:, 5, :],
                                    ALU.mult).then_inc(act_ready, 1)

    def transposes_pe():
        for k in range(KT):
            for tile in range(TILES):
                c = (k % 2) * SEQ + tile * P
                last = nc.tensor.transpose(ps[:, 4 + k // 2, c:c + P], tok[:, tile, k * P:(k + 1) * P], IDENT)
        return last

    def hT_half(i):
        return hT[:, 4 * i:4 * i + 4, :].rearrange("p (b k) t -> p b (k t)", b=2), ps[:, 4 + 2 * i:6 + 2 * i, :]

    def pre_pe(pe, g):
        pe.wait_ge(pre_v.sem, pre_v.at("tok", g))
        transposes_pe().then_inc(pre_t.done("trans"), 1)

    def pre_act(a, g, normed):
        a.wait_ge(x_ready, g * 16 + 16)
        if normed:
            for tile in range(TILES):
                last = nc.scalar.activation(tok[:, tile, :], x[:, tile, :], ACT.Square,
                                            accum_out=stat[:, tile:tile + 1])
            last.then_inc(pre_a.done("ssq"), 1)
            a.wait_ge(pre_v.sem, pre_v.at("mean", g))
            nc.scalar.activation(stat[:, 2:4], stat[:, 2:4], ACT.Sqrt).then_inc(pre_a.done("root"), 1)
        else:
            nc.scalar.activation(stat[:, 6:7], x[:, 0, 0:1], ACT.Copy).then_inc(pre_a.done("ssq"), 1)
            nc.scalar.activation(stat[:, 7:8], x[:, 0, 0:1], ACT.Copy).then_inc(pre_a.done("root"), 1)
        a.wait_ge(pre_t.sem, pre_t.at("trans", g))
        dst, src = hT_half(0)
        nc.scalar.activation(dst, src, ACT.Copy).then_inc(pre_a.done("copy"), 1)

    def rows_wait(v, L, pos):
        if pos == 1:
            v.wait_ge(rows_in[1], L * 16 + 16)
        else:
            v.wait_ge(rows_in[0], L * 32 + (16 if pos == 0 else 32))

    def pre_dve(v, L, pos, normed):
        g = L * 3 + pos
        rows_wait(v, L, pos)
        v.wait_ge(x_ready, g * 16 + 16)
        if normed:
            v.wait_ge(pre_a.sem, pre_a.at("ssq", g))
            nc.vector.tensor_scalar(stat[:, 2:4], stat[:, 0:2], 1.0 / D, EPS, ALU.mult,
                                    ALU.add).then_inc(pre_v.done("mean"), 1)
            v.wait_ge(pre_a.sem, pre_a.at("root", g))
            nc.vector.reciprocal(stat[:, 4:6], stat[:, 2:4]).then_inc(pre_v.done("rstd"), 1)
            v.wait_ge(pre_v.sem, pre_v.at("rstd", g))
            for tile in range(TILES):
                last = nc.vector.scalar_tensor_tensor(tok[:, tile, :], x[:, tile, :], stat[:, 4 + tile:5 + tile],
                                                      rows[:, pos % 2, 0, :], ALU.mult, ALU.mult)
            last.then_inc(pre_v.done("tok"), 1)
        else:
            shift, scale1 = mrow[:, 0, :], mrow[:, 1, :]
            v.wait_ge(mod_v.sem, mod_v.at("rows", g - 6))
            nc.vector.tensor_tensor(tok[:], x[:], over(scale1, [P, TILES, D], 1),
                                    ALU.mult).then_inc(pre_v.done("mean"), 1)
            nc.vector.memset(stat[:, 5:6], 0.0).then_inc(pre_v.done("rstd"), 1)
            v.wait_ge(pre_v.sem, pre_v.at("mean", g))
            nc.vector.tensor_tensor(tok[:], tok[:], over(shift, [P, TILES, D], 1),
                                    ALU.add).then_inc(pre_v.done("tok"), 1)
        v.wait_ge(pre_t.sem, pre_t.at("trans", g))
        dst, src = hT_half(1)
        nc.vector.tensor_copy(dst, src).then_inc(pre_v.done("copy"), 1)

    def post_act(a, g, ready):
        a.wait_ge(*ready)
        for tile in range(TILES):
            last = nc.scalar.activation(tok[:, tile, :].rearrange("p (b n) -> p b n", b=2), acc(tile), ACT.Square,
                                        accum_out=stat[:, tile:tile + 1])
        last.then_inc(post_a.done("ssq"), 1)
        a.wait_ge(post_v.sem, post_v.at("mean", g))
        nc.scalar.activation(stat[:, 2:4], stat[:, 2:4], ACT.Sqrt).then_inc(post_a.done("root"), 1)

    def post_dve(v, g, pos, weight):
        v.wait_ge(post_a.sem, post_a.at("ssq", g))
        nc.vector.tensor_scalar(stat[:, 2:4], stat[:, 0:2], 1.0 / D, EPS, ALU.mult,
                                ALU.add).then_inc(post_v.done("mean"), 1)
        v.wait_ge(post_a.sem, post_a.at("root", g))
        nc.vector.reciprocal(stat[:, 4:6], stat[:, 2:4]).then_inc(post_v.done("stats"), 1)
        v.wait_ge(post_v.sem, post_v.at("stats", g))
        nc.vector.tensor_scalar(stat[:, 6:8], stat[:, 4:6], weight, None, ALU.mult).then_inc(post_v.done("rstd"), 1)
        v.wait_ge(post_v.sem, post_v.at("rstd", g))
        for tile in range(TILES):
            last = nc.vector.scalar_tensor_tensor(
                tok[:, tile, :].rearrange("p (b n) -> p b n", b=2), acc(tile), stat[:, 6 + tile:7 + tile],
                rows[:, pos % 2, 1, :].rearrange("p (b n) -> p b n", b=2), ALU.mult, ALU.mult)
        last.then_inc(post_v.done("scaled"), 1)
        v.wait_ge(post_v.sem, post_v.at("scaled", g))
        nc.vector.tensor_tensor(x[:], x[:], tok[:], ALU.add).then_inc(x_ready, 16)

    def ln_act(a, h):
        a.wait_ge(ln_v.sem, ln_v.at("var", h))
        nc.scalar.activation(stat[:, 2:4], stat[:, 0:2], ACT.Sqrt).then_inc(ln_a.done("root"), 1)

    def ln_dve(v, h, pos, ready, gate):
        v.wait_ge(*ready)
        for tile in range(TILES):
            last = nc.vector.tensor_tensor(tok[:, tile, :].rearrange("p (b n) -> p b n", b=2), acc(tile),
                                           gate.rearrange("p (b n) -> p b n", b=2), ALU.mult)
        last.then_inc(ln_v.done("gated"), 1)
        v.wait_ge(ln_v.sem, ln_v.at("gated", h))
        nc.vector.scalar_tensor_tensor(tok[:], x[:], ALPHA, tok[:], ALU.mult, ALU.add).then_inc(ln_v.done("mixed"), 1)
        v.wait_ge(ln_v.sem, ln_v.at("mixed", h))
        for tile in range(TILES):
            for half in range(2):
                last = nc.vector.bn_stats(bn[:, tile, half, :], tok[:, tile, half * 512:(half + 1) * 512])
        last.then_inc(ln_v.done("stats"), 1)
        v.wait_ge(ln_v.sem, ln_v.at("stats", h))
        settle(v)
        for tile in range(TILES):
            last = nc.vector.bn_aggr(mv[:, tile, :], bn[:, tile, :, :].rearrange("p a b -> p (a b)"))
        last.then_inc(bn_done, 1)
        v.wait_ge(bn_done, h + 1)
        nc.vector.tensor_scalar(stat[:, 0:2], mv[:, :, 1], LN_EPS, None, ALU.add).then_inc(ln_v.done("var"), 1)
        v.wait_ge(ln_a.sem, ln_a.at("root", h))
        nc.vector.reciprocal(stat[:, 4:6], stat[:, 2:4]).then_inc(ln_r, 1)
        v.wait_ge(ln_r, h + 1)
        for tile in range(TILES):
            last = nc.vector.tensor_scalar(tok[:, tile, :], tok[:, tile, :], mv[:, tile, 0:1],
                                           stat[:, 4 + tile:5 + tile], ALU.subtract, ALU.mult)
        last.then_inc(ln_v.done("centred"), 1)
        v.wait_ge(ln_v.sem, ln_v.at("centred", h))
        nc.vector.tensor_tensor(tok[:], tok[:], over(rows[:, pos % 2, 0, :], [P, TILES, D], 1),
                                ALU.mult).then_inc(ln_v.done("gained"), 1)
        v.wait_ge(ln_v.sem, ln_v.at("gained", h))
        nc.vector.tensor_tensor(x[:], tok[:], over(rows[:, pos % 2, 1, :], [P, TILES, D], 1),
                                ALU.add).then_inc(x_ready, 16)


    def ring_load(sp, slot, src, width=KT * FB):
        sp.dma_start(ring[:, slot, 0:width], src).then_inc(ring_in[slot], 16)

    def ring_value(slot, done, nth):
        return (done + nth) * 16

    def feature_product(bank, slot, n):
        w = ring[:, slot, :].rearrange("p (k n) -> p k n", k=KT)
        for s in range(FB // P):
            for k in range(KT):
                last = nc.tensor.matmul(ps[:, bank, s * SEQ:(s + 1) * SEQ], w[:, k, s * P:(s + 1) * P], hT[:, k, :],
                                        start=(k == 0), stop=(k == KT - 1))
        return last

    def token_product(bank, slot, width=FB):
        w = ring[:, slot, 0:KT * width].rearrange("p (k n) -> p k n", k=KT)
        for tile in range(TILES):
            for k in range(KT):
                last = nc.tensor.matmul(ps[:, bank, tile * width:(tile + 1) * width], hT[:, k, tile * P:(tile + 1) * P],
                                        w[:, k, :], start=(k == 0), stop=(k == KT - 1))
        return last

    def out_product(pe, first, L):
        for q in range(WO):
            n = first + q
            pe.wait_ge(ring_in[n % RING], ring_value(n % RING, L, n // RING + 1))
            w = ring[:, n % RING, :].rearrange("p (k n) -> p k n", k=2)
            for kk in range(2):
                k = 2 * q + kk
                for tile in range(TILES):
                    for half in range(2):
                        last = nc.tensor.matmul(ps[:, 2 * tile + half, :], hT[:, k, tile * P:(tile + 1) * P],
                                                w[:, kk, half * 512:(half + 1) * 512], start=(k == 0),
                                                stop=(k == KT - 1))
            last.then_inc(ring_used, 1)

    def scores_T(bank, kT_s, qT_t, h):
        nc.tensor.matmul(ps[:, bank, 0:SEQ], kT_s[:, 0:P], qT_t[:, 0:SEQ], start=True, stop=True)
        return nc.tensor.matmul(ps[:, bank, SEQ:SEQ + P], kT_s[:, P:SEQ], qT_t[:, P:SEQ], start=True, stop=True)

    def weighted_values(out0, out1, pT, v0, v1):
        nc.tensor.matmul(out0, pT[:, 0:P], v0, start=True, stop=True)
        nc.tensor.matmul(out1, pT[:, P:SEQ], v0, start=True, stop=False)
        return nc.tensor.matmul(out1, pT[:, SEQ:SEQ + P], v1, start=False, stop=True)

    def row_of(out, col):
        return nc.tensor.matmul(out, col.to_broadcast([P, P]), IDENT, start=True, stop=True)

    def prefix_row(bank, off, col0, col1):
        nc.tensor.matmul(ps[:, bank, off:off + SEQ], col0.to_broadcast([P, P]), TU, start=True, stop=False)
        return nc.tensor.matmul(ps[:, bank, off + P:off + SEQ], col1.to_broadcast([P, P]), TRIU, start=False, stop=True)

    def diag(buf):
        return buf[:].rearrange("p h (b n) -> p h b n", b=3)[:, :, 0:3:2, :]


    class Arena:

        def __init__(self):
            self.at = 0

        def take(self, *shape):
            n = int(np.prod(shape))
            piece = arena[:, self.at:self.at + n]
            self.at += n
            assert self.at <= ARENA, (self.at, ARENA)
            if len(shape) == 2:
                piece = piece.rearrange("p (a b) -> p a b", a=shape[0])
            if len(shape) == 3:
                piece = piece.rearrange("p (a b c) -> p a b c", a=shape[0], b=shape[1])
            if len(shape) == 4:
                piece = piece.rearrange("p (a b c d) -> p a b c d", a=shape[0], b=shape[1], c=shape[2])
            return piece

    m = Arena()
    con = m.take(N1 - NBASE)
    par = m.take(NR)
    fp = m.take(NFP)
    u = m.take(12, PAD + SEQ)
    cv = m.take(12, SEQ)
    qk_m = m.take(4, SEQ)
    small = m.take(TILES, SMALL)
    gate_g = m.take(TILES, SEQ)
    rope_in = m.take(TILES, 512)
    v_d = m.take(TILES, SEQ)
    z_s = m.take(TILES, SEQ)
    v_m = m.take(TILES, H, 65)
    o_m = m.take(TILES, SEQ)
    sp_x, sp_e, sp_u, sp_l, sp_c = (m.take(TILES, 12) for _ in range(5))
    ld = m.take(TILES, 12)
    ea = m.take(12)
    gc = m.take(TILES, 12)
    beta = m.take(TILES, H)
    dt = m.take(TILES, H)
    acol, mcol, negm, em, den = (m.take(TILES, H) for _ in range(5))
    md = m.take(H, TILES)
    mfull = m.take(H)
    coef = m.take(TILES, 8)
    rmax = m.take(TILES, 8)
    lamb = m.take(8)
    lamp = m.take(2, 32)
    ms = m.take(TILES, 16)
    gsum = m.take(TILES, 2)
    dT2 = m.take(H, 384)
    xs = m.take(TILES, SEQ)
    xdt = m.take(TILES, SEQ)
    mark = m.at
    dT = m.take(H, 384)
    lT = m.take(H, 384)
    xT, xi, bT, pm = (m.take(8, P) for _ in range(4))
    kb = m.take(2, SEQ)
    vb, uu = m.take(TILES, SEQ), m.take(TILES, SEQ)
    r2 = m.take(SEQ)
    m.at = mark
    dS = m.take(8, 384)
    pD = m.take(H, 384)
    pT = m.take(H, 384)
    qkr = m.take(TILES, 512)
    dqk = m.take(4, SEQ)
    rt = m.take(2, 16 * 16)
    sq = dS.rearrange("p a b -> p (a b)")[:, 0:TILES * D].rearrange("p (a b) -> p a b", a=TILES)
    mix = tok

    def K(c, n=P):
        return con[:, c - NBASE:c - NBASE + n]

    BLOCKS, NEGM, NEGD = K(C_BLOCK), K(C_NEGM), K(C_NEGD, 384)
    COS = K(C_ROPE, 32).rearrange("p (t n) -> p t n", t=2)
    SIN = K(C_ROPE + 32, 32).rearrange("p (t n) -> p t n", t=2)
    con_in, par_in = sem("con_in"), sem("par_in")
    pads = sem("pads")
    inv_b, inv_p, inv_c, inv_r, inv_x = (sem(f"inv_{c}") for c in "bpcrx")

    T1 = steps("mix1_t", "small_sums rows_g sumsq beta_rows kk qk x0 vt u1 l21 u2 o_g rows_s xt_s cb o_s "
                         "rows_a rows_m qk_m o_m rope_t sc_d trans_d o_d trans")
    A1 = steps("mix1_a", "silu_g sq silu_s sp_e sp_l ea eb gc dec_g root xi u1 u2 o_g xs dec_s dec_m em den "
                         "dqk exp_d lam pT o_d gates sq_o root_o copy")
    V1 = steps("mix1_v", "cg0 cg1 cg2 conv_g cs0 cs1 cs2 conv_s sp_in sp_sgn sp_abs sp_u sp_um sp_em sp_ru sp_corr sp_max sp_l sp dt ld eb1 beta dec_g rs "
                         "rrs qkn kb lT aT mt1 xT vb r2 "
                         "xdt dec_s w_s skip o_s "
                         "ai acol tmp_m md mf m0 m1 dec_m w_m mt negm denm rden o_m "
                         "ra1 rb1 rc1 rd1 re1 rf1 ra2 rb2 rc2 rd2 re2 rf2 mask_d max_d sub_d sum_d rec_d lam0 lam1 lam2 coef "
                         "scale_d add_d "
                         "pre_gate sums_o pair0 pair1 mean_o rstd_o gl norm_o gain_o gate_o copy")
    G1 = steps("mix1_g", "dec_g dec_s dec_m")

    def block_of(n):
        return n % RING, n // RING + 1

    def mixer1_sp(sp, l):
        at = 0
        for n in range(U1):
            sp.wait_ge(ring_used, l * U1 + n + 1)
            if n == SMALL_AT:
                ring_load(sp, n % RING, t["w_small"][bass.ds(l, 1), :, :].rearrange("l p n -> p (l n)"), KT * SMALL)
            elif n < IN1:
                ring_load(sp, n % RING,
                          t["w_in"][bass.ds(l, 1), at:at + 1, :, :].rearrange("l i p n -> p (l i n)"))
                at += 1
            else:
                ring_load(sp, n % RING,
                          t["w_out"][bass.ds(l, 1), n - IN1:n - IN1 + 1, :, :].rearrange("l i p n -> p (l i n)"))

    def mixer1_pe(pe, l, g):
        def after(S, name):
            pe.wait_ge(S.sem, S.at(name, l))

        pe.wait_ge(pre_a.sem, pre_a.at("copy", g))
        pe.wait_ge(pre_v.sem, pre_v.at("copy", g))
        for n in range(IN1):
            slot, turn = block_of(n)
            pe.wait_ge(ring_in[slot], ring_value(slot, l * (U1 // RING), turn))
            pe.wait_ge(proj_evac, l * IN1 + n + 1)
            if n < SMALL_AT:
                last = feature_product(4 + n % 4, slot, n)
            else:
                last = token_product(4 + n % 4, slot, SMALL if n == SMALL_AT else FB)
            last.then_inc(ring_used, 1)
        pe.wait_ge(proj_evac, l * IN1 + IN1 + 4)

        after(V1, "ld")
        nc.tensor.matmul(ps[:, 7, 0:12], TRIU, ld[:, 0, :], start=True, stop=True)
        nc.tensor.matmul(ps[:, 7, 12:24], ONES, ld[:, 0, :], start=True, stop=False)
        nc.tensor.matmul(ps[:, 7, 12:24], TRIU, ld[:, 1, :], start=False,
                         stop=True).then_inc(T1.done("small_sums"), 1)
        for h in range(H):
            last = prefix_row(4 + h // 2, (h % 2) * SEQ, ld[:, 0, h:h + 1], ld[:, 1, h:h + 1])
        last.then_inc(T1.done("rows_g"), 1)
        after(A1, "sq")
        for c in range(4):
            last = nc.tensor.matmul(ps[:, c // 2, (c % 2) * SEQ:(c % 2 + 1) * SEQ], BLOCKS,
                                    pm_sq[:, c, :], start=True, stop=True)
        last.then_inc(T1.done("sumsq"), 1)
        after(V1, "beta")
        for h in range(H):
            for tile in range(TILES):
                c = (h % 2) * SEQ + tile * P
                last = row_of(ps[:, 2 + h // 2, c:c + P], beta[:, tile, h:h + 1])
        last.then_inc(T1.done("beta_rows"), 1)
        after(V1, "kb")
        for h in range(H):
            half = slice(64 * (h % 2), 64 * (h % 2) + 64)
            last = scores_T(h, cv[half, 2 + h // 2, :], kb[half, h // 2, :], h)
        last.then_inc(T1.done("kk"), 1)
        after(V1, "dec_g")
        for h in range(H):
            half = slice(64 * (h % 2), 64 * (h % 2) + 64)
            last = scores_T(4 + h, cv[half, 2 + h // 2, :], cv[half, h // 2, :], h)
        last.then_inc(T1.done("qk"), 1)
        after(V1, "xT")
        for i in range(8):
            last = nc.tensor.transpose(ps[:, i // 4, (i % 4) * P:(i % 4 + 1) * P], xT[:, i, :], IDENT)
        last.then_inc(T1.done("x0"), 1)
        after(A1, "xi")
        after(V1, "aT")
        settle(pe)
        with pe.Fori(0, LEVELS) as j:
            n = l * LEVELS + j
            pe.wait_ge(inv_x, n + 1)
            pe.wait_ge(inv_b, n + 1)
            for i in range(8):
                last = nc.tensor.matmul(ps[:, 2 + i // 4, (i % 4) * P:(i % 4 + 1) * P], bT[:, i, :], xi[:, i, :],
                                        start=True, stop=True)
            last.then_inc(inv_p, 1)
            pe.wait_ge(inv_c, n + 1)
            for i in range(8):
                nc.tensor.matmul(ps[:, 4 + i // 4, (i % 4) * P:(i % 4 + 1) * P], xT[:, i, :], pm[:, i, :],
                                 start=True, stop=True)
            for i in range(8):
                last = nc.tensor.matmul(ps[:, 6 + i // 4, (i % 4) * P:(i % 4 + 1) * P], pm[:, i, :], xT[:, i, :],
                                        start=True, stop=True)
            last.then_inc(inv_r, 1)
        for c in range(2):
            for tile in range(TILES):
                o = tile * SEQ + c * P
                last = nc.tensor.transpose(ps[:, 0, o:o + P], cv[:, 4 + c, tile * P:(tile + 1) * P], IDENT)
        last.then_inc(T1.done("vt"), 1)
        pe.wait_ge(inv_x, l * LEVELS + LEVELS + 1)
        after(V1, "vb")
        for h in range(H):
            last = nc.tensor.matmul(ps[:, 1, h * 64:(h + 1) * 64], xT[:, 2 * h, :], vb[:, 0, h * 64:(h + 1) * 64],
                                    start=True, stop=True)
        last.then_inc(T1.done("u1"), 1)
        after(A1, "u1")
        for h in range(H):
            last = nc.tensor.matmul(ps[:, 2, h * 64:(h + 1) * 64], lT[:, h, P:SEQ], uu[:, 0, h * 64:(h + 1) * 64],
                                    start=True, stop=True)
        last.then_inc(T1.done("l21"), 1)
        after(V1, "r2")
        for h in range(H):
            last = nc.tensor.matmul(ps[:, 3, h * 64:(h + 1) * 64], xT[:, 2 * h + 1, :], r2[:, h * 64:(h + 1) * 64],
                                    start=True, stop=True)
        last.then_inc(T1.done("u2"), 1)
        after(A1, "u2")
        for h in range(H):
            c = slice(h * 64, (h + 1) * 64)
            last = weighted_values(ps[:, 4, h * 64:(h + 1) * 64], ps[:, 4, SEQ + h * 64:SEQ + (h + 1) * 64],
                                   dT[:, h, :], uu[:, 0, c], uu[:, 1, c])
        last.then_inc(T1.done("o_g"), 1)

        for h in range(H):
            last = prefix_row(6 + h // 2, (h % 2) * SEQ, ld[:, 0, 4 + h:5 + h], ld[:, 1, 4 + h:5 + h])
        last.then_inc(T1.done("rows_s"), 1)
        after(A1, "silu_s")
        for c in range(2):
            for tile in range(TILES):
                o = tile * SEQ + c * P
                last = nc.tensor.transpose(ps[:, 0, o:o + P], cv[:, 6 + c, tile * P:(tile + 1) * P], IDENT)
        last.then_inc(T1.done("xt_s"), 1)
        for grp in range(2):
            last = scores_T(1 + grp, cv[:, 8 + grp, :], cv[:, 10 + grp, :], grp)
        last.then_inc(T1.done("cb"), 1)
        after(V1, "w_s")
        after(V1, "xdt")
        for h in range(H):
            c = slice(h * 64, (h + 1) * 64)
            last = weighted_values(ps[:, 3, h * 64:(h + 1) * 64], ps[:, 3, SEQ + h * 64:SEQ + (h + 1) * 64],
                                   dT2[:, h, :], xdt[:, 0, c], xdt[:, 1, c])
        last.then_inc(T1.done("o_s"), 1)

        after(A1, "o_g")
        after(V1, "acol")
        for h in range(H):
            for tile in range(TILES):
                c = (h % 2) * SEQ + tile * P
                last = row_of(ps[:, 4 + h // 2, c:c + P], acol[:, tile, h:h + 1])
        last.then_inc(T1.done("rows_a"), 1)
        after(V1, "m1")
        for h in range(H):
            for tile in range(TILES):
                c = (h % 2) * SEQ + tile * P
                last = row_of(ps[:, 6 + h // 2, c:c + P], mcol[:, tile, h:h + 1])
        last.then_inc(T1.done("rows_m"), 1)
        after(V1, "o_s")
        for h in range(H):
            half = slice(64 * (h % 2), 64 * (h % 2) + 64)
            last = scores_T(h, qk_m[half, 2 + h // 2, :], qk_m[half, h // 2, :], h)
        last.then_inc(T1.done("qk_m"), 1)
        after(V1, "w_m")
        for h in range(H):
            last = weighted_values(ps[:, 4, h * 65:(h + 1) * 65], ps[:, 5, h * 65:(h + 1) * 65], dT2[:, h, :],
                                   v_m[:, 0, h, :], v_m[:, 1, h, :])
        last.then_inc(T1.done("o_m"), 1)

        after(V1, "rf2")
        for c in range(4):
            for tile in range(TILES):
                o = (c % 2) * SEQ + tile * P
                last = nc.tensor.transpose(ps[:, c // 2, o:o + P], qkr[:, tile, c * P:(c + 1) * P], IDENT)
        last.then_inc(T1.done("rope_t"), 1)
        after(A1, "dqk")
        after(V1, "o_m")
        for j in range(8):
            part, c = slice(32 * (j % 4), 32 * (j % 4) + 32), j // 4
            nc.tensor.matmul(ps[:, j % 4, c * P:(c + 1) * P], dqk[part, c, 0:P], dqk[part, 2 + c, 0:P],
                             start=True, stop=True, tile_position=(32 * (j % 4), 0))
            last = nc.tensor.matmul(ps[:, 4 + j % 4, c * SEQ:(c + 1) * SEQ], dqk[part, c, P:SEQ], dqk[part, 2 + c, :],
                                    start=True, stop=True, tile_position=(32 * (j % 4), 0))
        last.then_inc(T1.done("sc_d"), 1)
        after(V1, "add_d")
        for h in range(H):
            for b in range(3):
                last = nc.tensor.transpose(ps[:, h, b * P:(b + 1) * P], pD[:, h, b * P:(b + 1) * P], IDENT)
        last.then_inc(T1.done("trans_d"), 1)
        after(A1, "pT")
        for h in range(H):
            c = slice(h * 64, (h + 1) * 64)
            last = weighted_values(ps[:, 4, h * 64:(h + 1) * 64], ps[:, 4, SEQ + h * 64:SEQ + (h + 1) * 64],
                                   pT[:, h, :], v_d[:, 0, c], v_d[:, 1, c])
        last.then_inc(T1.done("o_d"), 1)

        after(V1, "gate_o")
        transposes_pe().then_inc(T1.done("trans"), 1)
        after(A1, "copy")
        after(V1, "copy")
        out_product(pe, IN1, l * (U1 // RING))

    def mixer1_act(a, l):
        def after(S, name):
            a.wait_ge(S.sem, S.at(name, l))

        token_homes = {9: gate_g, 10: rope_in[:, :, 0:SEQ], 11: rope_in[:, :, SEQ:512], 12: v_d, 13: z_s, 15: o_m}
        for n in range(IN1):
            a.wait_ge(ring_used, l * U1 + n + (1 + RING))
            bank = ps[:, 4 + n % 4, :]
            two = bank.rearrange("p (a b) -> p a b", a=2)
            if n < 6:
                last = nc.scalar.activation(u[:, 2 * n:2 * n + 2, PAD:], two, ACT.Copy)
            elif n < 8:
                last = nc.scalar.activation(qk_m[:, 2 * (n - 6):2 * (n - 6) + 2, :], two, ACT.Copy,
                                            scale=1.0 if n == 6 else 64.0 ** -0.5)
            elif n == SMALL_AT:
                last = nc.scalar.activation(small, bank[:, 0:2 * SMALL].rearrange("p (a b) -> p a b", a=2), ACT.Copy)
            elif n == 14:
                for tile in range(TILES):
                    last = nc.scalar.activation(v_m[:, tile, :, 0:64],
                                                two[:, tile, :].rearrange("p (h d) -> p h d", h=H), ACT.Copy)
            else:
                last = nc.scalar.activation(token_homes[n], two, ACT.Copy)
            last.then_inc(proj_evac, 1)
            if n == 11:
                after(V1, "conv_g")
                nc.scalar.activation(cv[:, 0:6, :], cv[:, 0:6, :], ACT.Silu).then_inc(A1.done("silu_g"), 1)
                after(A1, "silu_g")
                nc.scalar.activation(pm_sq, cv[:, 0:4, :], ACT.Square).then_inc(A1.done("sq"), 1)
            if n == 13:
                after(V1, "conv_s")
                for c in range(6):
                    last = nc.scalar.activation(cv[:, 6 + c, :], cv[:, 6 + c, :], ACT.Silu, bias=fp[:, F_CB + c:F_CB + c + 1])
                last.then_inc(A1.done("silu_s"), 1)

        after(V1, "sp_abs")
        nc.scalar.activation(sp_e, sp_c, ACT.Exp, scale=-1.0).then_inc(A1.done("sp_e"), 1)
        after(V1, "sp_u")
        nc.scalar.activation(sp_l, sp_u, ACT.Ln).then_inc(A1.done("sp_l"), 1)
        a.wait_ge(par_in, l * 32 + 32)
        nc.scalar.activation(ea, par[:, R_ALOG:R_ALOG + 12], ACT.Exp).then_inc(A1.done("ea"), 1)
        nc.scalar.activation(beta, small[:, :, 0:H], ACT.Exp, scale=-1.0).then_inc(A1.done("eb"), 1)
        a.wait_ge(T1.sem, T1.at("small_sums", l))
        nc.scalar.activation(gc, ps[:, 7, 0:24].rearrange("p (a b) -> p a b", a=2), ACT.Copy).then_inc(A1.done("gc"), 1)
        after(V1, "dec_g")
        nc.scalar.activation(dT, dT, ACT.Exp).then_inc(A1.done("dec_g"), 1)
        after(V1, "rs")
        nc.scalar.activation(pm_sq, pm_sq, ACT.Sqrt).then_inc(A1.done("root"), 1)
        after(T1, "x0")
        nc.scalar.activation(xi.rearrange("p (a i) n -> p a (i n)", a=2), ps[:, 0:2, :], ACT.Copy).then_inc(A1.done("xi"), 1)
        with a.Fori(0, LEVELS) as j:
            a.wait_ge(inv_p, l * LEVELS + j + 2)
            nc.scalar.activation(pm.rearrange("p (a i) n -> p a (i n)", a=2), ps[:, 2:4, :], ACT.Copy).then_inc(inv_c, 1)
        after(T1, "u1")
        nc.scalar.activation(uu[:, 0, :], ps[:, 1, 0:SEQ], ACT.Copy).then_inc(A1.done("u1"), 1)
        after(T1, "u2")
        nc.scalar.activation(uu[:, 1, :], ps[:, 3, 0:SEQ], ACT.Copy).then_inc(A1.done("u2"), 1)
        after(T1, "o_g")
        nc.scalar.activation(mix[:, :, 0:SEQ], ps[:, 4, :].rearrange("p (a b) -> p a b", a=2),
                             ACT.Copy).then_inc(A1.done("o_g"), 1)
        after(T1, "xt_s")
        nc.scalar.activation(xs, ps[:, 0, :].rearrange("p (a b) -> p a b", a=2), ACT.Copy).then_inc(A1.done("xs"), 1)
        after(V1, "dec_s")
        nc.scalar.activation(dT2, dT2, ACT.Exp).then_inc(A1.done("dec_s"), 1)
        after(V1, "dec_m")
        nc.scalar.activation(dT2, dT2, ACT.Exp, scale=-1.0).then_inc(A1.done("dec_m"), 1)
        after(V1, "negm")
        nc.scalar.activation(em, negm, ACT.Exp).then_inc(A1.done("em"), 1)
        after(T1, "o_m")
        o65 = ps[:, 4:6, 0:H * 65].rearrange("p a (h d) -> p a h d", h=H)
        nc.scalar.activation(den, o65[:, :, :, 64], ACT.Abs).then_inc(A1.done("den"), 1)
        after(T1, "rope_t")
        nc.scalar.activation(dqk.rearrange("p (a i) n -> p a (i n)", a=2), ps[:, 0:2, :], ACT.Copy).then_inc(A1.done("dqk"), 1)
        after(V1, "sub_d")
        nc.scalar.activation(dS, dS, ACT.Exp, scale=32.0 ** -0.5).then_inc(A1.done("exp_d"), 1)
        after(V1, "lam1")
        nc.scalar.activation(lamb[:, 2:4], lamb[:, 0:2], ACT.Exp).then_inc(A1.done("lam"), 1)
        after(T1, "trans_d")
        nc.scalar.activation(pT, ps[:, 0:4, 0:384], ACT.Copy).then_inc(A1.done("pT"), 1)
        after(T1, "o_d")
        nc.scalar.activation(mix[:, :, SEQ:512], ps[:, 4, :].rearrange("p (a b) -> p a b", a=2),
                             ACT.Copy).then_inc(A1.done("o_d"), 1)
        nc.scalar.activation(gate_g, gate_g, ACT.Silu)
        nc.scalar.activation(z_s, z_s, ACT.Silu)
        nc.scalar.activation(o_m, o_m, ACT.Sigmoid).then_inc(A1.done("gates"), 1)
        after(V1, "pre_gate")
        nc.scalar.activation(sq, mix[:], ACT.Square).then_inc(A1.done("sq_o"), 1)
        after(V1, "mean_o")
        nc.scalar.activation(ms, ms, ACT.Sqrt).then_inc(A1.done("root_o"), 1)
        after(T1, "trans")
        dst, src = hT_half(0)
        nc.scalar.activation(dst, src, ACT.Copy).then_inc(A1.done("copy"), 1)

    def rotate(v, V, after, tile, src, dst, cos, sin, half, heads, names, shape):
        na, nb, nc_, nd, ne, nf = names
        x1, x2, y1, y2 = src[0], src[1], dst[0], dst[1]
        nc.vector.tensor_tensor(y1, x1, cos, ALU.mult).then_inc(V.done(na), 1)
        nc.vector.tensor_tensor(half, x2, sin, ALU.mult).then_inc(V.done(nb), 1)
        after(V, nb)
        nc.vector.tensor_tensor(y1, y1, half, ALU.subtract).then_inc(V.done(nc_), 1)
        nc.vector.tensor_tensor(y2, x1, sin, ALU.mult).then_inc(V.done(nd), 1)
        after(V, nc_)
        nc.vector.tensor_tensor(half, x2, cos, ALU.mult).then_inc(V.done(ne), 1)
        after(V, ne)
        nc.vector.tensor_tensor(y2, y2, half, ALU.add).then_inc(V.done(nf), 1)

    def decays(rows_bank, first, buf, col, op0, op1):
        for h in range(H):
            r = ps[:, rows_bank + h // 2, (h % 2) * SEQ:(h % 2) * SEQ + SEQ]
            nc.vector.tensor_scalar(buf[:, h, 0:SEQ], r, col[:, 0, first + h:first + h + 1], 0.0, op0, op1)
            last = nc.vector.tensor_scalar(buf[:, h, SEQ:384], r[:, P:SEQ], col[:, 1, first + h:first + h + 1], 0.0,
                                           op0, op1)
        return last

    def convolve(v, after, chunks, names):
        for c in chunks:
            last = nc.vector.tensor_scalar(cv[:, c, :], u[:, c, 0:SEQ], fp[:, F_CONV + 4 * c:F_CONV + 4 * c + 1],
                                           None, ALU.mult)
        last.then_inc(V1.done(names[0]), 1)
        for k in range(1, 4):
            after(V1, names[k - 1])
            for c in chunks:
                last = nc.vector.scalar_tensor_tensor(cv[:, c, :], u[:, c, k:k + SEQ],
                                                      fp[:, F_CONV + 4 * c + k:F_CONV + 4 * c + k + 1], cv[:, c, :],
                                                      ALU.mult, ALU.add)
            last.then_inc(V1.done(names[k]), 1)

    pm_sq = pm.rearrange("p a b -> p (a b)").rearrange("p (c n) -> p c n", c=4)

    def mixer1_dve(v, l):
        def after(S, name):
            v.wait_ge(S.sem, S.at(name, l))

        v.wait_ge(par_in, l * 32 + 32)
        v.wait_ge(con_in, 16)
        v.wait_ge(pads, 1)
        v.wait_ge(proj_evac, l * IN1 + 3 + 4)
        convolve(v, after, range(0, 6), ("cg0", "cg1", "cg2", "conv_g"))
        v.wait_ge(proj_evac, l * IN1 + 6 + 4)
        convolve(v, after, range(6, 12), ("cs0", "cs1", "cs2", "conv_s"))
        v.wait_ge(proj_evac, l * IN1 + SMALL_AT + 1 + 4)
        nc.vector.tensor_tensor(sp_x, small[:, :, 8:SMALL], over(par[:, R_SPB:R_SPB + 12], [P, TILES, 12], 1),
                                ALU.add).then_inc(V1.done("sp_in"), 1)
        after(V1, "sp_in")
        nc.vector.tensor_tensor(sp_x, sp_x, over(K(C_SGN, 12), [P, TILES, 12], 1), ALU.mult).then_inc(V1.done("sp_sgn"), 1)
        after(V1, "sp_sgn")
        nc.vector.scalar_tensor_tensor(sp_c, sp_x, -1.0, sp_x, ALU.mult, ALU.max).then_inc(V1.done("sp_abs"), 1)
        after(A1, "sp_e")
        nc.vector.tensor_scalar(sp_u, sp_e, 1.0, None, ALU.add).then_inc(V1.done("sp_u"), 1)
        after(V1, "sp_u")
        nc.vector.tensor_scalar(sp_c, sp_u, -1.0, None, ALU.add).then_inc(V1.done("sp_um"), 1)
        after(V1, "sp_um")
        nc.vector.tensor_tensor(sp_e, sp_e, sp_c, ALU.subtract).then_inc(V1.done("sp_em"), 1)
        after(V1, "sp_em")
        nc.vector.reciprocal(sp_c, sp_u).then_inc(V1.done("sp_ru"), 1)
        after(V1, "sp_ru")
        nc.vector.tensor_tensor(sp_e, sp_e, sp_c, ALU.mult).then_inc(V1.done("sp_corr"), 1)
        nc.vector.tensor_scalar(sp_x, sp_x, 0.0, None, ALU.max).then_inc(V1.done("sp_max"), 1)
        after(A1, "sp_l")
        after(V1, "sp_max")
        nc.vector.tensor_tensor(sp_x, sp_x, sp_l, ALU.add).then_inc(V1.done("sp_l"), 1)
        after(V1, "sp_l")
        nc.vector.tensor_tensor(sp_x, sp_x, sp_e, ALU.add).then_inc(V1.done("sp"), 1)
        after(V1, "sp")
        nc.vector.tensor_copy(dt, sp_x[:, :, 4:8]).then_inc(V1.done("dt"), 1)
        after(A1, "ea")
        nc.vector.scalar_tensor_tensor(ld, sp_x, -1.0, over(ea, [P, TILES, 12], 1), ALU.mult,
                                       ALU.mult).then_inc(V1.done("ld"), 1)
        after(A1, "eb")
        nc.vector.tensor_scalar(negm, beta, 1.0, None, ALU.add).then_inc(V1.done("eb1"), 1)
        after(V1, "eb1")
        nc.vector.reciprocal(beta, negm).then_inc(V1.done("beta"), 1)
        after(A1, "gc")
        after(T1, "rows_g")
        decays(4, 0, dT, gc, ALU.subtract, ALU.min).then_inc(V1.done("dec_g"), 1)
        after(T1, "sumsq")
        nc.vector.tensor_scalar(pm_sq.rearrange("p (a c) n -> p a (c n)", a=2), ps[:, 0:2, :], EPS, None,
                                ALU.add).then_inc(V1.done("rs"), 1)
        after(A1, "root")
        nc.vector.reciprocal(pm_sq, pm_sq).then_inc(V1.done("rrs"), 1)
        after(V1, "rrs")
        nc.vector.scalar_tensor_tensor(cv[:, 0:2, :], cv[:, 0:2, :], 64.0 ** -0.5, pm_sq[:, 0:2, :], ALU.mult, ALU.mult)
        nc.vector.tensor_tensor(cv[:, 2:4, :], cv[:, 2:4, :], pm_sq[:, 2:4, :], ALU.mult).then_inc(V1.done("qkn"), 1)
        after(V1, "qkn")
        after(T1, "beta_rows")
        for h in range(H):
            half = slice(64 * (h % 2), 64 * (h % 2) + 64)
            last = nc.vector.tensor_tensor(kb[half, h // 2, :], cv[half, 2 + h // 2, :],
                                           ps[half, 2 + h // 2, (h % 2) * SEQ:(h % 2 + 1) * SEQ], ALU.mult)
        last.then_inc(V1.done("kb"), 1)
        after(G1, "dec_g")
        after(T1, "kk")
        nc.vector.tensor_tensor(lT, ps[:, 0:4, 0:384], dT, ALU.mult).then_inc(V1.done("lT"), 1)
        after(T1, "qk")
        nc.vector.tensor_tensor(dT, ps[:, 4:8, 0:384], dT, ALU.mult).then_inc(V1.done("aT"), 1)
        after(V1, "lT")
        lTd = diag(lT)
        xT4 = xT.rearrange("p (h b) n -> p h b n", h=H)
        nc.vector.tensor_tensor(xT4, lTd, over(K(C_MT), [P, H, 2, P], 1, 1), ALU.mult).then_inc(V1.done("mt1"), 1)
        after(V1, "mt1")
        nc.vector.scalar_tensor_tensor(xT, xT, -1.0, over(IDENT, [P, 8, P], 1), ALU.mult, ALU.add).then_inc(V1.done("xT"), 1)
        with v.Fori(0, LEVELS) as j:
            n = l * LEVELS + j
            v.wait_ge(inv_r, n + 1)
            nc.vector.tensor_tensor(xi.rearrange("p (a i) n -> p a (i n)", a=2),
                                    xi.rearrange("p (a i) n -> p a (i n)", a=2), ps[:, 4:6, :], ALU.subtract)
            nc.vector.tensor_tensor(xT.rearrange("p (a i) n -> p a (i n)", a=2),
                                    xT.rearrange("p (a i) n -> p a (i n)", a=2), ps[:, 6:8, :],
                                    ALU.subtract).then_inc(inv_x, 1)
        after(T1, "vt")
        nc.vector.tensor_tensor(vb.rearrange("p a (h d) -> p (a h) d", h=H),
                                ps[:, 0, :].rearrange("p (i d) -> p i d", d=64),
                                over(beta.rearrange("p a h -> p (a h)"), [P, 8, 64], 2), ALU.mult).then_inc(V1.done("vb"), 1)
        after(T1, "l21")
        nc.vector.tensor_tensor(r2, vb[:, 1, :], ps[:, 2, 0:SEQ], ALU.subtract).then_inc(V1.done("r2"), 1)

        after(A1, "xs")
        nc.vector.tensor_tensor(xdt.rearrange("p a (h d) -> p (a h) d", h=H),
                                xs.rearrange("p a (h d) -> p (a h) d", h=H),
                                over(dt.rearrange("p a h -> p (a h)"), [P, 8, 64], 2), ALU.mult).then_inc(V1.done("xdt"), 1)
        after(T1, "rows_s")
        decays(6, 4, dT2, gc, ALU.subtract, ALU.min).then_inc(V1.done("dec_s"), 1)
        after(G1, "dec_s")
        after(T1, "cb")
        for grp in range(2):
            last = nc.vector.tensor_tensor(dT2[:, 2 * grp:2 * grp + 2, :], over(ps[:, 1 + grp, 0:384], [P, 2, 384], 1),
                                           dT2[:, 2 * grp:2 * grp + 2, :], ALU.mult)
        last.then_inc(V1.done("w_s"), 1)
        nc.vector.tensor_tensor(xs.rearrange("p a (h d) -> p a h d", h=H), xs.rearrange("p a (h d) -> p a h d", h=H),
                                over(par[:, R_DSK:R_DSK + H], [P, TILES, H, 64], 1, 3), ALU.mult).then_inc(V1.done("skip"), 1)
        after(V1, "skip")
        after(T1, "o_s")
        nc.vector.tensor_tensor(mix[:, :, 512:768], xs, ps[:, 3, :].rearrange("p (a b) -> p a b", a=2),
                                ALU.add).then_inc(V1.done("o_s"), 1)

        nc.vector.tensor_tensor(negm, small[:, :, 4:8], over(par[:, R_IB:R_IB + H], [P, TILES, H], 1),
                                ALU.add).then_inc(V1.done("ai"), 1)
        after(V1, "ai")
        nc.vector.tensor_tensor(acol, negm, gc[:, :, 8:12], ALU.subtract).then_inc(V1.done("acol"), 1)
        after(T1, "rows_a")
        tmp = sq_m
        for h in range(H):
            last = nc.vector.tensor_tensor(tmp[:, 2 * h:2 * h + 2, :],
                                           ps[:, 4 + h // 2, (h % 2) * SEQ:(h % 2 + 1) * SEQ].rearrange("p (a n) -> p a n", a=2),
                                           over(NEGM, [P, 2, P], 1), ALU.add)
        last.then_inc(V1.done("tmp_m"), 1)
        after(V1, "tmp_m")
        nc.vector.reduce_max(md.rearrange("p h t -> p (h t)"), tmp, AX).then_inc(V1.done("md"), 1)
        nc.vector.reduce_max(mfull.rearrange("p (a b) -> p a b", a=2),
                             ps[:, 4:6, :].rearrange("p a (b n) -> p a b n", b=2)[:, :, :, 0:P],
                             AX).then_inc(V1.done("mf"), 1)
        after(V1, "mf")
        nc.vector.tensor_scalar(mcol[:, 0, :], md[:, :, 0], 0.0, None, ALU.max).then_inc(V1.done("m0"), 1)
        nc.vector.scalar_tensor_tensor(mcol[:, 1, :], md[:, :, 1], 0.0, mfull, ALU.max, ALU.max).then_inc(V1.done("m1"), 1)
        after(T1, "rows_m")
        decays(6, 0, dT2, acol, ALU.subtract, ALU.max).then_inc(V1.done("dec_m"), 1)
        after(G1, "dec_m")
        after(T1, "qk_m")
        nc.vector.tensor_tensor(dT2, ps[:, 0:4, 0:384], dT2, ALU.mult).then_inc(V1.done("w_m"), 1)
        after(V1, "m1")
        nc.vector.tensor_tensor(negm, mcol, gc[:, :, 8:12], ALU.add).then_inc(V1.done("mt"), 1)
        after(V1, "mt")
        nc.vector.tensor_scalar(negm, negm, -1.0, 85.0, ALU.mult, ALU.min).then_inc(V1.done("negm"), 1)
        after(T1, "o_m")
        o65 = ps[:, 4:6, 0:H * 65].rearrange("p a (h d) -> p a h d", h=H)
        after(A1, "den")
        nc.vector.tensor_tensor(den, den, em, ALU.max).then_inc(V1.done("denm"), 1)
        after(V1, "denm")
        nc.vector.reciprocal(den, den).then_inc(V1.done("rden"), 1)
        after(V1, "rden")
        nc.vector.tensor_tensor(mix[:, :, 768:D].rearrange("p a (h d) -> p a h d", h=H), o65[:, :, :, 0:64],
                                over(den, [P, TILES, H, 64], 3), ALU.mult).then_inc(V1.done("o_m"), 1)

        after(A1, "o_g")
        v.wait_ge(proj_evac, l * IN1 + IN1 + 4)
        for tile in range(TILES):
            s_ = rope_in[:, tile, :].rearrange("p (h z n) -> p h z n", h=16, z=2)
            d_ = qkr[:, tile, :].rearrange("p (h z n) -> p h z n", h=16, z=2)
            names = [f"r{c}{tile + 1}" for c in "abcdef"]
            rotate(v, V1, after, tile, (s_[:, :, 0, :], s_[:, :, 1, :]), (d_[:, :, 0, :], d_[:, :, 1, :]),
                   over(COS[:, tile, :], [P, 16, 16], 1), over(SIN[:, tile, :], [P, 16, 16], 1),
                   rt[:, tile, :].rearrange("p (h n) -> p h n", h=16), 16, names, None)
        after(T1, "sc_d")
        for q in range(2):
            nc.vector.tensor_tensor(dS[:, 4 * q:4 * q + 4, 0:P], ps[:, 0:4, q * P:(q + 1) * P],
                                    over(NEGD[:, 0:P], [P, 4, P], 1), ALU.add)
            last = nc.vector.tensor_tensor(dS[:, 4 * q:4 * q + 4, P:384], ps[:, 4:8, q * SEQ:(q + 1) * SEQ],
                                           over(NEGD[:, P:384], [P, 4, SEQ], 1), ALU.add)
        last.then_inc(V1.done("mask_d"), 1)
        after(V1, "mask_d")
        part = (slice(0, P), slice(P, 384))
        for tile in range(TILES):
            last = nc.vector.reduce_max(rmax[:, tile, :], dS[:, :, part[tile]], AX)
        last.then_inc(V1.done("max_d"), 1)
        after(V1, "max_d")
        for tile in range(TILES):
            w = P if tile == 0 else SEQ
            last = nc.vector.tensor_tensor(dS[:, :, part[tile]], dS[:, :, part[tile]],
                                           over(rmax[:, tile, :], [P, 8, w], 2), ALU.subtract)
        last.then_inc(V1.done("sub_d"), 1)
        after(A1, "exp_d")
        for tile in range(TILES):
            last = nc.vector.reduce_sum(coef[:, tile, :], dS[:, :, part[tile]], AX)
        last.then_inc(V1.done("sum_d"), 1)
        after(V1, "sum_d")
        nc.vector.reciprocal(coef, coef).then_inc(V1.done("rec_d"), 1)
        lam4 = par[:, R_LAM:R_LAM + 128].rearrange("p (a b n) -> p a b n", a=2, b=2)
        nc.vector.tensor_tensor(lamp, lam4[:, :, 0, :], lam4[:, :, 1, :], ALU.mult).then_inc(V1.done("lam0"), 1)
        after(V1, "lam0")
        nc.vector.reduce_sum(lamb[:, 0:2], lamp, AX).then_inc(V1.done("lam1"), 1)
        after(A1, "lam")
        nc.vector.scalar_tensor_tensor(lamb[:, 4:5], lamb[:, 3:4], par[:, R_LI:R_LI + 1], lamb[:, 2:3], ALU.subtract,
                                       ALU.subtract).then_inc(V1.done("lam2"), 1)
        after(V1, "lam2")
        second = coef.rearrange("p a (j c) -> p (a j) c", c=2)[:, :, 1]
        nc.vector.tensor_scalar(second, second, lamb[:, 4:5], None, ALU.mult).then_inc(V1.done("coef"), 1)
        after(V1, "coef")
        for tile in range(TILES):
            w = P if tile == 0 else SEQ
            last = nc.vector.tensor_tensor(dS[:, :, part[tile]], dS[:, :, part[tile]],
                                           over(coef[:, tile, :], [P, 8, w], 2), ALU.mult)
        last.then_inc(V1.done("scale_d"), 1)
        after(V1, "scale_d")
        dS2 = dS.rearrange("p (h c) n -> p h c n", c=2)
        nc.vector.tensor_tensor(pD, dS2[:, :, 0, :], dS2[:, :, 1, :], ALU.add).then_inc(V1.done("add_d"), 1)

        after(A1, "gates")
        nc.vector.tensor_tensor(mix[:, :, 512:768], mix[:, :, 512:768], z_s, ALU.mult)
        nc.vector.tensor_tensor(mix[:, :, 768:D], mix[:, :, 768:D], o_m, ALU.mult).then_inc(V1.done("pre_gate"), 1)
        after(A1, "sq_o")
        nc.vector.reduce_sum(ms.rearrange("p a h -> p (a h)"), sq.rearrange("p a (h d) -> p (a h) d", d=64),
                             AX).then_inc(V1.done("sums_o"), 1)
        after(V1, "sums_o")
        pairs = ms[:, :, 8:12].rearrange("p a (g c) -> p a g c", c=2)
        nc.vector.tensor_tensor(gsum, pairs[:, :, :, 0], pairs[:, :, :, 1], ALU.add).then_inc(V1.done("pair0"), 1)
        after(V1, "pair0")
        nc.vector.tensor_scalar(pairs, over(gsum, [P, TILES, 2, 2], 3), 0.5, None, ALU.mult).then_inc(V1.done("pair1"), 1)
        after(V1, "pair1")
        nc.vector.tensor_scalar(ms, ms, 1.0 / 64, EPS, ALU.mult, ALU.add).then_inc(V1.done("mean_o"), 1)
        after(A1, "root_o")
        nc.vector.reciprocal(ms, ms).then_inc(V1.done("rstd_o"), 1)
        gain = par[:, R_GAIN:R_GAIN + D]
        nc.vector.tensor_scalar(gain[:, SEQ:512], gain[:, SEQ:512], par[:, R_LI + 1:R_LI + 2], None,
                                ALU.mult).then_inc(V1.done("gl"), 1)
        after(V1, "gl")
        mix16 = mix[:].rearrange("p a (h d) -> p (a h) d", d=64)
        nc.vector.tensor_tensor(mix16, mix16, over(ms.rearrange("p a h -> p (a h)"), [P, 32, 64], 2),
                                ALU.mult).then_inc(V1.done("norm_o"), 1)
        after(V1, "norm_o")
        nc.vector.tensor_tensor(mix[:], mix[:], over(gain, [P, TILES, D], 1), ALU.mult).then_inc(V1.done("gain_o"), 1)
        after(V1, "gain_o")
        nc.vector.tensor_tensor(mix[:, :, 0:SEQ], mix[:, :, 0:SEQ], gate_g, ALU.mult).then_inc(V1.done("gate_o"), 1)
        after(T1, "trans")
        dst, src = hT_half(1)
        nc.vector.tensor_copy(dst, src).then_inc(V1.done("copy"), 1)

    sq_m = u[:, 0:8, PAD:PAD + P]
    def mixer1_pool(p, l):
        def after(S, name):
            p.wait_ge(S.sem, S.at(name, l))

        def mask(buf):
            d_ = diag(buf)
            return nc.gpsimd.tensor_tensor(d_, d_, over(TRIU, [P, H, 2, P], 1, 1), ALU.mult)

        p.wait_ge(con_in, 16)
        after(A1, "dec_g")
        mask(dT).then_inc(G1.done("dec_g"), 1)
        after(V1, "xT")
        lTd = diag(lT)
        bT4 = bT.rearrange("p (h b) n -> p h b n", h=H)
        settle(p)
        with p.Fori(0, LEVELS) as j:
            n = l * LEVELS + j
            p.wait_ge(inv_p, n + 1)
            lev = con[:, bass.ds(j * P + (C_MT + P - NBASE), P)]
            nc.gpsimd.tensor_tensor(bT4, lTd, over(lev, [P, H, 2, P], 1, 1), ALU.mult).then_inc(inv_b, 1)
        after(A1, "dec_s")
        mask(dT2).then_inc(G1.done("dec_s"), 1)
        after(A1, "dec_m")
        mask(dT2).then_inc(G1.done("dec_m"), 1)

    m2 = Arena()
    con2 = m2.take(N2)
    ada = m2.take(3, D)
    mrow = m2.take(3, D)
    brow = mrow
    cond = m2.take(KT)
    rot_in = m2.take(TILES, 4 * SEQ)
    rot = m2.take(TILES, 4 * SEQ)
    half = m2.take(TILES, 512)
    rqk = m2.take(8, SEQ)
    sqk = m2.take(4, SEQ)
    v_r, g_r = m2.take(TILES, 512), m2.take(TILES, 512)
    v_2, v_b = m2.take(TILES, SEQ), m2.take(TILES, SEQ)
    b1, b2, b3 = (m2.take(H, 384) for _ in range(3))
    bn8 = m2.take(8, 6)
    mv8 = m2.take(8, 2)
    rstd8 = m2.take(8)
    max2 = m2.take(TILES, H)
    sum2 = m2.take(TILES, H)
    SL, NEGC, CNT = con2[:, C2_SL:C2_SL + P], con2[:, C2_NEGC:C2_NEGC + 384], con2[:, C2_CNT:C2_CNT + 384]
    RET = con2[:, C2_RET:C2_RET + H * 384].rearrange("p (h n) -> p h n", h=H)
    ROT = con2[:, C2_ROT:C2_ROT + 256].rearrange("p (z t k n) -> p z t k n", z=2, t=2, k=2)
    c_in, cond_done = sem("c_in"), sem("cond_done")
    ada_acc = sem("ada_acc")
    brow_in, mod_t = sem("brow_in"), sem("mod_t")
    T2 = steps("mix2_t", "qkt sc_r o_r sc_d zt trans_d o_d between o_b trans")
    A2 = steps("mix2_a", "rqk gate root_r exp_d abs_b e_b l_b pT exp_b o_b copy")
    V2 = steps("mix2_v", "ra1 rb1 rc1 rd1 re1 rf1 ra2 rb2 rc2 rd2 re2 rf2 w_r stats_r aggr_r var_r rstd_r norm_r "
                         "mask_d max_d sub_d cnt_d sum_d rec_d sp_b t_b o_d exp_arg gated copy")
    G2 = steps("mix2_g", "keep a")
    RING1 = DEPTH * (U1 // RING)
    ADA_TURNS = 3 * NADA // 3 // 3
    PER2 = 3 * ADA_TURNS + U2 // RING
    TURN0 = (0, ADA_TURNS, 2 * ADA_TURNS + U2 // RING)

    def mod_sp(sp, l, pos):
        h = l * 3 + pos
        sp.wait_ge(ring_used, l * U2 + (DEPTH * U1 + RING + (U2 if pos == 2 else 0)))
        settle(sp)
        with sp.Fori(0, 3) as k:
            for q in range(ADAQ):
                sp.wait_ge(ada_acc, (h * 3 + k) * 8 + (2 * q + 2))
                settle(sp)
                ring_load(sp, q, t["w_ada"][bass.ds(l, 1), bass.ds(k + 3 * pos, 1), q:q + 1, :, :]
                          .rearrange("l i q p n -> p (l i q n)"))
        sp.wait_ge(x_ready, (h + 6) * 16 + 16)
        settle(sp)
        sp.dma_start(brow[0:1, :, :].rearrange("p a b -> p (a b)"),
                     t["b_ada"][bass.ds(l, 1), pos * 3 * D:(pos + 1) * 3 * D]).then_inc(brow_in, 16)

    def mod_dve(v, l, pos, weight):
        h = l * 3 + pos
        v.wait_ge(cond_done, 1)
        flat = ada.rearrange("p a b -> p (a b)")
        with v.Fori(0, 3) as k:
            to = flat[:, bass.ds(k * D, D)]
            for q in range(ADAQ):
                v.wait_ge(ring_in[q], (l * PER2 + k) * 16 + (RING1 + TURN0[pos] + 1) * 16)
                for kk in range(2):
                    w = ring[:, q, kk * D:(kk + 1) * D]
                    c = cond[:, 2 * q + kk:2 * q + kk + 1]
                    if q == kk == 0:
                        nc.vector.tensor_scalar(to, w, c, None, ALU.mult).then_inc(ada_acc, 1)
                    else:
                        v.wait_ge(ada_acc, (h * 3 + k) * 8 + (8 + 2 * q + kk))
                        nc.vector.scalar_tensor_tensor(to, w, c, to, ALU.mult, ALU.add).then_inc(ada_acc, 1)
        v.wait_ge(mod_t, h + 1)
        two = "p (b n) -> p b n"
        nc.vector.tensor_copy(mrow[:, 0, :].rearrange(two, b=2), ps[:, 0:2, :]).then_inc(mod_v.done("shift"), 1)
        nc.vector.tensor_scalar(mrow[:, 1, :].rearrange(two, b=2), ps[:, 2:4, :], 1.0, None,
                                ALU.add).then_inc(mod_v.done("scale"), 1)
        nc.vector.tensor_scalar(mrow[:, 2, :].rearrange(two, b=2), ps[:, 4:6, :], 1.0, weight, ALU.add,
                                ALU.mult).then_inc(mod_v.done("rows"), 1)

    def mod_pe(pe, l, pos):
        h = l * 3 + pos
        pe.wait_ge(ada_acc, h * 24 + 32)
        pe.wait_ge(brow_in, h * 16 + 16)
        pe.wait_ge(x_ready, (h + 6) * 16 + 16)
        for b in range(6):
            c = slice((b % 2) * 512, (b % 2 + 1) * 512)
            nc.tensor.matmul(ps[:, b, :], ONES, ada[:, b // 2, c], start=True, stop=False)
            last = nc.tensor.matmul(ps[:, b, :], ONES[0:1, :], brow[0:1, b // 2, c], start=False, stop=True)
        last.then_inc(mod_t, 1)

    def mixer2_sp(sp, l):
        sp.wait_ge(ada_acc, (l * 3 + 2) * 24 + 8)
        settle(sp)
        for n in range(U2):
            sp.wait_ge(ring_used, l * U2 + (DEPTH * U1 + n + 1))
            name, i = ("w_in_2", n) if n < IN2 else ("w_out_2", n - IN2)
            ring_load(sp, n % RING, t[name][bass.ds(l, 1), i:i + 1, :, :].rearrange("l i p n -> p (l i n)"))

    def mixer2_pe(pe, l, g):
        def after(S, name):
            pe.wait_ge(S.sem, S.at(name, l))

        done = l * PER2 + (RING1 + TURN0[1] + ADA_TURNS)
        pe.wait_ge(pre_a.sem, pre_a.at("copy", g))
        pe.wait_ge(pre_v.sem, pre_v.at("copy", g))
        for n in range(IN2):
            slot, turn = block_of(n)
            pe.wait_ge(ring_in[slot], ring_value(slot, done, turn))
            pe.wait_ge(proj_evac, l * IN2 + (DEPTH * IN1 + n + 1))
            if n in (4, 5):
                last = feature_product(4 + n % 4, slot, n)
            else:
                last = token_product(4 + n % 4, slot)
            last.then_inc(ring_used, 1)
        pe.wait_ge(proj_evac, l * IN2 + (DEPTH * IN1 + IN2 + 4))

        after(V2, "rf2")
        for c in range(8):
            for tile in range(TILES):
                o = (c % 2) * SEQ + tile * P
                last = nc.tensor.transpose(ps[:, c // 2, o:o + P], rot[:, tile, c * P:(c + 1) * P], IDENT)
        last.then_inc(T2.done("qkt"), 1)
        after(A2, "rqk")
        for h in range(H):
            hf = slice(64 * (h % 2), 64 * (h % 2) + 64)
            last = scores_T(4 + h, rqk[hf, 2 + h // 2, :], rqk[hf, h // 2, :], h)
        last.then_inc(T2.done("sc_r"), 1)
        after(V2, "w_r")
        for h in range(H):
            c = slice(h * P, (h + 1) * P)
            last = weighted_values(ps[:, 0, c], ps[:, 1, c], b1[:, h, :], v_r[:, 0, c], v_r[:, 1, c])
        last.then_inc(T2.done("o_r"), 1)
        for h in range(H):
            hf = slice(64 * (h % 2), 64 * (h % 2) + 64)
            q_, k_ = rqk[hf, 4 + h // 2, :], rqk[hf, 6 + h // 2, :]
            nc.tensor.matmul(ps[:, 4 + h, 0:P], q_[:, 0:P], k_[:, 0:P], start=True, stop=True)
            last = nc.tensor.matmul(ps[:, 4 + h, P:384], q_[:, P:SEQ], k_, start=True, stop=True)
        last.then_inc(T2.done("sc_d"), 1)
        after(V2, "mask_d")
        for h in range(H):
            hf = slice(64 * (h % 2), 64 * (h % 2) + 64)
            last = scores_T(4 + h, sqk[hf, 2 + h // 2, :], sqk[hf, h // 2, :], h)
        last.then_inc(T2.done("zt"), 1)
        after(V2, "norm_r")
        after(V2, "cnt_d")
        for h in range(H):
            for b in range(3):
                last = nc.tensor.transpose(ps[:, h, b * P:(b + 1) * P], b1[:, h, b * P:(b + 1) * P], IDENT)
        last.then_inc(T2.done("trans_d"), 1)
        after(A2, "pT")
        after(V2, "t_b")
        for h in range(H):
            c = slice(h * 64, (h + 1) * 64)
            last = weighted_values(ps[:, 4, c], ps[:, 4, SEQ + h * 64:SEQ + (h + 1) * 64], b2[:, h, :],
                                   v_2[:, 0, c], v_2[:, 1, c])
        last.then_inc(T2.done("o_d"), 1)
        after(G2, "keep")
        for h in range(H):
            nc.tensor.matmul(ps[:, h, 0:384], SL, b3[:, h, :], start=True, stop=False)
            last = nc.tensor.matmul(ps[:, h, P:SEQ], ONES, b3[:, h, SEQ:384], start=False, stop=True)
        last.then_inc(T2.done("between"), 1)
        after(G2, "a")
        for h in range(H):
            c = slice(h * 64, (h + 1) * 64)
            last = weighted_values(ps[:, 5, c], ps[:, 5, SEQ + h * 64:SEQ + (h + 1) * 64], b1[:, h, :],
                                   v_b[:, 0, c], v_b[:, 1, c])
        last.then_inc(T2.done("o_b"), 1)
        after(A2, "o_b")
        after(V2, "gated")
        transposes_pe().then_inc(T2.done("trans"), 1)
        after(A2, "copy")
        after(V2, "copy")
        out_product(pe, IN2, done)

    def mixer2_act(a, l):
        def after(S, name):
            a.wait_ge(S.sem, S.at(name, l))

        for n in range(IN2):
            a.wait_ge(ring_used, l * U2 + (DEPTH * U1 + n + 1 + RING))
            two = ps[:, 4 + n % 4, :].rearrange("p (a b) -> p a b", a=2)
            if n < 4:
                last = nc.scalar.activation(rot_in[:, :, n * SEQ:(n + 1) * SEQ], two, ACT.Copy)
            elif n < 6:
                last = nc.scalar.activation(sqk[:, 2 * (n - 4):2 * (n - 4) + 2, :], two, ACT.Copy,
                                            scale=64.0 ** -0.5 if n == 4 else 1.0)
            elif n < 8:
                last = nc.scalar.activation(v_r[:, :, (n - 6) * SEQ:(n - 5) * SEQ], two, ACT.Copy)
            elif n < 10:
                last = nc.scalar.activation(g_r[:, :, (n - 8) * SEQ:(n - 7) * SEQ], two, ACT.Copy)
            else:
                last = nc.scalar.activation(v_2 if n == 10 else v_b, two, ACT.Copy)
            last.then_inc(proj_evac, 1)
        after(T2, "qkt")
        nc.scalar.activation(rqk.rearrange("p (a i) n -> p a (i n)", a=4), ps[:, 0:4, :], ACT.Copy).then_inc(A2.done("rqk"), 1)
        a.wait_ge(proj_evac, l * IN2 + (DEPTH * IN1 + IN2 + 4))
        nc.scalar.activation(g_r, g_r, ACT.Silu).then_inc(A2.done("gate"), 1)
        after(V2, "var_r")
        nc.scalar.activation(rstd8, rstd8, ACT.Sqrt).then_inc(A2.done("root_r"), 1)
        after(V2, "sub_d")
        nc.scalar.activation(b1, b1, ACT.Exp, scale=64.0 ** -0.5).then_inc(A2.done("exp_d"), 1)
        after(T2, "zt")
        nc.scalar.activation(b3, ps[:, 4:8, 0:384], ACT.Abs).then_inc(A2.done("abs_b"), 1)
        after(A2, "abs_b")
        nc.scalar.activation(b3, b3, ACT.Exp, scale=-1.0).then_inc(A2.done("e_b"), 1)
        after(A2, "e_b")
        nc.scalar.activation(b3, b3, ACT.Ln, bias=one[:, 0:1]).then_inc(A2.done("l_b"), 1)
        after(T2, "trans_d")
        nc.scalar.activation(b2, ps[:, 0:4, 0:384], ACT.Copy).then_inc(A2.done("pT"), 1)
        after(V2, "exp_arg")
        nc.scalar.activation(b1, b1, ACT.Exp).then_inc(A2.done("exp_b"), 1)
        after(T2, "o_b")
        nc.scalar.activation(mix[:, :, 768:D], ps[:, 5, :].rearrange("p (a b) -> p a b", a=2),
                             ACT.Copy).then_inc(A2.done("o_b"), 1)
        after(T2, "trans")
        dst, src = hT_half(0)
        nc.scalar.activation(dst, src, ACT.Copy).then_inc(A2.done("copy"), 1)

    def mixer2_dve(v, l):
        def after(S, name):
            v.wait_ge(S.sem, S.at(name, l))

        v.wait_ge(proj_evac, l * IN2 + (DEPTH * IN1 + 4 + 4))
        for tile in range(TILES):
            s_ = rot_in[:, tile, :].rearrange("p (k h z n) -> p k h z n", k=2, h=8, z=2)
            d_ = rot[:, tile, :].rearrange("p (k h z n) -> p k h z n", k=2, h=8, z=2)
            rotate(v, V2, after, tile, (s_[:, :, :, 0, :], s_[:, :, :, 1, :]), (d_[:, :, :, 0, :], d_[:, :, :, 1, :]),
                   over(ROT[:, 0, tile, :, :], [P, 2, 8, 32], 2), over(ROT[:, 1, tile, :, :], [P, 2, 8, 32], 2),
                   half[:, tile, :].rearrange("p (k h n) -> p k h n", k=2, h=8), 16,
                   [f"r{c}{tile + 1}" for c in "abcdef"], None)
        after(T2, "sc_r")
        nc.vector.tensor_tensor(b1, ps[:, 4:8, 0:384], RET, ALU.mult).then_inc(V2.done("w_r"), 1)
        after(T2, "o_r")
        for i in range(8):
            last = nc.vector.bn_stats(bn8[:, i, :], ps[:, i // 4, (i % 4) * P:(i % 4 + 1) * P])
        last.then_inc(V2.done("stats_r"), 1)
        after(V2, "stats_r")
        settle(v)
        for i in range(8):
            last = nc.vector.bn_aggr(mv8[:, i, :], bn8[:, i, :])
        last.then_inc(V2.done("aggr_r"), 1)
        after(V2, "aggr_r")
        nc.vector.tensor_scalar(rstd8, mv8[:, :, 1], EPS, None, ALU.add).then_inc(V2.done("var_r"), 1)
        after(A2, "root_r")
        nc.vector.reciprocal(rstd8, rstd8).then_inc(V2.done("rstd_r"), 1)
        after(V2, "rstd_r")
        for i in range(8):
            last = nc.vector.tensor_scalar(mix[:, i // 4, (i % 4) * P:(i % 4 + 1) * P],
                                           ps[:, i // 4, (i % 4) * P:(i % 4 + 1) * P], mv8[:, i, 0:1],
                                           rstd8[:, i:i + 1], ALU.subtract, ALU.mult)
        last.then_inc(V2.done("norm_r"), 1)
        part = (slice(0, P), slice(P, 384))
        after(T2, "sc_d")
        nc.vector.tensor_tensor(b1, ps[:, 4:8, 0:384], over(NEGC, [P, H, 384], 1), ALU.add).then_inc(V2.done("mask_d"), 1)
        after(V2, "mask_d")
        for tile in range(TILES):
            last = nc.vector.reduce_max(max2[:, tile, :], b1[:, :, part[tile]], AX)
        last.then_inc(V2.done("max_d"), 1)
        after(V2, "max_d")
        for tile in range(TILES):
            w = P if tile == 0 else SEQ
            last = nc.vector.tensor_tensor(b1[:, :, part[tile]], b1[:, :, part[tile]],
                                           over(max2[:, tile, :], [P, H, w], 2), ALU.subtract)
        last.then_inc(V2.done("sub_d"), 1)
        after(A2, "exp_d")
        nc.vector.tensor_tensor(b1, b1, over(CNT, [P, H, 384], 1), ALU.mult).then_inc(V2.done("cnt_d"), 1)
        after(V2, "cnt_d")
        for tile in range(TILES):
            last = nc.vector.reduce_sum(sum2[:, tile, :], b1[:, :, part[tile]], AX)
        last.then_inc(V2.done("sum_d"), 1)
        after(V2, "sum_d")
        nc.vector.reciprocal(sum2, sum2).then_inc(V2.done("rec_d"), 1)
        after(A2, "l_b")
        nc.vector.scalar_tensor_tensor(b3, ps[:, 4:8, 0:384], 0.0, b3, ALU.max, ALU.add).then_inc(V2.done("sp_b"), 1)
        after(V2, "sp_b")
        after(T2, "trans_d")
        nc.vector.tensor_tensor(b1, ps[:, 4:8, 0:384], b3, ALU.subtract).then_inc(V2.done("t_b"), 1)
        after(T2, "o_d")
        nc.vector.tensor_tensor(mix[:, :, 512:768].rearrange("p a (h d) -> p a h d", h=H),
                                ps[:, 4, :].rearrange("p (a h d) -> p a h d", a=2, h=H),
                                over(sum2, [P, TILES, H, 64], 3), ALU.mult).then_inc(V2.done("o_d"), 1)
        after(T2, "between")
        nc.vector.tensor_tensor(b1, b1, ps[:, 0:4, 0:384], ALU.subtract).then_inc(V2.done("exp_arg"), 1)
        after(A2, "gate")
        nc.vector.tensor_tensor(mix[:, :, 0:512], mix[:, :, 0:512], g_r, ALU.mult).then_inc(V2.done("gated"), 1)
        after(T2, "trans")
        dst, src = hT_half(1)
        nc.vector.tensor_copy(dst, src).then_inc(V2.done("copy"), 1)

    def mixer2_pool(p, l):
        def after(S, name):
            p.wait_ge(S.sem, S.at(name, l))

        after(V2, "t_b")
        d_ = diag(b3)
        nc.gpsimd.tensor_tensor(d_, d_, over(SU, [P, H, 2, P], 1, 1), ALU.mult).then_inc(G2.done("keep"), 1)
        after(A2, "exp_b")
        d_ = diag(b1)
        nc.gpsimd.tensor_tensor(d_, d_, over(SU, [P, H, 2, P], 1, 1), ALU.mult).then_inc(G2.done("a"), 1)

    one = sb("one", [P, 1])
    first = sb("first", [P, 10])
    one_set = sem("one_set")
    out_sent = sem("out_sent")

    def rows_load(sp, L, pos):
        sp.dma_start(rows[:, pos % 2, :, :].rearrange("p a b -> p (a b)"),
                     t["rows"][bass.ds(L * 3 + pos, 1), :].to_broadcast([P, 2 * D])).then_inc(rows_in[pos % 2], 16)

    block = ctx.enter_context(nc.Block())

    @block.sync
    def _(sp):
        sp.dma_start(x[:], t["x"].rearrange("(a p) d -> p a d", p=P)).then_inc(x_ready, 16)
        sp.dma_start(base[:], t["con1"][:, 0:NBASE]).then_inc(base_in, 16)
        sp.dma_start(con, t["con1"][:, NBASE:N1]).then_inc(con_in, 16)
        with sp.Fori(0, DEPTH) as l:
            L = l
            sp.wait_ge(x_ready, L * 48 + 16)
            rows_load(sp, L, 0)
            rows_load(sp, L, 1)
            sp.dma_start(par, t["par"][bass.ds(l, 1), :].to_broadcast([P, NR])).then_inc(par_in, 16)
            sp.dma_start(fp, t["fpar"][bass.ds(l, 1), :, :].rearrange("l p n -> p (l n)")).then_inc(par_in, 16)
            ffn_sp(sp, l * 2, l, t["g1"], t["u1"], t["d1"])
            mixer1_sp(sp, l)
            sp.wait_ge(x_ready, L * 48 + 32)
            rows_load(sp, L, 2)
            ffn_sp(sp, l * 2 + 1, l, t["g2"], t["u2"], t["d2"])
        sp.wait_ge(x_ready, DEPTH * 48 + 16)
        sp.dma_start(con2, t["con2"][:, :]).then_inc(con_in, 16)
        sp.dma_start(cond, t["c"][:, :]).then_inc(c_in, 16)
        with sp.Fori(0, DEPTH) as l:
            L = l + DEPTH
            sp.wait_ge(x_ready, L * 48 + 16)
            rows_load(sp, L, 0)
            rows_load(sp, L, 1)
            mod_sp(sp, l, 0)
            ffn_sp(sp, l * 2 + 4, l, t["g3"], t["u3"], t["d3"])
            mod_sp(sp, l, 1)
            mixer2_sp(sp, l)
            sp.wait_ge(x_ready, L * 48 + 32)
            rows_load(sp, L, 2)
            mod_sp(sp, l, 2)
            ffn_sp(sp, l * 2 + 5, l, t["g4"], t["u4"], t["d4"])
        sp.wait_ge(x_ready, 12 * 16 + 16)
        sp.dma_start(out.rearrange("(a p) d -> p a d", p=P), x[:]).then_inc(out_sent, 16)
        sp.wait_ge(out_sent, 16)

    @block.tensor
    def _(pe):
        pe.wait_ge(base_in, 16)
        with pe.Fori(0, DEPTH) as l:
            g = l * 3
            pre_pe(pe, g)
            ffn_pe(pe, l * 2, g)
            pre_pe(pe, g + 1)
            mixer1_pe(pe, l, g + 1)
            pre_pe(pe, g + 2)
            ffn_pe(pe, l * 2 + 1, g + 2)
        with pe.Fori(0, DEPTH) as l:
            g = l * 3 + 6
            mod_pe(pe, l, 0)
            pre_pe(pe, g)
            ffn_pe(pe, l * 2 + 4, g)
            mod_pe(pe, l, 1)
            pre_pe(pe, g + 1)
            mixer2_pe(pe, l, g + 1)
            mod_pe(pe, l, 2)
            pre_pe(pe, g + 2)
            ffn_pe(pe, l * 2 + 5, g + 2)

    @block.scalar
    def _(a):
        a.wait_ge(one_set, 1)
        with a.Fori(0, DEPTH) as l:
            g = l * 3
            pre_act(a, g, True)
            ffn_act(a, l * 2)
            post_act(a, g, (down_done, (l * 2 + 1) * NF + 1))
            pre_act(a, g + 1, True)
            mixer1_act(a, l)
            post_act(a, g + 1, (ring_used, l * U1 + (U1 + RING)))
            pre_act(a, g + 2, True)
            ffn_act(a, l * 2 + 1)
            post_act(a, g + 2, (down_done, (l * 2 + 2) * NF + 1))
        a.wait_ge(c_in, 16)
        nc.scalar.activation(cond, cond, ACT.Silu).then_inc(cond_done, 1)
        with a.Fori(0, DEPTH) as l:
            g = l * 3 + 6
            h = l * 3
            pre_act(a, g, False)
            ffn_act(a, l * 2 + 4)
            ln_act(a, h)
            pre_act(a, g + 1, False)
            mixer2_act(a, l)
            ln_act(a, h + 1)
            pre_act(a, g + 2, False)
            ffn_act(a, l * 2 + 5)
            ln_act(a, h + 2)

    @block.vector
    def _(v):
        nc.vector.memset(zero[:], 0.0).then_inc(zero_set, 1)
        nc.vector.memset(one[:], 1.0).then_inc(one_set, 1)
        nc.vector.memset(v_m[:, :, :, 64:65], 1.0)
        nc.vector.memset(u[:, :, 0:PAD], 0.0).then_inc(pads, 1)
        for i, (credit, n) in enumerate(((gate_done, 1), (up_done, 1), (down_done, 1), (silu_done, 1), (act_ready, 1),
                          (ring_used, RING), (proj_evac, 4), (inv_x, 1), (inv_p, 1), (ada_acc, 8))):
            nc.vector.memset(first[:, i:i + 1], 0.0).then_inc(credit, n)
        with v.Fori(0, DEPTH) as l:
            g = l * 3
            pre_dve(v, l, 0, True)
            ffn_dve(v, l * 2)
            post_dve(v, g, 0, 0.5)
            pre_dve(v, l, 1, True)
            mixer1_dve(v, l)
            post_dve(v, g + 1, 1, 1.0)
            pre_dve(v, l, 2, True)
            ffn_dve(v, l * 2 + 1)
            post_dve(v, g + 2, 2, 0.5)
        v.wait_ge(con_in, 32)
        with v.Fori(0, DEPTH) as l:
            L = l + DEPTH
            h = l * 3
            mod_dve(v, l, 0, 0.5)
            pre_dve(v, L, 0, False)
            ffn_dve(v, l * 2 + 4)
            ln_dve(v, h, 0, (down_done, (l * 2 + 5) * NF + 1), mrow[:, 2, :])
            mod_dve(v, l, 1, 1.0)
            pre_dve(v, L, 1, False)
            mixer2_dve(v, l)
            ln_dve(v, h + 1, 1, (ring_used, l * U2 + (DEPTH * U1 + U2 + RING)), mrow[:, 2, :])
            mod_dve(v, l, 2, 0.5)
            pre_dve(v, L, 2, False)
            ffn_dve(v, l * 2 + 5)
            ln_dve(v, h + 2, 2, (down_done, (l * 2 + 6) * NF + 1), mrow[:, 2, :])

    @block.gpsimd
    def _(p):
        with p.Fori(0, DEPTH) as l:
            mixer1_pool(p, l)
        with p.Fori(0, DEPTH) as l:
            mixer2_pool(p, l)

    ctx.close()


def tables():
    f32 = np.float32
    i = np.arange(P)
    k, n = i[:, None], i[None, :]
    con = np.zeros((P, N1), f32)
    con[:, C_IDENT:C_IDENT + P] = k == n
    con[:, C_TRIU:C_TRIU + P] = k <= n
    con[:, C_ONES:C_ONES + P] = 1
    con[:, C_SU:C_SU + P] = k < n
    con[:, C_BLOCK:C_BLOCK + P] = k // 64 == n // 64
    for j in range(7):
        s = 1 << j
        con[:, C_MT + j * P:C_MT + (j + 1) * P] = (k // (2 * s) == n // (2 * s)) & (n // s % 2 == 1) & (k // s % 2 == 0)
    con[:, C_NEGM:C_NEGM + P] = np.where(n > k, NEG, 0)
    key = np.arange(SEQ)[None, :]
    negd = [np.where(key // 64 > (k + tile * P) // 64, NEG, 0) for tile in range(TILES)]
    con[:, C_NEGD:C_NEGD + 384] = np.concatenate([negd[0][:, :P], negd[1]], 1)
    con[:, C_SGN:C_SGN + 12] = [1] * 8 + [-1] * 4

    def angles(freq):
        a = np.arange(SEQ, dtype=f32)[:, None] * freq[None, :]
        return np.cos(a).astype(f32), np.sin(a).astype(f32)

    def tiled(a):
        return a.reshape(TILES, P, -1).transpose(1, 0, 2)

    c, s = angles((f32(10000.0) ** (-np.arange(0, 32, 2, dtype=f32) / f32(32))).astype(f32))
    con[:, C_ROPE:C_ROPE + 32] = tiled(c).reshape(P, -1)
    con[:, C_ROPE + 32:C_ROPE + 64] = tiled(s).reshape(P, -1)

    con2 = np.zeros((P, N2), f32)
    con2[:, C2_SL:C2_SL + P] = k > n
    tq = k + np.array([0, P])[:, None, None]
    dist = tq - key[None]
    cnt = sum(((dist >= 0) & (dist % dl == 0) & (dist <= w)).astype(f32)
              for w, dl in ((128, 1), (512, 4), (2048, 16)))
    cnt = np.concatenate([cnt[0][:, :P], cnt[1]], 1)
    con2[:, C2_CNT:C2_CNT + 384] = cnt
    con2[:, C2_NEGC:C2_NEGC + 384] = np.where(cnt > 0, 0, NEG)
    lg = np.log1p(-np.exp2(-5.0 - np.arange(H)))
    d0 = key - k
    dd = np.concatenate([d0, d0[:, :P]], 1)
    ret = np.where(dd >= 0, np.exp(lg[:, None, None] * np.maximum(dd, 0)), 0) * 64.0 ** -0.5
    con2[:, C2_RET:C2_RET + H * 384] = ret.transpose(1, 0, 2).reshape(P, -1)
    rf = (1.0 / f32(10000.0) ** np.linspace(0.0, 1.0, 32, dtype=f32)).astype(f32)
    pf = (1.0 / f32(10000.0) ** (np.arange(0, 64, 2, dtype=f32) / f32(64))).astype(f32)
    kinds = [angles(rf), angles(pf)]
    rot = np.stack([np.stack([tiled(kd[z]) for kd in kinds], 2) for z in range(2)], 1)
    con2[:, C2_ROT:C2_ROT + 256] = rot.reshape(P, -1)
    return con, con2


def column_tiles(w, width=FB):
    L_, k, n = w.shape
    return np.ascontiguousarray(w.reshape(L_, k // P, P, n // width, width).transpose(0, 3, 2, 1, 4)
                                .reshape(L_, n // width, P, -1))


def row_tiles(w):
    L_, k, n = w.shape
    return np.ascontiguousarray(w.reshape(L_, k // 256, 2, P, n).transpose(0, 1, 3, 2, 4).reshape(L_, k // 256, P, -1))


def layout(i):
    con, con2 = tables()
    a = {"x": i["x"][0], "con1": con, "con2": con2}
    for n, (s, sfx) in enumerate((("ffn1", ""), ("ffn2", ""), ("ffn1", "_2"), ("ffn2", "_2"))):
        a[f"g{n + 1}"] = column_tiles(i[f"{s}_w_gate{sfx}"])
        a[f"u{n + 1}"] = column_tiles(i[f"{s}_w_up{sfx}"])
        a[f"d{n + 1}"] = row_tiles(i[f"{s}_w_down{sfx}"])
    w = i["w_in"]
    big = [0, 256, 512, 2056, 2312, 2568, 2828, 3084, 768, 1032, 1288, 1544, 1800, 3340, 3596]
    a["w_in"] = column_tiles(np.concatenate([w[:, :, c:c + 256] for c in big], 2))
    ws = np.concatenate([w[:, :, 1024:1028], w[:, :, 3852:3856], w[:, :, 1028:1032], w[:, :, 2824:2828],
                         w[:, :, 3856:3860]], 2)
    a["w_small"] = column_tiles(ws, SMALL)[:, 0]
    a["w_out"] = row_tiles(i["w_out"])
    w = i["w_in_2"]
    a["w_in_2"] = column_tiles(np.concatenate([w[:, :, c:c + 256] for c in
                                               (0, 256, 1536, 1792, 2304, 2560, 512, 768, 1024, 1280, 2048, 2816)], 2))
    a["w_out_2"] = row_tiles(i["w_out_2"])
    a["w_ada"] = np.ascontiguousarray(i["w_ada_2"].reshape(DEPTH, ADAQ, 2, P, NADA, D).transpose(0, 4, 1, 3, 2, 5)
                                      .reshape(DEPTH, NADA, ADAQ, P, 2 * D))
    a["b_ada"] = i["b_ada_2"]
    a["c"] = np.ascontiguousarray(i["c_2"].reshape(KT, P).T)
    r1 = np.stack([np.stack([i[f"{s}_pre_g"], i[f"{s}_post_g"]], 1) for s in ("ffn1", "mix", "ffn2")], 1)
    r2 = np.stack([i["ln_gain_2"], i["ln_bias_2"]], 2)
    a["rows"] = np.concatenate([r1, r2]).reshape(4 * 3, 2 * D)
    zeros = np.zeros((DEPTH, H), np.float32)
    li = np.array([[0.8 - 0.6 * np.exp(-0.3 * l)] for l in range(DEPTH)])
    one_less = (1.0 - li).astype(np.float32)
    tile4 = lambda v: np.concatenate([v] * H, 1)
    a["par"] = np.concatenate([
        i["gdn_dt_bias"], i["ssd_dt_bias"], i["mlstm_f_bias"], i["gdn_a_log"], i["ssd_a_log"], zeros,
        i["mlstm_i_bias"], i["ssd_d"], i["diff_lam_q1"], i["diff_lam_k1"], i["diff_lam_q2"], i["diff_lam_k2"],
        li.astype(np.float32), one_less,
        tile4(i["gdn_norm_g"]), tile4(i["diff_norm_g"]), i["ssd_norm_g"], i["mlstm_norm_g"]], 1)
    taps = np.concatenate([i["gdn_conv_w"], i["ssd_conv_w"]], 2).reshape(DEPTH, 4, 12, P).transpose(0, 3, 2, 1)
    a["fpar"] = np.concatenate([taps.reshape(DEPTH, P, 48), i["ssd_conv_b"].reshape(DEPTH, 6, P).transpose(0, 2, 1)], 2)
    return {k: np.ascontiguousarray(v, dtype=np.float32) for k, v in a.items()}


def kernel(**inputs):
    import concourse.bacc as _bacc
    from concourse.bass_utils import run_bass_kernel_spmd as _run

    arrays = layout({k: np.asarray(v) for k, v in inputs.items()})
    nc = _bacc.Bacc("TRN2", target_bir_lowering=False, num_devices=1)
    t = {k: nc.dram_tensor(f"in_{k}", v.shape, F32, kind="ExternalInput").ap() for k, v in arrays.items()}
    out = nc.dram_tensor("out", (SEQ, D), F32, kind="ExternalOutput").ap()
    build(nc, t, out)
    r = _run(nc, [{f"in_{k}": v for k, v in arrays.items()}], core_ids=[0])
    return r.results[0]["out"].reshape(1, SEQ, D)
```

```python
from contextlib import ExitStack

import numpy as np

import concourse.bass as bass
from concourse import mybir

F32 = mybir.dt.float32
F32R = mybir.dt.float32r
BF16 = mybir.dt.bfloat16
ALU = mybir.AluOpType
ACT = mybir.ActivationFunctionType
AX = mybir.AxisListType.X

P = 128
SEQ = 256
TILES = SEQ // P
D = 1024
KT = D // P
DFF = 2816
FB = 256
NF = DFF // FB
DEPTH = 2
H = 4
NEG = -1.0e30
EPS = 1e-6
LN_EPS = 1e-5
ALPHA = (2.0 * DEPTH) ** 0.25
SLOTS = 4
UNIT = 1024
UBUF = 3
CREDIT = 8
IN1 = 16
IN2 = 12
WO = 4
SMALL = 20
SMALL_AT = 8
NADA = 9
LEVELS = 6
PAD = 3
FU = 6 * NF
ENDS1 = [2 * n + 2 - (n >= SMALL_AT) for n in range(IN1 + WO)]
ENDS2 = [2 * n + 2 for n in range(IN2 + WO)]
LU1 = 2 * FU + ENDS1[-1]
LU2 = 2 * FU + ENDS2[-1]
LOADS1 = 2 * NF + (IN1 + WO) // SLOTS
LOADS2 = 2 * NF + (IN2 + WO) // SLOTS

C_IDENT, C_TRIU, C_ONES, C_SU, C_BLOCK = 0, 128, 256, 384, 512
C_MT = 640
C_NEGM = C_MT + 7 * 128
C_NEGD = C_NEGM + 128
C_SGN = C_NEGD + 384
C_ROPE = C_SGN + 12
N1 = C_ROPE + 64
C2_SL, C2_NEGC, C2_CNT, C2_RET, C2_ROT = 0, 128, 512, 896, 896 + 4 * 384
N2 = C2_ROT + 2 * 2 * 2 * 32
NBASE = C_BLOCK

R_SPB, R_ALOG, R_IB, R_DSK, R_LAM, R_LI, R_GAIN = 0, 12, 24, 28, 32, 160, 162
NR = R_GAIN + D
F_CONV, F_CB = 0, 48
NFP = 54
ARENA = 23700


class Steps:

    def __init__(self, sem, names):
        self.sem, self.names, self.turn = sem, names.split(), 0
        assert len(set(self.names)) == len(self.names)

    def at(self, name, use):
        return use * len(self.names) + (self.names.index(name) + 1)

    def done(self, name):
        assert self.names[self.turn] == name, (self.names[self.turn], name)
        self.turn = (self.turn + 1) % len(self.names)
        return self.sem


def over(ap, shape, *dims):
    for d in dims:
        ap = ap.unsqueeze(d)
    return ap.to_broadcast(shape)


def build(nc, t, out):
    ctx = ExitStack()

    def sb(name, shape, dt=F32):
        return ctx.enter_context(nc.sbuf_tensor(name, shape, dt))

    def sem(name):
        return ctx.enter_context(nc.semaphore(name))

    def steps(name, names):
        return Steps(sem(name), names)

    ps = ctx.enter_context(nc.psum_tensor("ps", [P, 8, 512], F32))
    x = sb("x", [P, TILES, D])
    tok = sb("tok", [P, TILES, D])
    hT_hi = sb("hT_hi", [P, KT, SEQ], F32R)
    hT_lo = sb("hT_lo", [P, KT, SEQ], F32R)
    raw = sb("raw", [P, SLOTS, KT * FB])
    w_hi = sb("w_hi", [P, UBUF, UNIT], F32R)
    w_lo = sb("w_lo", [P, UBUF, UNIT], F32R)
    silu_g = sb("silu_g", [P, 2 * SEQ])
    act = sb("act", [P, 2 * SEQ])
    act_hi = sb("act_hi", [P, FB // P, SEQ], F32R)
    act_lo = sb("act_lo", [P, FB // P, SEQ], F32R)
    rows = sb("rows", [P, 2, 2, D])
    arena = sb("arena", [P, ARENA])
    base = sb("base", [P, NBASE])
    zero = sb("zero", [P, 512], BF16)
    stat = sb("stat", [P, 8])
    bn = sb("bn", [P, TILES, 2, 6])
    mv = sb("mv", [P, TILES, 2])
    IDENT, TRIU = base[:, C_IDENT:C_IDENT + P], base[:, C_TRIU:C_TRIU + P]
    ONES, SU = base[:, C_ONES:C_ONES + P], base[:, C_SU:C_SU + P]
    TU = base[:, C_TRIU:C_TRIU + SEQ]

    x_ready = sem("x_ready")
    base_in = sem("base_in")
    settled = sem("settled")
    rows_in = [sem("rows_in0"), sem("rows_in1")]
    zero_set = sem("zero_set")
    raw_in = [sem(f"raw_in{i}") for i in range(SLOTS)]
    unit_hi, unit_lo = sem("unit_hi"), sem("unit_lo")
    unit_done = sem("unit_done")
    silu_done, act_ready = sem("silu_done"), sem("act_ready")
    act_split, act_rest = sem("act_split"), sem("act_rest")
    proj_evac = sem("proj_evac")
    pre_t = steps("pre_t", "trans0 trans1")
    pre_a = steps("pre_a", "ssq root hi0 hi1")
    pre_v = steps("pre_v", "mean rstd tok0 tok1 lo0 lo1")
    post_a = steps("post_a", "ssq root")
    post_v = steps("post_v", "mean stats rstd scaled")
    bn_done, ln_r = sem("bn_done"), sem("ln_r")
    mod_v = steps("mod_v", "shift scale rows")
    ln_v = steps("ln_v", "gated mixed stats var centred gained")
    ln_a = steps("ln_a", "root")

    def settle(eng):
        eng.sem_inc(settled, 1)

    def acc(tile):
        return ps[:, 2 * tile:2 * tile + 2, :]

    def hi_unit(a, B, j, buf, slot, loads, half, width=UNIT):
        if half == 0:
            a.wait_ge(raw_in[slot], loads * 16)
        a.wait_ge(unit_done, B + (j - UBUF + 1 + CREDIT if not isinstance(j, tuple) else j[0] + (j[1] - UBUF + 1 + CREDIT)))
        nc.scalar.activation(w_hi[:, buf, 0:width], raw[:, slot, half * UNIT:half * UNIT + width],
                             ACT.Copy).then_inc(unit_hi, 1)

    def lo_unit(v, B, j, buf, slot, half, width=UNIT):
        v.wait_ge(unit_hi, B + (j + 1 if not isinstance(j, tuple) else j[0] + (j[1] + 1)))
        nc.vector.tensor_tensor(w_lo[:, buf, 0:width], raw[:, slot, half * UNIT:half * UNIT + width],
                                w_hi[:, buf, 0:width].bitcast(F32), ALU.subtract).then_inc(unit_lo, 1)

    def unit_ready(pe, which, B, j):
        n = 1 + (CREDIT if which is unit_lo else 0)
        pe.wait_ge(which, B + (j + n if not isinstance(j, tuple) else j[0] + (j[1] + n)))

    def feature_unit(pe, B, j, buf, bank, half):
        h_, l_ = (w[:, buf, :].rearrange("p (k n) -> p k n", k=4) for w in (w_hi, w_lo))
        unit_ready(pe, unit_hi, B, j)
        for s in range(2):
            o, c = ps[:, bank, s * SEQ:(s + 1) * SEQ], slice(s * P, (s + 1) * P)
            for k in range(4):
                nc.tensor.matmul(o, h_[:, k, c], hT_hi[:, 4 * half + k, :], start=(half == s == k == 0), stop=False)
                nc.tensor.matmul(o, h_[:, k, c], hT_lo[:, 4 * half + k, :], start=False, stop=False)
        unit_ready(pe, unit_lo, B, j)
        for s in range(2):
            o, c = ps[:, bank, s * SEQ:(s + 1) * SEQ], slice(s * P, (s + 1) * P)
            for k in range(4):
                last = nc.tensor.matmul(o, l_[:, k, c], hT_hi[:, 4 * half + k, :], start=False,
                                        stop=(half == s == 1 and k == 3))
        last.then_inc(unit_done, 1)

    def token_unit(pe, B, j, buf, bank, half, width=FB, chunks=4):
        h_, l_ = (w[:, buf, 0:chunks * width].rearrange("p (k n) -> p k n", k=chunks) for w in (w_hi, w_lo))
        end = half == 1 or chunks == KT
        unit_ready(pe, unit_hi, B, j)
        for tile in range(TILES):
            o, c = ps[:, bank, tile * width:(tile + 1) * width], slice(tile * P, (tile + 1) * P)
            for k in range(chunks):
                nc.tensor.matmul(o, hT_hi[:, 4 * half + k, c], h_[:, k, :], start=(half == tile == k == 0), stop=False)
                nc.tensor.matmul(o, hT_lo[:, 4 * half + k, c], h_[:, k, :], start=False, stop=False)
        unit_ready(pe, unit_lo, B, j)
        for tile in range(TILES):
            o, c = ps[:, bank, tile * width:(tile + 1) * width], slice(tile * P, (tile + 1) * P)
            for k in range(chunks):
                last = nc.tensor.matmul(o, hT_hi[:, 4 * half + k, c], l_[:, k, :], start=False,
                                        stop=(end and tile == 1 and k == chunks - 1))
        last.then_inc(unit_done, 1)

    def row_unit(pe, B, j, buf, left, start, stop):
        unit_ready(pe, unit_hi, B, j)
        for tile in range(TILES):
            c = slice(tile * P, (tile + 1) * P)
            for i, part in enumerate(left):
                for half in range(2):
                    nc.tensor.matmul(ps[:, 2 * tile + half, :], part[:, c], w_hi[:, buf, half * 512:(half + 1) * 512],
                                     start=start and i == 0, stop=False)
        unit_ready(pe, unit_lo, B, j)
        for tile in range(TILES):
            c = slice(tile * P, (tile + 1) * P)
            for half in range(2):
                last = nc.tensor.matmul(ps[:, 2 * tile + half, :], left[0][:, c],
                                        w_lo[:, buf, half * 512:(half + 1) * 512], start=False, stop=stop)
        last.then_inc(unit_done, 1)

    def ffn_sp(sp, B, loads, l, wg, wu, wd, between=None):
        def load(slot, w, i):
            sp.dma_start(raw[:, slot, :], w[bass.ds(l, 1), i, :, :].rearrange("l i p n -> p (l i n)")).then_inc(
                raw_in[slot], 16)

        sp.wait_ge(unit_lo, B + (CREDIT - 6))
        load(0, wg, slice(0, 1))
        sp.wait_ge(unit_lo, B + (CREDIT - 4))
        load(1, wu, slice(0, 1))
        if between:
            between[0]()
        for first, end in ((1, 9), (9, NF)):
            with sp.Fori(first, end) as i:
                sp.wait_ge(unit_lo, B + i * 6 + (CREDIT - 4))
                load(0, wg, bass.ds(i, 1))
                sp.wait_ge(unit_lo, B + i * 6 + (CREDIT - 2))
                load(1, wu, bass.ds(i, 1))
                load(2, wd, bass.ds(i - 1, 1))
                if between and first == 1:
                    between[1](i - 1)
        sp.wait_ge(unit_lo, B + (6 * NF - 2 + CREDIT))
        load(2, wd, slice(NF - 1, NF))

    def ffn_pe(pe, B, f, g):
        pe.wait_ge(zero_set, 1)
        for b in range(4):
            nc.tensor.matmul(ps[:, b, :], zero[:, 0:P], zero[:], start=True, stop=False)
        pre_done(pe, g)
        left = lambda kk: (act_hi[:, kk, :], act_lo[:, kk, :])

        def gate_up(n, j):
            pe.wait_ge(silu_done, n + 1)
            feature_unit(pe, B, j(0), (j(0) if not isinstance(j(0), tuple) else j(0)[1]) % UBUF, 4, 0)
            feature_unit(pe, B, j(1), (j(1) if not isinstance(j(1), tuple) else j(1)[1]) % UBUF, 4, 1)
            pe.wait_ge(act_ready, n + 1)
            feature_unit(pe, B, j(2), (j(2) if not isinstance(j(2), tuple) else j(2)[1]) % UBUF, 5, 0)
            feature_unit(pe, B, j(3), (j(3) if not isinstance(j(3), tuple) else j(3)[1]) % UBUF, 5, 1)

        gate_up(f * NF, lambda r: r)
        with pe.Fori(1, NF) as i:
            gate_up(f * NF + i, lambda r: (i * 6, r - 2))
            pe.wait_ge(act_split, f * NF + i)
            pe.wait_ge(act_rest, f * NF + i)
            row_unit(pe, B, (i * 6, 2), 2, left(0), False, False)
            row_unit(pe, B, (i * 6, 3), 0, left(1), False, False)
        pe.wait_ge(act_split, f * NF + NF)
        pe.wait_ge(act_rest, f * NF + NF)
        row_unit(pe, B, 6 * NF - 2, (6 * NF - 2) % UBUF, left(0), False, False)
        row_unit(pe, B, 6 * NF - 1, (6 * NF - 1) % UBUF, left(1), False, True)

    def ffn_act(a, B, loads, f):
        def split_act(n, done):
            a.wait_ge(act_ready, n + 2)
            a.wait_ge(unit_done, done)
            nc.scalar.activation(act_hi[:].rearrange("p s t -> p (s t)"), act[:], ACT.Copy).then_inc(act_split, 1)

        def silu(n, done):
            a.wait_ge(unit_done, done)
            a.wait_ge(act_ready, n + 1)
            nc.scalar.activation(silu_g[:], ps[:, 4, :], ACT.Silu).then_inc(silu_done, 1)

        for r in range(4):
            hi_unit(a, B, r if r >= UBUF - 1 else UBUF - 1, r % UBUF, r // 2, loads + 1, r % 2)
        silu(f * NF, B + (2 + CREDIT))
        with a.Fori(1, NF) as i:
            for r in range(2):
                hi_unit(a, B, (i * 6, r - 2), (r - 2) % UBUF, 0, loads + i + 1, r)
            split_act(f * NF + i - 1, B + i * 6 + (CREDIT - 2))
            for r in range(2, 4):
                hi_unit(a, B, (i * 6, r - 2), (r - 2) % UBUF, 1, loads + i + 1, r - 2)
            silu(f * NF + i, B + i * 6 + CREDIT)
            for r in range(4, 6):
                hi_unit(a, B, (i * 6, r - 2), (r - 2) % UBUF, 2, loads + i, r - 4)
        split_act(f * NF + (NF - 1), B + (NF * 6 - 2 + CREDIT))
        for r in range(2):
            hi_unit(a, B, 6 * NF - 2 + r, (6 * NF - 2 + r) % UBUF, 2, loads + NF, r)

    def ffn_dve(v, B, f, between=None):
        def rest_act(n):
            v.wait_ge(act_split, n + 1)
            nc.vector.tensor_tensor(act_lo[:].rearrange("p s t -> p (s t)"), act[:],
                                    act_hi[:].rearrange("p s t -> p (s t)").bitcast(F32), ALU.subtract).then_inc(act_rest, 1)

        def product(n, done):
            v.wait_ge(silu_done, n + 2)
            v.wait_ge(unit_done, done)
            nc.vector.tensor_tensor(act[:], silu_g[:], ps[:, 5, :], ALU.mult).then_inc(act_ready, 1)

        if between:
            between[0]()
        for r in range(4):
            lo_unit(v, B, r, r % UBUF, r // 2, r % 2)
        product(f * NF, B + (4 + CREDIT))
        for first, end in ((1, 9), (9, NF)):
            with v.Fori(first, end) as i:
                for r in range(2):
                    lo_unit(v, B, (i * 6, r - 2), (r - 2) % UBUF, 0, r)
                rest_act(f * NF + i - 1)
                for r in range(2, 6):
                    lo_unit(v, B, (i * 6, r - 2), (r - 2) % UBUF, r // 2, r % 2)
                if between and first == 1:
                    between[1](i - 1)
                v.wait_ge(act_rest, f * NF + i)
                product(f * NF + i, B + i * 6 + (2 + CREDIT))
        rest_act(f * NF + (NF - 1))
        for r in range(2):
            lo_unit(v, B, 6 * NF - 2 + r, (6 * NF - 2 + r) % UBUF, 2, r)

    def ffn_end(B):
        return unit_done, B + (6 * NF + CREDIT)

    def transposes_pe(tile):
        for k in range(KT):
            c = (k % 2) * SEQ + tile * P
            last = nc.tensor.transpose(ps[:, 4 + k // 2, c:c + P], tok[:, tile, k * P:(k + 1) * P], IDENT)
        return last

    def hT_half(w, i):
        return w[:, 4 * i:4 * i + 4, :].rearrange("p (b k) t -> p b (k t)", b=2)

    def split_hi(a, i, A):
        nc.scalar.activation(hT_half(hT_hi, i), ps[:, 4 + 2 * i:6 + 2 * i, :], ACT.Copy).then_inc(A.done(f"hi{i}"), 1)

    def split_lo(v, i, A, use, V):
        v.wait_ge(A.sem, A.at(f"hi{i}", use))
        nc.vector.tensor_tensor(hT_half(hT_lo, i), ps[:, 4 + 2 * i:6 + 2 * i, :], hT_half(hT_hi, i).bitcast(F32),
                                ALU.subtract).then_inc(V.done(f"lo{i}"), 1)

    def pre_done(pe, g):
        pe.wait_ge(pre_v.sem, pre_v.at("lo1", g))

    def pre_pe(pe, g):
        for tile in range(TILES):
            pe.wait_ge(pre_v.sem, pre_v.at(f"tok{tile}", g))
            transposes_pe(tile).then_inc(pre_t.done(f"trans{tile}"), 1)

    def pre_act(a, g, normed):
        a.wait_ge(x_ready, g * 16 + 16)
        if normed:
            for tile in range(TILES):
                last = nc.scalar.activation(tok[:, tile, :], x[:, tile, :], ACT.Square,
                                            accum_out=stat[:, tile:tile + 1])
            last.then_inc(pre_a.done("ssq"), 1)
            a.wait_ge(pre_v.sem, pre_v.at("mean", g))
            nc.scalar.activation(stat[:, 2:4], stat[:, 2:4], ACT.Sqrt).then_inc(pre_a.done("root"), 1)
        else:
            nc.scalar.activation(stat[:, 6:7], x[:, 0, 0:1], ACT.Copy).then_inc(pre_a.done("ssq"), 1)
            nc.scalar.activation(stat[:, 7:8], x[:, 0, 0:1], ACT.Copy).then_inc(pre_a.done("root"), 1)
        a.wait_ge(pre_t.sem, pre_t.at("trans1", g))
        for i in range(2):
            split_hi(a, i, pre_a)

    def rows_wait(v, L, pos):
        if pos == 1:
            v.wait_ge(rows_in[1], L * 16 + 16)
        else:
            v.wait_ge(rows_in[0], L * 32 + (16 if pos == 0 else 32))

    def pre_dve(v, L, pos, normed):
        g = L * 3 + pos
        rows_wait(v, L, pos)
        v.wait_ge(x_ready, g * 16 + 16)
        if normed:
            v.wait_ge(pre_a.sem, pre_a.at("ssq", g))
            nc.vector.tensor_scalar(stat[:, 2:4], stat[:, 0:2], 1.0 / D, EPS, ALU.mult,
                                    ALU.add).then_inc(pre_v.done("mean"), 1)
            v.wait_ge(pre_a.sem, pre_a.at("root", g))
            nc.vector.reciprocal(stat[:, 4:6], stat[:, 2:4]).then_inc(pre_v.done("rstd"), 1)
            v.wait_ge(pre_v.sem, pre_v.at("rstd", g))
            for tile in range(TILES):
                nc.vector.scalar_tensor_tensor(tok[:, tile, :], x[:, tile, :], stat[:, 4 + tile:5 + tile],
                                               rows[:, pos % 2, 0, :], ALU.mult, ALU.mult).then_inc(
                                                   pre_v.done(f"tok{tile}"), 1)
        else:
            shift, scale1 = mrow[:, 0, :], mrow[:, 1, :]
            v.wait_ge(mod_v.sem, mod_v.at("rows", g - 6))
            nc.vector.tensor_tensor(tok[:], x[:], over(scale1, [P, TILES, D], 1),
                                    ALU.mult).then_inc(pre_v.done("mean"), 1)
            nc.vector.memset(stat[:, 5:6], 0.0).then_inc(pre_v.done("rstd"), 1)
            v.wait_ge(pre_v.sem, pre_v.at("mean", g))
            for tile in range(TILES):
                nc.vector.tensor_tensor(tok[:, tile, :], tok[:, tile, :], shift, ALU.add).then_inc(
                    pre_v.done(f"tok{tile}"), 1)
        for i in range(2):
            split_lo(v, i, pre_a, g, pre_v)

    def post_act(a, g, ready):
        a.wait_ge(*ready)
        for tile in range(TILES):
            last = nc.scalar.activation(tok[:, tile, :].rearrange("p (b n) -> p b n", b=2), acc(tile), ACT.Square,
                                        accum_out=stat[:, tile:tile + 1])
        last.then_inc(post_a.done("ssq"), 1)
        a.wait_ge(post_v.sem, post_v.at("mean", g))
        nc.scalar.activation(stat[:, 2:4], stat[:, 2:4], ACT.Sqrt).then_inc(post_a.done("root"), 1)

    def post_dve(v, g, pos, weight):
        v.wait_ge(post_a.sem, post_a.at("ssq", g))
        nc.vector.tensor_scalar(stat[:, 2:4], stat[:, 0:2], 1.0 / D, EPS, ALU.mult,
                                ALU.add).then_inc(post_v.done("mean"), 1)
        v.wait_ge(post_a.sem, post_a.at("root", g))
        nc.vector.reciprocal(stat[:, 4:6], stat[:, 2:4]).then_inc(post_v.done("stats"), 1)
        v.wait_ge(post_v.sem, post_v.at("stats", g))
        nc.vector.tensor_scalar(stat[:, 6:8], stat[:, 4:6], weight, None, ALU.mult).then_inc(post_v.done("rstd"), 1)
        v.wait_ge(post_v.sem, post_v.at("rstd", g))
        for tile in range(TILES):
            last = nc.vector.scalar_tensor_tensor(
                tok[:, tile, :].rearrange("p (b n) -> p b n", b=2), acc(tile), stat[:, 6 + tile:7 + tile],
                rows[:, pos % 2, 1, :].rearrange("p (b n) -> p b n", b=2), ALU.mult, ALU.mult)
        last.then_inc(post_v.done("scaled"), 1)
        v.wait_ge(post_v.sem, post_v.at("scaled", g))
        nc.vector.tensor_tensor(x[:], x[:], tok[:], ALU.add).then_inc(x_ready, 16)

    def ln_act(a, h):
        a.wait_ge(ln_v.sem, ln_v.at("var", h))
        nc.scalar.activation(stat[:, 2:4], stat[:, 0:2], ACT.Sqrt).then_inc(ln_a.done("root"), 1)

    def ln_dve(v, h, pos, ready, gate):
        v.wait_ge(*ready)
        for tile in range(TILES):
            last = nc.vector.tensor_tensor(tok[:, tile, :].rearrange("p (b n) -> p b n", b=2), acc(tile),
                                           gate.rearrange("p (b n) -> p b n", b=2), ALU.mult)
        last.then_inc(ln_v.done("gated"), 1)
        v.wait_ge(ln_v.sem, ln_v.at("gated", h))
        nc.vector.scalar_tensor_tensor(tok[:], x[:], ALPHA, tok[:], ALU.mult, ALU.add).then_inc(ln_v.done("mixed"), 1)
        v.wait_ge(ln_v.sem, ln_v.at("mixed", h))
        for tile in range(TILES):
            for half in range(2):
                last = nc.vector.bn_stats(bn[:, tile, half, :], tok[:, tile, half * 512:(half + 1) * 512])
        last.then_inc(ln_v.done("stats"), 1)
        v.wait_ge(ln_v.sem, ln_v.at("stats", h))
        settle(v)
        for tile in range(TILES):
            last = nc.vector.bn_aggr(mv[:, tile, :], bn[:, tile, :, :].rearrange("p a b -> p (a b)"))
        last.then_inc(bn_done, 1)
        v.wait_ge(bn_done, h + 1)
        nc.vector.tensor_scalar(stat[:, 0:2], mv[:, :, 1], LN_EPS, None, ALU.add).then_inc(ln_v.done("var"), 1)
        v.wait_ge(ln_a.sem, ln_a.at("root", h))
        nc.vector.reciprocal(stat[:, 4:6], stat[:, 2:4]).then_inc(ln_r, 1)
        v.wait_ge(ln_r, h + 1)
        for tile in range(TILES):
            last = nc.vector.tensor_scalar(tok[:, tile, :], tok[:, tile, :], mv[:, tile, 0:1],
                                           stat[:, 4 + tile:5 + tile], ALU.subtract, ALU.mult)
        last.then_inc(ln_v.done("centred"), 1)
        v.wait_ge(ln_v.sem, ln_v.at("centred", h))
        nc.vector.tensor_tensor(tok[:], tok[:], over(rows[:, pos % 2, 0, :], [P, TILES, D], 1),
                                ALU.mult).then_inc(ln_v.done("gained"), 1)
        v.wait_ge(ln_v.sem, ln_v.at("gained", h))
        nc.vector.tensor_tensor(x[:], tok[:], over(rows[:, pos % 2, 1, :], [P, TILES, D], 1),
                                ALU.add).then_inc(x_ready, 16)


    def mixer_load(sp, B, ends, n, src, width=KT * FB):
        sp.wait_ge(unit_lo, B + (CREDIT + (ends[n - SLOTS] if n >= SLOTS else (-4, -2, 0, 0)[n])))
        sp.dma_start(raw[:, n % SLOTS, 0:width], src).then_inc(raw_in[n % SLOTS], 16)

    def mixer_units(ends, n):
        first = ends[n - 1] if n else 0
        return [(j, j - first) for j in range(first, ends[n])]

    def mixer_hi(a, B, ends, n, loads):
        for j, half in mixer_units(ends, n):
            width = UNIT if ends[n] - (ends[n - 1] if n else 0) == 2 else KT * SMALL
            hi_unit(a, B, max(j, UBUF - 1), j % UBUF, n % SLOTS, loads[n % SLOTS] + (n // SLOTS + 1), half, width)

    def mixer_lo(v, B, ends, n):
        for j, half in mixer_units(ends, n):
            width = UNIT if ends[n] - (ends[n - 1] if n else 0) == 2 else KT * SMALL
            lo_unit(v, B, j, j % UBUF, n % SLOTS, half, width)

    def out_product(pe, B, ends, first):
        for n in range(first, first + WO):
            for j, half in mixer_units(ends, n):
                k = 2 * (n - first) + half
                row_unit(pe, B, j, j % UBUF, (hT_hi[:, k, :], hT_lo[:, k, :]), k == 0, k == KT - 1)

    def scores_T(bank, kT_s, qT_t, h):
        nc.tensor.matmul(ps[:, bank, 0:SEQ], kT_s[:, 0:P], qT_t[:, 0:SEQ], start=True, stop=True)
        return nc.tensor.matmul(ps[:, bank, SEQ:SEQ + P], kT_s[:, P:SEQ], qT_t[:, P:SEQ], start=True, stop=True)

    def weighted_values(out0, out1, pT, v0, v1):
        nc.tensor.matmul(out0, pT[:, 0:P], v0, start=True, stop=True)
        nc.tensor.matmul(out1, pT[:, P:SEQ], v0, start=True, stop=False)
        return nc.tensor.matmul(out1, pT[:, SEQ:SEQ + P], v1, start=False, stop=True)

    def row_of(out, col):
        return nc.tensor.matmul(out, col.to_broadcast([P, P]), IDENT, start=True, stop=True)

    def prefix_row(bank, off, col0, col1):
        nc.tensor.matmul(ps[:, bank, off:off + SEQ], col0.to_broadcast([P, P]), TU, start=True, stop=False)
        return nc.tensor.matmul(ps[:, bank, off + P:off + SEQ], col1.to_broadcast([P, P]), TRIU, start=False, stop=True)

    def diag(buf):
        return buf[:].rearrange("p h (b n) -> p h b n", b=3)[:, :, 0:3:2, :]


    class Arena:

        def __init__(self):
            self.at = 0

        def take(self, *shape):
            n = int(np.prod(shape))
            piece = arena[:, self.at:self.at + n]
            self.at += n
            assert self.at <= ARENA, (self.at, ARENA)
            if len(shape) == 2:
                piece = piece.rearrange("p (a b) -> p a b", a=shape[0])
            if len(shape) == 3:
                piece = piece.rearrange("p (a b c) -> p a b c", a=shape[0], b=shape[1])
            if len(shape) == 4:
                piece = piece.rearrange("p (a b c d) -> p a b c d", a=shape[0], b=shape[1], c=shape[2])
            return piece

    m = Arena()
    con = m.take(N1 - NBASE)
    par = m.take(NR)
    fp = m.take(NFP)
    u = m.take(12, PAD + SEQ)
    cv = m.take(12, SEQ)
    qk_m = m.take(4, SEQ)
    small = m.take(TILES, SMALL)
    gate_g = m.take(TILES, SEQ)
    rope_in = m.take(TILES, 512)
    v_d = m.take(TILES, SEQ)
    z_s = m.take(TILES, SEQ)
    v_m = m.take(TILES, H, 65)
    o_m = m.take(TILES, SEQ)
    sp_x, sp_e, sp_u, sp_l, sp_c = (m.take(TILES, 12) for _ in range(5))
    ld = m.take(TILES, 12)
    ea = m.take(12)
    gc = m.take(TILES, 12)
    beta = m.take(TILES, H)
    dt = m.take(TILES, H)
    acol, mcol, negm, em, den = (m.take(TILES, H) for _ in range(5))
    md = m.take(H, TILES)
    mfull = m.take(H)
    coef = m.take(TILES, 8)
    rmax = m.take(TILES, 8)
    lamb = m.take(8)
    lamp = m.take(2, 32)
    ms = m.take(TILES, 16)
    gsum = m.take(TILES, 2)
    uflat = u.rearrange("p a b -> p (a b)")
    dT2 = uflat[:, 0:1536].rearrange("p (a b) -> p a b", a=H)
    xs = uflat[:, 1536:2048].rearrange("p (a b) -> p a b", a=TILES)
    xdt = uflat[:, 2048:2560].rearrange("p (a b) -> p a b", a=TILES)
    mark = m.at
    dT = m.take(H, 384)
    lT = m.take(H, 384)
    xT, xi, bT, pm = (m.take(8, P) for _ in range(4))
    kb = m.take(2, SEQ)
    vb, uu = m.take(TILES, SEQ), m.take(TILES, SEQ)
    r2 = m.take(SEQ)
    m.at = mark
    dS = m.take(8, 384)
    pD = m.take(H, 384)
    pT = m.take(H, 384)
    qkr = m.take(TILES, 512)
    dqk = m.take(4, SEQ)
    rt = m.take(2, 16 * 16)
    sq = dS.rearrange("p a b -> p (a b)")[:, 0:TILES * D].rearrange("p (a b) -> p a b", a=TILES)
    mix = tok

    def K(c, n=P):
        return con[:, c - NBASE:c - NBASE + n]

    BLOCKS, NEGM, NEGD = K(C_BLOCK), K(C_NEGM), K(C_NEGD, 384)
    COS = K(C_ROPE, 32).rearrange("p (t n) -> p t n", t=2)
    SIN = K(C_ROPE + 32, 32).rearrange("p (t n) -> p t n", t=2)
    con_in, par_in = sem("con_in"), sem("par_in")
    pads = sem("pads")
    ones_set = sem("ones_set")
    inv_b, inv_p, inv_c, inv_r, inv_x = (sem(f"inv_{c}") for c in "bpcrx")

    T1 = steps("mix1_t", "small_sums rows_g sumsq beta_rows kk qk x0 vt u1 l21 u2 o_g rows_s xt_s cb o_s "
                         "rows_a rows_m qk_m o_m rope_t sc_d trans_d o_d trans")
    A1 = steps("mix1_a", "silu_g sq silu_s sp_e sp_l ea eb gc dec_g root xi u1 u2 o_g xs dec_s dec_m em den "
                         "dqk exp_d lam pT o_d gates sq_o root_o hi0 hi1")
    V1 = steps("mix1_v", "cg0 cg1 cg2 conv_g cs0 cs1 cs2 conv_s sp_in sp_sgn sp_abs sp_u sp_um sp_em sp_ru sp_corr sp_max sp_l sp dt ld eb1 beta dec_g rs "
                         "rrs qkn kb lT aT mt1 xT vb r2 "
                         "xdt dec_s w_s skip o_s "
                         "ai acol tmp_m md mf m0 m1 dec_m w_m mt negm denm rden o_m "
                         "ra1 rb1 rc1 rd1 re1 rf1 ra2 rb2 rc2 rd2 re2 rf2 mask_d max_d sub_d sum_d rec_d lam0 lam1 lam2 coef "
                         "scale_d add_d "
                         "pre_gate sums_o pair0 pair1 mean_o rstd_o gl norm_o gain_o gate_o lo0 lo1")
    G1 = steps("mix1_g", "dec_g dec_s dec_m")

    def mixer1_sp(sp, B, l):
        at = 0
        for n in range(IN1 + WO):
            if n == SMALL_AT:
                mixer_load(sp, B, ENDS1, n, t["w_small"][bass.ds(l, 1), :, :].rearrange("l p n -> p (l n)"), KT * SMALL)
            elif n < IN1:
                mixer_load(sp, B, ENDS1, n, t["w_in"][bass.ds(l, 1), at:at + 1, :, :].rearrange("l i p n -> p (l i n)"))
                at += 1
            else:
                mixer_load(sp, B, ENDS1, n,
                           t["w_out"][bass.ds(l, 1), n - IN1:n - IN1 + 1, :, :].rearrange("l i p n -> p (l i n)"))

    def mixer1_pe(pe, B, l, g):
        def after(S, name):
            pe.wait_ge(S.sem, S.at(name, l))

        pe.wait_ge(ones_set, 1)
        pre_done(pe, g)
        for n in range(IN1):
            pe.wait_ge(proj_evac, l * IN1 + n + 1)
            for j, half in mixer_units(ENDS1, n):
                if n < SMALL_AT:
                    feature_unit(pe, B, j, j % UBUF, 4 + n % 4, half)
                elif n == SMALL_AT:
                    token_unit(pe, B, j, j % UBUF, 4 + n % 4, 0, SMALL, KT)
                else:
                    token_unit(pe, B, j, j % UBUF, 4 + n % 4, half)
        pe.wait_ge(proj_evac, l * IN1 + IN1 + 4)

        after(V1, "ld")
        nc.tensor.matmul(ps[:, 7, 0:12], TRIU, ld[:, 0, :], start=True, stop=True)
        nc.tensor.matmul(ps[:, 7, 12:24], ONES, ld[:, 0, :], start=True, stop=False)
        nc.tensor.matmul(ps[:, 7, 12:24], TRIU, ld[:, 1, :], start=False,
                         stop=True).then_inc(T1.done("small_sums"), 1)
        for h in range(H):
            last = prefix_row(4 + h // 2, (h % 2) * SEQ, ld[:, 0, h:h + 1], ld[:, 1, h:h + 1])
        last.then_inc(T1.done("rows_g"), 1)
        after(A1, "sq")
        for c in range(4):
            last = nc.tensor.matmul(ps[:, c // 2, (c % 2) * SEQ:(c % 2 + 1) * SEQ], BLOCKS,
                                    pm_sq[:, c, :], start=True, stop=True)
        last.then_inc(T1.done("sumsq"), 1)
        after(V1, "beta")
        for h in range(H):
            for tile in range(TILES):
                c = (h % 2) * SEQ + tile * P
                last = row_of(ps[:, 2 + h // 2, c:c + P], beta[:, tile, h:h + 1])
        last.then_inc(T1.done("beta_rows"), 1)
        after(V1, "kb")
        for h in range(H):
            half = slice(64 * (h % 2), 64 * (h % 2) + 64)
            last = scores_T(h, cv[half, 2 + h // 2, :], kb[half, h // 2, :], h)
        last.then_inc(T1.done("kk"), 1)
        after(V1, "dec_g")
        for h in range(H):
            half = slice(64 * (h % 2), 64 * (h % 2) + 64)
            last = scores_T(4 + h, cv[half, 2 + h // 2, :], cv[half, h // 2, :], h)
        last.then_inc(T1.done("qk"), 1)
        after(V1, "xT")
        for i in range(8):
            last = nc.tensor.transpose(ps[:, i // 4, (i % 4) * P:(i % 4 + 1) * P], xT[:, i, :], IDENT)
        last.then_inc(T1.done("x0"), 1)
        after(A1, "xi")
        after(V1, "aT")
        settle(pe)
        with pe.Fori(0, LEVELS) as j:
            n = l * LEVELS + j
            pe.wait_ge(inv_x, n + 1)
            pe.wait_ge(inv_b, n + 1)
            for i in range(8):
                last = nc.tensor.matmul(ps[:, 2 + i // 4, (i % 4) * P:(i % 4 + 1) * P], bT[:, i, :], xi[:, i, :],
                                        start=True, stop=True)
            last.then_inc(inv_p, 1)
            pe.wait_ge(inv_c, n + 1)
            for i in range(8):
                nc.tensor.matmul(ps[:, 4 + i // 4, (i % 4) * P:(i % 4 + 1) * P], xT[:, i, :], pm[:, i, :],
                                 start=True, stop=True)
            for i in range(8):
                last = nc.tensor.matmul(ps[:, 6 + i // 4, (i % 4) * P:(i % 4 + 1) * P], pm[:, i, :], xT[:, i, :],
                                        start=True, stop=True)
            last.then_inc(inv_r, 1)
        for c in range(2):
            for tile in range(TILES):
                o = tile * SEQ + c * P
                last = nc.tensor.transpose(ps[:, 0, o:o + P], cv[:, 4 + c, tile * P:(tile + 1) * P], IDENT)
        last.then_inc(T1.done("vt"), 1)
        pe.wait_ge(inv_x, l * LEVELS + LEVELS + 1)
        after(V1, "vb")
        for h in range(H):
            last = nc.tensor.matmul(ps[:, 1, h * 64:(h + 1) * 64], xT[:, 2 * h, :], vb[:, 0, h * 64:(h + 1) * 64],
                                    start=True, stop=True)
        last.then_inc(T1.done("u1"), 1)
        after(A1, "u1")
        for h in range(H):
            last = nc.tensor.matmul(ps[:, 2, h * 64:(h + 1) * 64], lT[:, h, P:SEQ], uu[:, 0, h * 64:(h + 1) * 64],
                                    start=True, stop=True)
        last.then_inc(T1.done("l21"), 1)
        after(V1, "r2")
        for h in range(H):
            last = nc.tensor.matmul(ps[:, 3, h * 64:(h + 1) * 64], xT[:, 2 * h + 1, :], r2[:, h * 64:(h + 1) * 64],
                                    start=True, stop=True)
        last.then_inc(T1.done("u2"), 1)
        after(A1, "u2")
        for h in range(H):
            c = slice(h * 64, (h + 1) * 64)
            last = weighted_values(ps[:, 4, h * 64:(h + 1) * 64], ps[:, 4, SEQ + h * 64:SEQ + (h + 1) * 64],
                                   dT[:, h, :], uu[:, 0, c], uu[:, 1, c])
        last.then_inc(T1.done("o_g"), 1)

        for h in range(H):
            last = prefix_row(6 + h // 2, (h % 2) * SEQ, ld[:, 0, 4 + h:5 + h], ld[:, 1, 4 + h:5 + h])
        last.then_inc(T1.done("rows_s"), 1)
        after(A1, "silu_s")
        for c in range(2):
            for tile in range(TILES):
                o = tile * SEQ + c * P
                last = nc.tensor.transpose(ps[:, 0, o:o + P], cv[:, 6 + c, tile * P:(tile + 1) * P], IDENT)
        last.then_inc(T1.done("xt_s"), 1)
        for grp in range(2):
            last = scores_T(1 + grp, cv[:, 8 + grp, :], cv[:, 10 + grp, :], grp)
        last.then_inc(T1.done("cb"), 1)
        after(V1, "w_s")
        after(V1, "xdt")
        for h in range(H):
            c = slice(h * 64, (h + 1) * 64)
            last = weighted_values(ps[:, 3, h * 64:(h + 1) * 64], ps[:, 3, SEQ + h * 64:SEQ + (h + 1) * 64],
                                   dT2[:, h, :], xdt[:, 0, c], xdt[:, 1, c])
        last.then_inc(T1.done("o_s"), 1)

        after(A1, "o_g")
        after(V1, "acol")
        for h in range(H):
            for tile in range(TILES):
                c = (h % 2) * SEQ + tile * P
                last = row_of(ps[:, 4 + h // 2, c:c + P], acol[:, tile, h:h + 1])
        last.then_inc(T1.done("rows_a"), 1)
        after(V1, "m1")
        for h in range(H):
            for tile in range(TILES):
                c = (h % 2) * SEQ + tile * P
                last = row_of(ps[:, 6 + h // 2, c:c + P], mcol[:, tile, h:h + 1])
        last.then_inc(T1.done("rows_m"), 1)
        after(V1, "o_s")
        for h in range(H):
            half = slice(64 * (h % 2), 64 * (h % 2) + 64)
            last = scores_T(h, qk_m[half, 2 + h // 2, :], qk_m[half, h // 2, :], h)
        last.then_inc(T1.done("qk_m"), 1)
        after(V1, "w_m")
        for h in range(H):
            last = weighted_values(ps[:, 4, h * 65:(h + 1) * 65], ps[:, 5, h * 65:(h + 1) * 65], dT2[:, h, :],
                                   v_m[:, 0, h, :], v_m[:, 1, h, :])
        last.then_inc(T1.done("o_m"), 1)

        after(V1, "rf2")
        for c in range(4):
            for tile in range(TILES):
                o = (c % 2) * SEQ + tile * P
                last = nc.tensor.transpose(ps[:, c // 2, o:o + P], qkr[:, tile, c * P:(c + 1) * P], IDENT)
        last.then_inc(T1.done("rope_t"), 1)
        after(A1, "dqk")
        after(V1, "o_m")
        for j in range(8):
            part, c = slice(32 * (j % 4), 32 * (j % 4) + 32), j // 4
            nc.tensor.matmul(ps[:, j % 4, c * P:(c + 1) * P], dqk[part, c, 0:P], dqk[part, 2 + c, 0:P],
                             start=True, stop=True, tile_position=(32 * (j % 4), 0))
            last = nc.tensor.matmul(ps[:, 4 + j % 4, c * SEQ:(c + 1) * SEQ], dqk[part, c, P:SEQ], dqk[part, 2 + c, :],
                                    start=True, stop=True, tile_position=(32 * (j % 4), 0))
        last.then_inc(T1.done("sc_d"), 1)
        after(V1, "add_d")
        for h in range(H):
            for b in range(3):
                last = nc.tensor.transpose(ps[:, h, b * P:(b + 1) * P], pD[:, h, b * P:(b + 1) * P], IDENT)
        last.then_inc(T1.done("trans_d"), 1)
        after(A1, "pT")
        for h in range(H):
            c = slice(h * 64, (h + 1) * 64)
            last = weighted_values(ps[:, 4, h * 64:(h + 1) * 64], ps[:, 4, SEQ + h * 64:SEQ + (h + 1) * 64],
                                   pT[:, h, :], v_d[:, 0, c], v_d[:, 1, c])
        last.then_inc(T1.done("o_d"), 1)

        after(V1, "gate_o")
        transposes_pe(0)
        transposes_pe(1).then_inc(T1.done("trans"), 1)
        after(V1, "lo1")
        out_product(pe, B, ENDS1, IN1)

    def mixer1_act(a, B, loads, l):
        def after(S, name):
            a.wait_ge(S.sem, S.at(name, l))

        token_homes = {9: gate_g, 10: rope_in[:, :, 0:SEQ], 11: rope_in[:, :, SEQ:512], 12: v_d, 13: z_s, 15: o_m}
        for n in range(IN1):
            if n == 0:
                mixer_hi(a, B, ENDS1, 0, loads)
            mixer_hi(a, B, ENDS1, n + 1, loads)
            a.wait_ge(unit_done, B + (ENDS1[n] + CREDIT))
            bank = ps[:, 4 + n % 4, :]
            two = bank.rearrange("p (a b) -> p a b", a=2)
            if n < 6:
                last = nc.scalar.activation(u[:, 2 * n:2 * n + 2, PAD:], two, ACT.Copy)
            elif n < 8:
                last = nc.scalar.activation(qk_m[:, 2 * (n - 6):2 * (n - 6) + 2, :], two, ACT.Copy,
                                            scale=1.0 if n == 6 else 64.0 ** -0.5)
            elif n == SMALL_AT:
                last = nc.scalar.activation(small, bank[:, 0:2 * SMALL].rearrange("p (a b) -> p a b", a=2), ACT.Copy)
            elif n == 14:
                for tile in range(TILES):
                    last = nc.scalar.activation(v_m[:, tile, :, 0:64],
                                                two[:, tile, :].rearrange("p (h d) -> p h d", h=H), ACT.Copy)
            else:
                last = nc.scalar.activation(token_homes[n], two, ACT.Copy)
            last.then_inc(proj_evac, 1)
            if n == 11:
                after(V1, "conv_g")
                nc.scalar.activation(cv[:, 0:6, :], cv[:, 0:6, :], ACT.Silu).then_inc(A1.done("silu_g"), 1)
                after(A1, "silu_g")
                nc.scalar.activation(pm_sq, cv[:, 0:4, :], ACT.Square).then_inc(A1.done("sq"), 1)
            if n == 13:
                after(V1, "conv_s")
                for c in range(6):
                    last = nc.scalar.activation(cv[:, 6 + c, :], cv[:, 6 + c, :], ACT.Silu, bias=fp[:, F_CB + c:F_CB + c + 1])
                last.then_inc(A1.done("silu_s"), 1)

        after(V1, "sp_abs")
        nc.scalar.activation(sp_e, sp_c, ACT.Exp, scale=-1.0).then_inc(A1.done("sp_e"), 1)
        after(V1, "sp_u")
        nc.scalar.activation(sp_l, sp_u, ACT.Ln).then_inc(A1.done("sp_l"), 1)
        a.wait_ge(par_in, l * 32 + 32)
        nc.scalar.activation(ea, par[:, R_ALOG:R_ALOG + 12], ACT.Exp).then_inc(A1.done("ea"), 1)
        nc.scalar.activation(beta, small[:, :, 0:H], ACT.Exp, scale=-1.0).then_inc(A1.done("eb"), 1)
        a.wait_ge(T1.sem, T1.at("small_sums", l))
        nc.scalar.activation(gc, ps[:, 7, 0:24].rearrange("p (a b) -> p a b", a=2), ACT.Copy).then_inc(A1.done("gc"), 1)
        after(V1, "dec_g")
        nc.scalar.activation(dT, dT, ACT.Exp).then_inc(A1.done("dec_g"), 1)
        after(V1, "rs")
        nc.scalar.activation(pm_sq, pm_sq, ACT.Sqrt).then_inc(A1.done("root"), 1)
        after(T1, "x0")
        nc.scalar.activation(xi.rearrange("p (a i) n -> p a (i n)", a=2), ps[:, 0:2, :], ACT.Copy).then_inc(A1.done("xi"), 1)
        with a.Fori(0, LEVELS) as j:
            a.wait_ge(inv_p, l * LEVELS + j + 2)
            nc.scalar.activation(pm.rearrange("p (a i) n -> p a (i n)", a=2), ps[:, 2:4, :], ACT.Copy).then_inc(inv_c, 1)
        after(T1, "u1")
        nc.scalar.activation(uu[:, 0, :], ps[:, 1, 0:SEQ], ACT.Copy).then_inc(A1.done("u1"), 1)
        after(T1, "u2")
        nc.scalar.activation(uu[:, 1, :], ps[:, 3, 0:SEQ], ACT.Copy).then_inc(A1.done("u2"), 1)
        after(T1, "o_g")
        nc.scalar.activation(mix[:, :, 0:SEQ], ps[:, 4, :].rearrange("p (a b) -> p a b", a=2),
                             ACT.Copy).then_inc(A1.done("o_g"), 1)
        after(T1, "xt_s")
        nc.scalar.activation(xs, ps[:, 0, :].rearrange("p (a b) -> p a b", a=2), ACT.Copy).then_inc(A1.done("xs"), 1)
        after(V1, "dec_s")
        nc.scalar.activation(dT2, dT2, ACT.Exp).then_inc(A1.done("dec_s"), 1)
        after(V1, "dec_m")
        nc.scalar.activation(dT2, dT2, ACT.Exp, scale=-1.0).then_inc(A1.done("dec_m"), 1)
        after(V1, "negm")
        nc.scalar.activation(em, negm, ACT.Exp).then_inc(A1.done("em"), 1)
        after(T1, "o_m")
        o65 = ps[:, 4:6, 0:H * 65].rearrange("p a (h d) -> p a h d", h=H)
        nc.scalar.activation(den, o65[:, :, :, 64], ACT.Abs).then_inc(A1.done("den"), 1)
        after(T1, "rope_t")
        nc.scalar.activation(dqk.rearrange("p (a i) n -> p a (i n)", a=2), ps[:, 0:2, :], ACT.Copy).then_inc(A1.done("dqk"), 1)
        after(V1, "sub_d")
        nc.scalar.activation(dS, dS, ACT.Exp, scale=32.0 ** -0.5).then_inc(A1.done("exp_d"), 1)
        after(V1, "lam1")
        nc.scalar.activation(lamb[:, 2:4], lamb[:, 0:2], ACT.Exp).then_inc(A1.done("lam"), 1)
        after(T1, "trans_d")
        nc.scalar.activation(pT, ps[:, 0:4, 0:384], ACT.Copy).then_inc(A1.done("pT"), 1)
        after(T1, "o_d")
        nc.scalar.activation(mix[:, :, SEQ:512], ps[:, 4, :].rearrange("p (a b) -> p a b", a=2),
                             ACT.Copy).then_inc(A1.done("o_d"), 1)
        nc.scalar.activation(gate_g, gate_g, ACT.Silu)
        nc.scalar.activation(z_s, z_s, ACT.Silu)
        nc.scalar.activation(o_m, o_m, ACT.Sigmoid).then_inc(A1.done("gates"), 1)
        after(V1, "pre_gate")
        nc.scalar.activation(sq, mix[:], ACT.Square).then_inc(A1.done("sq_o"), 1)
        after(V1, "mean_o")
        nc.scalar.activation(ms, ms, ACT.Sqrt).then_inc(A1.done("root_o"), 1)
        after(T1, "trans")
        for i in range(2):
            split_hi(a, i, A1)
        for n in range(IN1 + 1, IN1 + WO):
            mixer_hi(a, B, ENDS1, n, loads)

    def rotate(v, V, after, tile, src, dst, cos, sin, half, heads, names, shape):
        na, nb, nc_, nd, ne, nf = names
        x1, x2, y1, y2 = src[0], src[1], dst[0], dst[1]
        nc.vector.tensor_tensor(y1, x1, cos, ALU.mult).then_inc(V.done(na), 1)
        nc.vector.tensor_tensor(half, x2, sin, ALU.mult).then_inc(V.done(nb), 1)
        after(V, nb)
        nc.vector.tensor_tensor(y1, y1, half, ALU.subtract).then_inc(V.done(nc_), 1)
        nc.vector.tensor_tensor(y2, x1, sin, ALU.mult).then_inc(V.done(nd), 1)
        after(V, nc_)
        nc.vector.tensor_tensor(half, x2, cos, ALU.mult).then_inc(V.done(ne), 1)
        after(V, ne)
        nc.vector.tensor_tensor(y2, y2, half, ALU.add).then_inc(V.done(nf), 1)

    def decays(rows_bank, first, buf, col, op0, op1):
        for h in range(H):
            r = ps[:, rows_bank + h // 2, (h % 2) * SEQ:(h % 2) * SEQ + SEQ]
            nc.vector.tensor_scalar(buf[:, h, 0:SEQ], r, col[:, 0, first + h:first + h + 1], 0.0, op0, op1)
            last = nc.vector.tensor_scalar(buf[:, h, SEQ:384], r[:, P:SEQ], col[:, 1, first + h:first + h + 1], 0.0,
                                           op0, op1)
        return last

    def convolve(v, after, chunks, names, between):
        for c in chunks:
            last = nc.vector.tensor_scalar(cv[:, c, :], u[:, c, 0:SEQ], fp[:, F_CONV + 4 * c:F_CONV + 4 * c + 1],
                                           None, ALU.mult)
        last.then_inc(V1.done(names[0]), 1)
        for k in range(1, 4):
            between(k)
            after(V1, names[k - 1])
            for c in chunks:
                last = nc.vector.scalar_tensor_tensor(cv[:, c, :], u[:, c, k:k + SEQ],
                                                      fp[:, F_CONV + 4 * c + k:F_CONV + 4 * c + k + 1], cv[:, c, :],
                                                      ALU.mult, ALU.add)
            last.then_inc(V1.done(names[k]), 1)

    pm_sq = pm.rearrange("p a b -> p (a b)").rearrange("p (c n) -> p c n", c=4)

    def mixer1_dve(v, B, l):
        def after(S, name):
            v.wait_ge(S.sem, S.at(name, l))

        v.wait_ge(par_in, l * 32 + 32)
        v.wait_ge(con_in, 16)
        nc.vector.memset(u[:, :, 0:PAD], 0.0).then_inc(pads, 1)
        for n in range(7):
            mixer_lo(v, B, ENDS1, n)
        v.wait_ge(pads, l + 1)
        v.wait_ge(proj_evac, l * IN1 + 3 + 4)
        convolve(v, after, range(0, 6), ("cg0", "cg1", "cg2", "conv_g"), lambda k: mixer_lo(v, B, ENDS1, 6 + k))
        for n in range(10, 11):
            mixer_lo(v, B, ENDS1, n)
        v.wait_ge(proj_evac, l * IN1 + 6 + 4)
        convolve(v, after, range(6, 12), ("cs0", "cs1", "cs2", "conv_s"), lambda k: mixer_lo(v, B, ENDS1, 10 + k))
        for n in range(14, IN1 + 1):
            mixer_lo(v, B, ENDS1, n)
        v.wait_ge(proj_evac, l * IN1 + SMALL_AT + 1 + 4)
        nc.vector.tensor_tensor(sp_x, small[:, :, 8:SMALL], over(par[:, R_SPB:R_SPB + 12], [P, TILES, 12], 1),
                                ALU.add).then_inc(V1.done("sp_in"), 1)
        after(V1, "sp_in")
        nc.vector.tensor_tensor(sp_x, sp_x, over(K(C_SGN, 12), [P, TILES, 12], 1), ALU.mult).then_inc(V1.done("sp_sgn"), 1)
        after(V1, "sp_sgn")
        nc.vector.scalar_tensor_tensor(sp_c, sp_x, -1.0, sp_x, ALU.mult, ALU.max).then_inc(V1.done("sp_abs"), 1)
        after(A1, "sp_e")
        nc.vector.tensor_scalar(sp_u, sp_e, 1.0, None, ALU.add).then_inc(V1.done("sp_u"), 1)
        after(V1, "sp_u")
        nc.vector.tensor_scalar(sp_c, sp_u, -1.0, None, ALU.add).then_inc(V1.done("sp_um"), 1)
        after(V1, "sp_um")
        nc.vector.tensor_tensor(sp_e, sp_e, sp_c, ALU.subtract).then_inc(V1.done("sp_em"), 1)
        after(V1, "sp_em")
        nc.vector.reciprocal(sp_c, sp_u).then_inc(V1.done("sp_ru"), 1)
        after(V1, "sp_ru")
        nc.vector.tensor_tensor(sp_e, sp_e, sp_c, ALU.mult).then_inc(V1.done("sp_corr"), 1)
        nc.vector.tensor_scalar(sp_x, sp_x, 0.0, None, ALU.max).then_inc(V1.done("sp_max"), 1)
        after(A1, "sp_l")
        after(V1, "sp_max")
        nc.vector.tensor_tensor(sp_x, sp_x, sp_l, ALU.add).then_inc(V1.done("sp_l"), 1)
        after(V1, "sp_l")
        nc.vector.tensor_tensor(sp_x, sp_x, sp_e, ALU.add).then_inc(V1.done("sp"), 1)
        after(V1, "sp")
        nc.vector.tensor_copy(dt, sp_x[:, :, 4:8]).then_inc(V1.done("dt"), 1)
        after(A1, "ea")
        nc.vector.scalar_tensor_tensor(ld, sp_x, -1.0, over(ea, [P, TILES, 12], 1), ALU.mult,
                                       ALU.mult).then_inc(V1.done("ld"), 1)
        after(A1, "eb")
        nc.vector.tensor_scalar(negm, beta, 1.0, None, ALU.add).then_inc(V1.done("eb1"), 1)
        after(V1, "eb1")
        nc.vector.reciprocal(beta, negm).then_inc(V1.done("beta"), 1)
        after(A1, "gc")
        after(T1, "rows_g")
        decays(4, 0, dT, gc, ALU.subtract, ALU.min).then_inc(V1.done("dec_g"), 1)
        after(T1, "sumsq")
        nc.vector.tensor_scalar(pm_sq.rearrange("p (a c) n -> p a (c n)", a=2), ps[:, 0:2, :], EPS, None,
                                ALU.add).then_inc(V1.done("rs"), 1)
        after(A1, "root")
        nc.vector.reciprocal(pm_sq, pm_sq).then_inc(V1.done("rrs"), 1)
        after(V1, "rrs")
        nc.vector.scalar_tensor_tensor(cv[:, 0:2, :], cv[:, 0:2, :], 64.0 ** -0.5, pm_sq[:, 0:2, :], ALU.mult, ALU.mult)
        nc.vector.tensor_tensor(cv[:, 2:4, :], cv[:, 2:4, :], pm_sq[:, 2:4, :], ALU.mult).then_inc(V1.done("qkn"), 1)
        after(V1, "qkn")
        after(T1, "beta_rows")
        for h in range(H):
            half = slice(64 * (h % 2), 64 * (h % 2) + 64)
            last = nc.vector.tensor_tensor(kb[half, h // 2, :], cv[half, 2 + h // 2, :],
                                           ps[half, 2 + h // 2, (h % 2) * SEQ:(h % 2 + 1) * SEQ], ALU.mult)
        last.then_inc(V1.done("kb"), 1)
        after(G1, "dec_g")
        after(T1, "kk")
        nc.vector.tensor_tensor(lT, ps[:, 0:4, 0:384], dT, ALU.mult).then_inc(V1.done("lT"), 1)
        after(T1, "qk")
        nc.vector.tensor_tensor(dT, ps[:, 4:8, 0:384], dT, ALU.mult).then_inc(V1.done("aT"), 1)
        after(V1, "lT")
        lTd = diag(lT)
        xT4 = xT.rearrange("p (h b) n -> p h b n", h=H)
        nc.vector.tensor_tensor(xT4, lTd, over(K(C_MT), [P, H, 2, P], 1, 1), ALU.mult).then_inc(V1.done("mt1"), 1)
        after(V1, "mt1")
        nc.vector.scalar_tensor_tensor(xT, xT, -1.0, over(IDENT, [P, 8, P], 1), ALU.mult, ALU.add).then_inc(V1.done("xT"), 1)
        with v.Fori(0, LEVELS) as j:
            n = l * LEVELS + j
            v.wait_ge(inv_r, n + 1)
            nc.vector.tensor_tensor(xi.rearrange("p (a i) n -> p a (i n)", a=2),
                                    xi.rearrange("p (a i) n -> p a (i n)", a=2), ps[:, 4:6, :], ALU.subtract)
            nc.vector.tensor_tensor(xT.rearrange("p (a i) n -> p a (i n)", a=2),
                                    xT.rearrange("p (a i) n -> p a (i n)", a=2), ps[:, 6:8, :],
                                    ALU.subtract).then_inc(inv_x, 1)
        after(T1, "vt")
        nc.vector.tensor_tensor(vb.rearrange("p a (h d) -> p (a h) d", h=H),
                                ps[:, 0, :].rearrange("p (i d) -> p i d", d=64),
                                over(beta.rearrange("p a h -> p (a h)"), [P, 8, 64], 2), ALU.mult).then_inc(V1.done("vb"), 1)
        after(T1, "l21")
        nc.vector.tensor_tensor(r2, vb[:, 1, :], ps[:, 2, 0:SEQ], ALU.subtract).then_inc(V1.done("r2"), 1)

        after(A1, "xs")
        nc.vector.tensor_tensor(xdt.rearrange("p a (h d) -> p (a h) d", h=H),
                                xs.rearrange("p a (h d) -> p (a h) d", h=H),
                                over(dt.rearrange("p a h -> p (a h)"), [P, 8, 64], 2), ALU.mult).then_inc(V1.done("xdt"), 1)
        after(T1, "rows_s")
        decays(6, 4, dT2, gc, ALU.subtract, ALU.min).then_inc(V1.done("dec_s"), 1)
        after(G1, "dec_s")
        after(T1, "cb")
        for grp in range(2):
            last = nc.vector.tensor_tensor(dT2[:, 2 * grp:2 * grp + 2, :], over(ps[:, 1 + grp, 0:384], [P, 2, 384], 1),
                                           dT2[:, 2 * grp:2 * grp + 2, :], ALU.mult)
        last.then_inc(V1.done("w_s"), 1)
        nc.vector.tensor_tensor(xs.rearrange("p a (h d) -> p a h d", h=H), xs.rearrange("p a (h d) -> p a h d", h=H),
                                over(par[:, R_DSK:R_DSK + H], [P, TILES, H, 64], 1, 3), ALU.mult).then_inc(V1.done("skip"), 1)
        after(V1, "skip")
        after(T1, "o_s")
        nc.vector.tensor_tensor(mix[:, :, 512:768], xs, ps[:, 3, :].rearrange("p (a b) -> p a b", a=2),
                                ALU.add).then_inc(V1.done("o_s"), 1)

        nc.vector.tensor_tensor(negm, small[:, :, 4:8], over(par[:, R_IB:R_IB + H], [P, TILES, H], 1),
                                ALU.add).then_inc(V1.done("ai"), 1)
        after(V1, "ai")
        nc.vector.tensor_tensor(acol, negm, gc[:, :, 8:12], ALU.subtract).then_inc(V1.done("acol"), 1)
        after(T1, "rows_a")
        tmp = sq_m
        for h in range(H):
            last = nc.vector.tensor_tensor(tmp[:, 2 * h:2 * h + 2, :],
                                           ps[:, 4 + h // 2, (h % 2) * SEQ:(h % 2 + 1) * SEQ].rearrange("p (a n) -> p a n", a=2),
                                           over(NEGM, [P, 2, P], 1), ALU.add)
        last.then_inc(V1.done("tmp_m"), 1)
        after(V1, "tmp_m")
        nc.vector.reduce_max(md.rearrange("p h t -> p (h t)"), tmp, AX).then_inc(V1.done("md"), 1)
        nc.vector.reduce_max(mfull.rearrange("p (a b) -> p a b", a=2),
                             ps[:, 4:6, :].rearrange("p a (b n) -> p a b n", b=2)[:, :, :, 0:P],
                             AX).then_inc(V1.done("mf"), 1)
        after(V1, "mf")
        nc.vector.tensor_scalar(mcol[:, 0, :], md[:, :, 0], 0.0, None, ALU.max).then_inc(V1.done("m0"), 1)
        nc.vector.scalar_tensor_tensor(mcol[:, 1, :], md[:, :, 1], 0.0, mfull, ALU.max, ALU.max).then_inc(V1.done("m1"), 1)
        after(T1, "rows_m")
        decays(6, 0, dT2, acol, ALU.subtract, ALU.max).then_inc(V1.done("dec_m"), 1)
        after(G1, "dec_m")
        after(T1, "qk_m")
        nc.vector.tensor_tensor(dT2, ps[:, 0:4, 0:384], dT2, ALU.mult).then_inc(V1.done("w_m"), 1)
        after(V1, "m1")
        nc.vector.tensor_tensor(negm, mcol, gc[:, :, 8:12], ALU.add).then_inc(V1.done("mt"), 1)
        after(V1, "mt")
        nc.vector.tensor_scalar(negm, negm, -1.0, 85.0, ALU.mult, ALU.min).then_inc(V1.done("negm"), 1)
        after(T1, "o_m")
        o65 = ps[:, 4:6, 0:H * 65].rearrange("p a (h d) -> p a h d", h=H)
        after(A1, "den")
        nc.vector.tensor_tensor(den, den, em, ALU.max).then_inc(V1.done("denm"), 1)
        after(V1, "denm")
        nc.vector.reciprocal(den, den).then_inc(V1.done("rden"), 1)
        after(V1, "rden")
        nc.vector.tensor_tensor(mix[:, :, 768:D].rearrange("p a (h d) -> p a h d", h=H), o65[:, :, :, 0:64],
                                over(den, [P, TILES, H, 64], 3), ALU.mult).then_inc(V1.done("o_m"), 1)

        after(A1, "o_g")
        v.wait_ge(proj_evac, l * IN1 + IN1 + 4)
        for tile in range(TILES):
            s_ = rope_in[:, tile, :].rearrange("p (h z n) -> p h z n", h=16, z=2)
            d_ = qkr[:, tile, :].rearrange("p (h z n) -> p h z n", h=16, z=2)
            names = [f"r{c}{tile + 1}" for c in "abcdef"]
            rotate(v, V1, after, tile, (s_[:, :, 0, :], s_[:, :, 1, :]), (d_[:, :, 0, :], d_[:, :, 1, :]),
                   over(COS[:, tile, :], [P, 16, 16], 1), over(SIN[:, tile, :], [P, 16, 16], 1),
                   rt[:, tile, :].rearrange("p (h n) -> p h n", h=16), 16, names, None)
        after(T1, "sc_d")
        for q in range(2):
            nc.vector.tensor_tensor(dS[:, 4 * q:4 * q + 4, 0:P], ps[:, 0:4, q * P:(q + 1) * P],
                                    over(NEGD[:, 0:P], [P, 4, P], 1), ALU.add)
            last = nc.vector.tensor_tensor(dS[:, 4 * q:4 * q + 4, P:384], ps[:, 4:8, q * SEQ:(q + 1) * SEQ],
                                           over(NEGD[:, P:384], [P, 4, SEQ], 1), ALU.add)
        last.then_inc(V1.done("mask_d"), 1)
        after(V1, "mask_d")
        part = (slice(0, P), slice(P, 384))
        for tile in range(TILES):
            last = nc.vector.reduce_max(rmax[:, tile, :], dS[:, :, part[tile]], AX)
        last.then_inc(V1.done("max_d"), 1)
        after(V1, "max_d")
        for tile in range(TILES):
            w = P if tile == 0 else SEQ
            last = nc.vector.tensor_tensor(dS[:, :, part[tile]], dS[:, :, part[tile]],
                                           over(rmax[:, tile, :], [P, 8, w], 2), ALU.subtract)
        last.then_inc(V1.done("sub_d"), 1)
        after(A1, "exp_d")
        for tile in range(TILES):
            last = nc.vector.reduce_sum(coef[:, tile, :], dS[:, :, part[tile]], AX)
        last.then_inc(V1.done("sum_d"), 1)
        after(V1, "sum_d")
        nc.vector.reciprocal(coef, coef).then_inc(V1.done("rec_d"), 1)
        lam4 = par[:, R_LAM:R_LAM + 128].rearrange("p (a b n) -> p a b n", a=2, b=2)
        nc.vector.tensor_tensor(lamp, lam4[:, :, 0, :], lam4[:, :, 1, :], ALU.mult).then_inc(V1.done("lam0"), 1)
        after(V1, "lam0")
        nc.vector.reduce_sum(lamb[:, 0:2], lamp, AX).then_inc(V1.done("lam1"), 1)
        after(A1, "lam")
        nc.vector.scalar_tensor_tensor(lamb[:, 4:5], lamb[:, 3:4], par[:, R_LI:R_LI + 1], lamb[:, 2:3], ALU.subtract,
                                       ALU.subtract).then_inc(V1.done("lam2"), 1)
        after(V1, "lam2")
        second = coef.rearrange("p a (j c) -> p (a j) c", c=2)[:, :, 1]
        nc.vector.tensor_scalar(second, second, lamb[:, 4:5], None, ALU.mult).then_inc(V1.done("coef"), 1)
        after(V1, "coef")
        for tile in range(TILES):
            w = P if tile == 0 else SEQ
            last = nc.vector.tensor_tensor(dS[:, :, part[tile]], dS[:, :, part[tile]],
                                           over(coef[:, tile, :], [P, 8, w], 2), ALU.mult)
        last.then_inc(V1.done("scale_d"), 1)
        after(V1, "scale_d")
        dS2 = dS.rearrange("p (h c) n -> p h c n", c=2)
        nc.vector.tensor_tensor(pD, dS2[:, :, 0, :], dS2[:, :, 1, :], ALU.add).then_inc(V1.done("add_d"), 1)

        after(A1, "gates")
        nc.vector.tensor_tensor(mix[:, :, 512:768], mix[:, :, 512:768], z_s, ALU.mult)
        nc.vector.tensor_tensor(mix[:, :, 768:D], mix[:, :, 768:D], o_m, ALU.mult).then_inc(V1.done("pre_gate"), 1)
        after(A1, "sq_o")
        nc.vector.reduce_sum(ms.rearrange("p a h -> p (a h)"), sq.rearrange("p a (h d) -> p (a h) d", d=64),
                             AX).then_inc(V1.done("sums_o"), 1)
        after(V1, "sums_o")
        pairs = ms[:, :, 8:12].rearrange("p a (g c) -> p a g c", c=2)
        nc.vector.tensor_tensor(gsum, pairs[:, :, :, 0], pairs[:, :, :, 1], ALU.add).then_inc(V1.done("pair0"), 1)
        after(V1, "pair0")
        nc.vector.tensor_scalar(pairs, over(gsum, [P, TILES, 2, 2], 3), 0.5, None, ALU.mult).then_inc(V1.done("pair1"), 1)
        after(V1, "pair1")
        nc.vector.tensor_scalar(ms, ms, 1.0 / 64, EPS, ALU.mult, ALU.add).then_inc(V1.done("mean_o"), 1)
        after(A1, "root_o")
        nc.vector.reciprocal(ms, ms).then_inc(V1.done("rstd_o"), 1)
        gain = par[:, R_GAIN:R_GAIN + D]
        nc.vector.tensor_scalar(gain[:, SEQ:512], gain[:, SEQ:512], par[:, R_LI + 1:R_LI + 2], None,
                                ALU.mult).then_inc(V1.done("gl"), 1)
        after(V1, "gl")
        mix16 = mix[:].rearrange("p a (h d) -> p (a h) d", d=64)
        nc.vector.tensor_tensor(mix16, mix16, over(ms.rearrange("p a h -> p (a h)"), [P, 32, 64], 2),
                                ALU.mult).then_inc(V1.done("norm_o"), 1)
        after(V1, "norm_o")
        nc.vector.tensor_tensor(mix[:], mix[:], over(gain, [P, TILES, D], 1), ALU.mult).then_inc(V1.done("gain_o"), 1)
        after(V1, "gain_o")
        nc.vector.tensor_tensor(mix[:, :, 0:SEQ], mix[:, :, 0:SEQ], gate_g, ALU.mult).then_inc(V1.done("gate_o"), 1)
        for i in range(2):
            split_lo(v, i, A1, l, V1)
        for n in range(IN1 + 1, IN1 + WO):
            mixer_lo(v, B, ENDS1, n)

    sq_m = cv.rearrange("p a b -> p (a b)")[:, 8 * SEQ:12 * SEQ].rearrange("p (a b) -> p a b", a=8)
    def mixer1_pool(p, l):
        def after(S, name):
            p.wait_ge(S.sem, S.at(name, l))

        def mask(buf):
            d_ = diag(buf)
            return nc.gpsimd.tensor_tensor(d_, d_, over(TRIU, [P, H, 2, P], 1, 1), ALU.mult)

        p.wait_ge(con_in, 16)
        after(A1, "dec_g")
        mask(dT).then_inc(G1.done("dec_g"), 1)
        after(V1, "xT")
        lTd = diag(lT)
        bT4 = bT.rearrange("p (h b) n -> p h b n", h=H)
        settle(p)
        with p.Fori(0, LEVELS) as j:
            n = l * LEVELS + j
            p.wait_ge(inv_p, n + 1)
            lev = con[:, bass.ds(j * P + (C_MT + P - NBASE), P)]
            nc.gpsimd.tensor_tensor(bT4, lTd, over(lev, [P, H, 2, P], 1, 1), ALU.mult).then_inc(inv_b, 1)
        after(A1, "dec_s")
        mask(dT2).then_inc(G1.done("dec_s"), 1)
        after(A1, "dec_m")
        mask(dT2).then_inc(G1.done("dec_m"), 1)

    m2 = Arena()
    con2 = m2.take(N2)
    ada = m2.take(3 * D)
    ada_w = m2.take(3 * D)
    mrow = m2.take(3, D)
    cond = m2.take(KT)
    mark2 = m2.at
    rot_in = m2.take(TILES, 4 * SEQ)
    rot = m2.take(TILES, 4 * SEQ)
    half = m2.take(TILES, 512)
    m2.at = mark2
    b1, b2, b3 = (m2.take(H, 384) for _ in range(3))
    m2.at = mark2 + 5 * 1024
    rqk = m2.take(8, SEQ)
    sqk = m2.take(4, SEQ)
    v_r, g_r = m2.take(TILES, 512), m2.take(TILES, 512)
    v_2, v_b = m2.take(TILES, SEQ), m2.take(TILES, SEQ)
    bn8 = m2.take(8, 6)
    mv8 = m2.take(8, 2)
    rstd8 = m2.take(8)
    max2 = m2.take(TILES, H)
    sum2 = m2.take(TILES, H)
    SL, NEGC, CNT = con2[:, C2_SL:C2_SL + P], con2[:, C2_NEGC:C2_NEGC + 384], con2[:, C2_CNT:C2_CNT + 384]
    RET = con2[:, C2_RET:C2_RET + H * 384].rearrange("p (h n) -> p h n", h=H)
    ROT = con2[:, C2_ROT:C2_ROT + 256].rearrange("p (z t k n) -> p z t k n", z=2, t=2, k=2)
    c_in, cond_done = sem("c_in"), sem("cond_done")
    ada_acc = sem("ada_acc")
    ada_in = sem("ada_in")
    ada_zero, bias_in, mod_t = sem("ada_zero"), sem("bias_in"), sem("mod_t")
    T2 = steps("mix2_t", "qkt sc_r o_r sc_d zt trans_d o_d between o_b trans")
    A2 = steps("mix2_a", "rqk gate root_r exp_d abs_b e_b l_b pT exp_b o_b hi0 hi1")
    V2 = steps("mix2_v", "ra1 rb1 rc1 rd1 re1 rf1 ra2 rb2 rc2 rd2 re2 rf2 w_r stats_r aggr_r var_r rstd_r norm_r "
                         "mask_d max_d sub_d cnt_d sum_d rec_d sp_b t_b o_d exp_arg gated lo0 lo1")
    G2 = steps("mix2_g", "keep a")

    def bias_sp(sp, h):
        sp.wait_ge(ada_zero, h + 1)
        settle(sp)
        sp.dma_start(ada[0:1, :], t["b_ada"][bass.ds(h, 1), :]).then_inc(bias_in, 16)

    def chunk_sp(sp, h, k):
        sp.wait_ge(ada_acc, h * KT + k + 1)
        settle(sp)
        sp.dma_start(ada_w, t["w_ada"][bass.ds(h, 1), bass.ds(k, 1) if not isinstance(k, int) else slice(k, k + 1), :, :]
                     .rearrange("h k p n -> p (h k n)")).then_inc(ada_in, 16)

    def zero_dve(v, h, earlier):
        if earlier is not None:
            v.wait_ge(mod_t, earlier)
        nc.vector.memset(ada, 0.0).then_inc(ada_zero, 1)

    def chunk_dve(v, h, k):
        if isinstance(k, int):
            if k == 0:
                v.wait_ge(bias_in, h * 16 + 16)
            c = cond[:, k:k + 1]
        else:
            v.wait_ge(bias_in, h * 16 + 16)
            c = cond[:, bass.ds(k, 1)]
        v.wait_ge(ada_in, h * (KT * 16) + k * 16 + 16)
        v.wait_ge(ada_acc, h * KT + k + 1)
        nc.vector.scalar_tensor_tensor(ada, ada_w, c, ada, ALU.mult, ALU.add).then_inc(ada_acc, 1)

    def mod_dve(v, h, weight):
        v.wait_ge(mod_t, h + 1)
        two = "p (b n) -> p b n"
        nc.vector.tensor_copy(mrow[:, 0, :].rearrange(two, b=2), ps[:, 0:2, :]).then_inc(mod_v.done("shift"), 1)
        nc.vector.tensor_scalar(mrow[:, 1, :].rearrange(two, b=2), ps[:, 2:4, :], 1.0, None,
                                ALU.add).then_inc(mod_v.done("scale"), 1)
        nc.vector.tensor_scalar(mrow[:, 2, :].rearrange(two, b=2), ps[:, 4:6, :], 1.0, weight, ALU.add,
                                ALU.mult).then_inc(mod_v.done("rows"), 1)

    def mod_pe(pe, h):
        pe.wait_ge(ada_acc, h * KT + (KT + 1))
        pe.wait_ge(x_ready, (h + 6) * 16 + 16)
        for b in range(6):
            last = nc.tensor.matmul(ps[:, b, :], ONES, ada[:, b * 512:(b + 1) * 512], start=True, stop=True)
        last.then_inc(mod_t, 1)

    def mixer2_sp(sp, B, l):
        bias_sp(sp, l * 3 + 2)
        for n in range(IN2 + WO):
            name, i = ("w_in_2", n) if n < IN2 else ("w_out_2", n - IN2)
            mixer_load(sp, B, ENDS2, n, t[name][bass.ds(l, 1), i:i + 1, :, :].rearrange("l i p n -> p (l i n)"))
            if n < KT:
                chunk_sp(sp, l * 3 + 2, n)

    def mixer2_pe(pe, B, l, g):
        def after(S, name):
            pe.wait_ge(S.sem, S.at(name, l))

        pre_done(pe, g)
        for n in range(IN2):
            pe.wait_ge(proj_evac, l * IN2 + (DEPTH * IN1 + n + 1))
            for j, half_ in mixer_units(ENDS2, n):
                (feature_unit if n in (4, 5) else token_unit)(pe, B, j, j % UBUF, 4 + n % 4, half_)
        pe.wait_ge(proj_evac, l * IN2 + (DEPTH * IN1 + IN2 + 4))

        after(V2, "rf2")
        for c in range(8):
            for tile in range(TILES):
                o = (c % 2) * SEQ + tile * P
                last = nc.tensor.transpose(ps[:, c // 2, o:o + P], rot[:, tile, c * P:(c + 1) * P], IDENT)
        last.then_inc(T2.done("qkt"), 1)
        after(A2, "rqk")
        for h in range(H):
            hf = slice(64 * (h % 2), 64 * (h % 2) + 64)
            last = scores_T(4 + h, rqk[hf, 2 + h // 2, :], rqk[hf, h // 2, :], h)
        last.then_inc(T2.done("sc_r"), 1)
        after(V2, "w_r")
        for h in range(H):
            c = slice(h * P, (h + 1) * P)
            last = weighted_values(ps[:, 0, c], ps[:, 1, c], b1[:, h, :], v_r[:, 0, c], v_r[:, 1, c])
        last.then_inc(T2.done("o_r"), 1)
        for h in range(H):
            hf = slice(64 * (h % 2), 64 * (h % 2) + 64)
            q_, k_ = rqk[hf, 4 + h // 2, :], rqk[hf, 6 + h // 2, :]
            nc.tensor.matmul(ps[:, 4 + h, 0:P], q_[:, 0:P], k_[:, 0:P], start=True, stop=True)
            last = nc.tensor.matmul(ps[:, 4 + h, P:384], q_[:, P:SEQ], k_, start=True, stop=True)
        last.then_inc(T2.done("sc_d"), 1)
        after(V2, "mask_d")
        for h in range(H):
            hf = slice(64 * (h % 2), 64 * (h % 2) + 64)
            last = scores_T(4 + h, sqk[hf, 2 + h // 2, :], sqk[hf, h // 2, :], h)
        last.then_inc(T2.done("zt"), 1)
        after(V2, "norm_r")
        after(V2, "cnt_d")
        for h in range(H):
            for b in range(3):
                last = nc.tensor.transpose(ps[:, h, b * P:(b + 1) * P], b1[:, h, b * P:(b + 1) * P], IDENT)
        last.then_inc(T2.done("trans_d"), 1)
        after(A2, "pT")
        after(V2, "t_b")
        for h in range(H):
            c = slice(h * 64, (h + 1) * 64)
            last = weighted_values(ps[:, 4, c], ps[:, 4, SEQ + h * 64:SEQ + (h + 1) * 64], b2[:, h, :],
                                   v_2[:, 0, c], v_2[:, 1, c])
        last.then_inc(T2.done("o_d"), 1)
        after(G2, "keep")
        for h in range(H):
            nc.tensor.matmul(ps[:, h, 0:384], SL, b3[:, h, :], start=True, stop=False)
            last = nc.tensor.matmul(ps[:, h, P:SEQ], ONES, b3[:, h, SEQ:384], start=False, stop=True)
        last.then_inc(T2.done("between"), 1)
        after(G2, "a")
        for h in range(H):
            c = slice(h * 64, (h + 1) * 64)
            last = weighted_values(ps[:, 5, c], ps[:, 5, SEQ + h * 64:SEQ + (h + 1) * 64], b1[:, h, :],
                                   v_b[:, 0, c], v_b[:, 1, c])
        last.then_inc(T2.done("o_b"), 1)
        after(A2, "o_b")
        after(V2, "gated")
        transposes_pe(0)
        transposes_pe(1).then_inc(T2.done("trans"), 1)
        after(V2, "lo1")
        out_product(pe, B, ENDS2, IN2)

    def mixer2_act(a, B, loads, l):
        def after(S, name):
            a.wait_ge(S.sem, S.at(name, l))

        for n in range(IN2):
            if n == 0:
                mixer_hi(a, B, ENDS2, 0, loads)
            mixer_hi(a, B, ENDS2, n + 1, loads)
            a.wait_ge(unit_done, B + (ENDS2[n] + CREDIT))
            two = ps[:, 4 + n % 4, :].rearrange("p (a b) -> p a b", a=2)
            if n < 4:
                last = nc.scalar.activation(rot_in[:, :, n * SEQ:(n + 1) * SEQ], two, ACT.Copy)
            elif n < 6:
                last = nc.scalar.activation(sqk[:, 2 * (n - 4):2 * (n - 4) + 2, :], two, ACT.Copy,
                                            scale=64.0 ** -0.5 if n == 4 else 1.0)
            elif n < 8:
                last = nc.scalar.activation(v_r[:, :, (n - 6) * SEQ:(n - 5) * SEQ], two, ACT.Copy)
            elif n < 10:
                last = nc.scalar.activation(g_r[:, :, (n - 8) * SEQ:(n - 7) * SEQ], two, ACT.Copy)
            else:
                last = nc.scalar.activation(v_2 if n == 10 else v_b, two, ACT.Copy)
            last.then_inc(proj_evac, 1)
        after(T2, "qkt")
        nc.scalar.activation(rqk.rearrange("p (a i) n -> p a (i n)", a=4), ps[:, 0:4, :], ACT.Copy).then_inc(A2.done("rqk"), 1)
        a.wait_ge(proj_evac, l * IN2 + (DEPTH * IN1 + IN2 + 4))
        nc.scalar.activation(g_r, g_r, ACT.Silu).then_inc(A2.done("gate"), 1)
        after(V2, "var_r")
        nc.scalar.activation(rstd8, rstd8, ACT.Sqrt).then_inc(A2.done("root_r"), 1)
        after(V2, "sub_d")
        nc.scalar.activation(b1, b1, ACT.Exp, scale=64.0 ** -0.5).then_inc(A2.done("exp_d"), 1)
        after(T2, "zt")
        nc.scalar.activation(b3, ps[:, 4:8, 0:384], ACT.Abs).then_inc(A2.done("abs_b"), 1)
        after(A2, "abs_b")
        nc.scalar.activation(b3, b3, ACT.Exp, scale=-1.0).then_inc(A2.done("e_b"), 1)
        after(A2, "e_b")
        nc.scalar.activation(b3, b3, ACT.Ln, bias=one[:, 0:1]).then_inc(A2.done("l_b"), 1)
        after(T2, "trans_d")
        nc.scalar.activation(b2, ps[:, 0:4, 0:384], ACT.Copy).then_inc(A2.done("pT"), 1)
        after(V2, "exp_arg")
        nc.scalar.activation(b1, b1, ACT.Exp).then_inc(A2.done("exp_b"), 1)
        after(T2, "o_b")
        nc.scalar.activation(mix[:, :, 768:D], ps[:, 5, :].rearrange("p (a b) -> p a b", a=2),
                             ACT.Copy).then_inc(A2.done("o_b"), 1)
        after(T2, "trans")
        for i in range(2):
            split_hi(a, i, A2)
        for n in range(IN2 + 1, IN2 + WO):
            mixer_hi(a, B, ENDS2, n, loads)

    def mixer2_dve(v, B, l):
        def after(S, name):
            v.wait_ge(S.sem, S.at(name, l))

        zero_dve(v, l * 3 + 2, l * 3 + 2)
        mixer_lo(v, B, ENDS2, 0)
        for n in range(IN2):
            mixer_lo(v, B, ENDS2, n + 1)
            if n < KT:
                chunk_dve(v, l * 3 + 2, n)
        v.wait_ge(proj_evac, l * IN2 + (DEPTH * IN1 + 4 + 4))
        for tile in range(TILES):
            s_ = rot_in[:, tile, :].rearrange("p (k h z n) -> p k h z n", k=2, h=8, z=2)
            d_ = rot[:, tile, :].rearrange("p (k h z n) -> p k h z n", k=2, h=8, z=2)
            rotate(v, V2, after, tile, (s_[:, :, :, 0, :], s_[:, :, :, 1, :]), (d_[:, :, :, 0, :], d_[:, :, :, 1, :]),
                   over(ROT[:, 0, tile, :, :], [P, 2, 8, 32], 2), over(ROT[:, 1, tile, :, :], [P, 2, 8, 32], 2),
                   half[:, tile, :].rearrange("p (k h n) -> p k h n", k=2, h=8), 16,
                   [f"r{c}{tile + 1}" for c in "abcdef"], None)
        after(T2, "sc_r")
        nc.vector.tensor_tensor(b1, ps[:, 4:8, 0:384], RET, ALU.mult).then_inc(V2.done("w_r"), 1)
        after(T2, "o_r")
        for i in range(8):
            last = nc.vector.bn_stats(bn8[:, i, :], ps[:, i // 4, (i % 4) * P:(i % 4 + 1) * P])
        last.then_inc(V2.done("stats_r"), 1)
        after(V2, "stats_r")
        settle(v)
        for i in range(8):
            last = nc.vector.bn_aggr(mv8[:, i, :], bn8[:, i, :])
        last.then_inc(V2.done("aggr_r"), 1)
        after(V2, "aggr_r")
        nc.vector.tensor_scalar(rstd8, mv8[:, :, 1], EPS, None, ALU.add).then_inc(V2.done("var_r"), 1)
        after(A2, "root_r")
        nc.vector.reciprocal(rstd8, rstd8).then_inc(V2.done("rstd_r"), 1)
        after(V2, "rstd_r")
        for i in range(8):
            last = nc.vector.tensor_scalar(mix[:, i // 4, (i % 4) * P:(i % 4 + 1) * P],
                                           ps[:, i // 4, (i % 4) * P:(i % 4 + 1) * P], mv8[:, i, 0:1],
                                           rstd8[:, i:i + 1], ALU.subtract, ALU.mult)
        last.then_inc(V2.done("norm_r"), 1)
        part = (slice(0, P), slice(P, 384))
        after(T2, "sc_d")
        nc.vector.tensor_tensor(b1, ps[:, 4:8, 0:384], over(NEGC, [P, H, 384], 1), ALU.add).then_inc(V2.done("mask_d"), 1)
        after(V2, "mask_d")
        for tile in range(TILES):
            last = nc.vector.reduce_max(max2[:, tile, :], b1[:, :, part[tile]], AX)
        last.then_inc(V2.done("max_d"), 1)
        after(V2, "max_d")
        for tile in range(TILES):
            w = P if tile == 0 else SEQ
            last = nc.vector.tensor_tensor(b1[:, :, part[tile]], b1[:, :, part[tile]],
                                           over(max2[:, tile, :], [P, H, w], 2), ALU.subtract)
        last.then_inc(V2.done("sub_d"), 1)
        after(A2, "exp_d")
        nc.vector.tensor_tensor(b1, b1, over(CNT, [P, H, 384], 1), ALU.mult).then_inc(V2.done("cnt_d"), 1)
        after(V2, "cnt_d")
        for tile in range(TILES):
            last = nc.vector.reduce_sum(sum2[:, tile, :], b1[:, :, part[tile]], AX)
        last.then_inc(V2.done("sum_d"), 1)
        after(V2, "sum_d")
        nc.vector.reciprocal(sum2, sum2).then_inc(V2.done("rec_d"), 1)
        after(A2, "l_b")
        nc.vector.scalar_tensor_tensor(b3, ps[:, 4:8, 0:384], 0.0, b3, ALU.max, ALU.add).then_inc(V2.done("sp_b"), 1)
        after(V2, "sp_b")
        after(T2, "trans_d")
        nc.vector.tensor_tensor(b1, ps[:, 4:8, 0:384], b3, ALU.subtract).then_inc(V2.done("t_b"), 1)
        after(T2, "o_d")
        nc.vector.tensor_tensor(mix[:, :, 512:768].rearrange("p a (h d) -> p a h d", h=H),
                                ps[:, 4, :].rearrange("p (a h d) -> p a h d", a=2, h=H),
                                over(sum2, [P, TILES, H, 64], 3), ALU.mult).then_inc(V2.done("o_d"), 1)
        after(T2, "between")
        nc.vector.tensor_tensor(b1, b1, ps[:, 0:4, 0:384], ALU.subtract).then_inc(V2.done("exp_arg"), 1)
        after(A2, "gate")
        nc.vector.tensor_tensor(mix[:, :, 0:512], mix[:, :, 0:512], g_r, ALU.mult).then_inc(V2.done("gated"), 1)
        for i in range(2):
            split_lo(v, i, A2, l, V2)
        for n in range(IN2 + 1, IN2 + WO):
            mixer_lo(v, B, ENDS2, n)

    def mixer2_pool(p, l):
        def after(S, name):
            p.wait_ge(S.sem, S.at(name, l))

        after(V2, "t_b")
        d_ = diag(b3)
        nc.gpsimd.tensor_tensor(d_, d_, over(SU, [P, H, 2, P], 1, 1), ALU.mult).then_inc(G2.done("keep"), 1)
        after(A2, "exp_b")
        d_ = diag(b1)
        nc.gpsimd.tensor_tensor(d_, d_, over(SU, [P, H, 2, P], 1, 1), ALU.mult).then_inc(G2.done("a"), 1)

    one = sb("one", [P, 1])
    first = sb("first", [P, 10])
    one_set = sem("one_set")
    out_sent = sem("out_sent")

    def rows_load(sp, L, pos):
        sp.dma_start(rows[:, pos % 2, :, :].rearrange("p a b -> p (a b)"),
                     t["rows"][bass.ds(L * 3 + pos, 1), :].to_broadcast([P, 2 * D])).then_inc(rows_in[pos % 2], 16)

    block = ctx.enter_context(nc.Block())

    def units1(l):
        B = l * LU1
        return B, B + FU, B + (FU + ENDS1[-1])

    def units2(l):
        B = l * LU2 + DEPTH * LU1
        return B, B + FU, B + (FU + ENDS2[-1])

    def loads1(l):
        n = l * LOADS1
        m_ = (IN1 + WO) // SLOTS
        return n, [n + NF] * 3 + [l * m_], n + (NF + m_)

    def loads2(l):
        n = l * LOADS2 + DEPTH * LOADS1
        m_ = (IN2 + WO) // SLOTS
        return n, [n + NF] * 3 + [l * m_ + DEPTH * (IN1 + WO) // SLOTS], n + (NF + m_)

    def ada_sp(sp, h):
        return (lambda: bias_sp(sp, h), lambda k: chunk_sp(sp, h, k))

    def ada_dve(v, h):
        return (lambda: zero_dve(v, h, h), lambda k: chunk_dve(v, h, k))

    @block.sync
    def _(sp):
        sp.dma_start(x[:], t["x"].rearrange("(a p) d -> p a d", p=P)).then_inc(x_ready, 16)
        sp.dma_start(base[:], t["con1"][:, 0:NBASE]).then_inc(base_in, 16)
        sp.dma_start(con, t["con1"][:, NBASE:N1]).then_inc(con_in, 16)
        with sp.Fori(0, DEPTH) as l:
            B, n = units1(l), loads1(l)
            sp.wait_ge(x_ready, l * 48 + 16)
            rows_load(sp, l, 0)
            rows_load(sp, l, 1)
            sp.dma_start(par, t["par"][bass.ds(l, 1), :].to_broadcast([P, NR])).then_inc(par_in, 16)
            sp.dma_start(fp, t["fpar"][bass.ds(l, 1), :, :].rearrange("l p n -> p (l n)")).then_inc(par_in, 16)
            ffn_sp(sp, B[0], n[0], l, t["g1"], t["u1"], t["d1"])
            mixer1_sp(sp, B[1], l)
            sp.wait_ge(x_ready, l * 48 + 32)
            rows_load(sp, l, 2)
            ffn_sp(sp, B[2], n[2], l, t["g2"], t["u2"], t["d2"])
        sp.wait_ge(x_ready, DEPTH * 48 + 16)
        sp.dma_start(con2, t["con2"][:, :]).then_inc(con_in, 16)
        sp.dma_start(cond, t["c"][:, :]).then_inc(c_in, 16)
        bias_sp(sp, 0)
        for k in range(KT):
            chunk_sp(sp, 0, k)
        with sp.Fori(0, DEPTH) as l:
            L = l + DEPTH
            B, n = units2(l), loads2(l)
            sp.wait_ge(x_ready, L * 48 + 16)
            rows_load(sp, L, 0)
            rows_load(sp, L, 1)
            ffn_sp(sp, B[0], n[0], l, t["g3"], t["u3"], t["d3"], ada_sp(sp, l * 3 + 1))
            mixer2_sp(sp, B[1], l)
            sp.wait_ge(x_ready, L * 48 + 32)
            rows_load(sp, L, 2)
            ffn_sp(sp, B[2], n[2], l, t["g4"], t["u4"], t["d4"], ada_sp(sp, l * 3 + 3))
        sp.wait_ge(x_ready, 12 * 16 + 16)
        sp.dma_start(out.rearrange("(a p) d -> p a d", p=P), x[:]).then_inc(out_sent, 16)
        sp.wait_ge(out_sent, 16)

    @block.tensor
    def _(pe):
        pe.wait_ge(base_in, 16)
        with pe.Fori(0, DEPTH) as l:
            g = l * 3
            B = units1(l)
            pre_pe(pe, g)
            ffn_pe(pe, B[0], l * 2, g)
            pre_pe(pe, g + 1)
            mixer1_pe(pe, B[1], l, g + 1)
            pre_pe(pe, g + 2)
            ffn_pe(pe, B[2], l * 2 + 1, g + 2)
        with pe.Fori(0, DEPTH) as l:
            g, h = l * 3 + 6, l * 3
            B = units2(l)
            mod_pe(pe, h)
            pre_pe(pe, g)
            ffn_pe(pe, B[0], l * 2 + 4, g)
            mod_pe(pe, h + 1)
            pre_pe(pe, g + 1)
            mixer2_pe(pe, B[1], l, g + 1)
            mod_pe(pe, h + 2)
            pre_pe(pe, g + 2)
            ffn_pe(pe, B[2], l * 2 + 5, g + 2)

    @block.scalar
    def _(a):
        a.wait_ge(one_set, 1)
        with a.Fori(0, DEPTH) as l:
            g = l * 3
            B, n = units1(l), loads1(l)
            pre_act(a, g, True)
            ffn_act(a, B[0], n[0], l * 2)
            post_act(a, g, ffn_end(B[0]))
            pre_act(a, g + 1, True)
            mixer1_act(a, B[1], n[1], l)
            post_act(a, g + 1, (unit_done, B[2] + CREDIT))
            pre_act(a, g + 2, True)
            ffn_act(a, B[2], n[2], l * 2 + 1)
            post_act(a, g + 2, ffn_end(B[2]))
        a.wait_ge(c_in, 16)
        nc.scalar.activation(cond, cond, ACT.Silu).then_inc(cond_done, 1)
        with a.Fori(0, DEPTH) as l:
            g, h = l * 3 + 6, l * 3
            B, n = units2(l), loads2(l)
            pre_act(a, g, False)
            ffn_act(a, B[0], n[0], l * 2 + 4)
            ln_act(a, h)
            pre_act(a, g + 1, False)
            mixer2_act(a, B[1], n[1], l)
            ln_act(a, h + 1)
            pre_act(a, g + 2, False)
            ffn_act(a, B[2], n[2], l * 2 + 5)
            ln_act(a, h + 2)

    @block.vector
    def _(v):
        nc.vector.memset(zero[:], 0.0).then_inc(zero_set, 1)
        nc.vector.memset(one[:], 1.0).then_inc(one_set, 1)
        nc.vector.memset(v_m[:, :, :, 64:65], 1.0).then_inc(ones_set, 1)
        for i, (credit, n) in enumerate(((unit_lo, CREDIT), (unit_done, CREDIT), (silu_done, 1), (act_ready, 1),
                                         (proj_evac, 4), (inv_x, 1), (inv_p, 1), (ada_acc, 1))):
            nc.vector.memset(first[:, i:i + 1], 0.0).then_inc(credit, n)
        with v.Fori(0, DEPTH) as l:
            g = l * 3
            B = units1(l)
            pre_dve(v, l, 0, True)
            ffn_dve(v, B[0], l * 2)
            post_dve(v, g, 0, 0.5)
            pre_dve(v, l, 1, True)
            mixer1_dve(v, B[1], l)
            post_dve(v, g + 1, 1, 1.0)
            pre_dve(v, l, 2, True)
            ffn_dve(v, B[2], l * 2 + 1)
            post_dve(v, g + 2, 2, 0.5)
        v.wait_ge(con_in, 32)
        v.wait_ge(cond_done, 1)
        zero_dve(v, 0, None)
        for k in range(KT):
            chunk_dve(v, 0, k)
        with v.Fori(0, DEPTH) as l:
            L = l + DEPTH
            h = l * 3
            B = units2(l)
            mod_dve(v, h, 0.5)
            pre_dve(v, L, 0, False)
            ffn_dve(v, B[0], l * 2 + 4, ada_dve(v, h + 1))
            ln_dve(v, h, 0, ffn_end(B[0]), mrow[:, 2, :])
            mod_dve(v, h + 1, 1.0)
            pre_dve(v, L, 1, False)
            mixer2_dve(v, B[1], l)
            ln_dve(v, h + 1, 1, (unit_done, B[2] + CREDIT), mrow[:, 2, :])
            mod_dve(v, h + 2, 0.5)
            pre_dve(v, L, 2, False)
            ffn_dve(v, B[2], l * 2 + 5, ada_dve(v, h + 3))
            ln_dve(v, h + 2, 2, ffn_end(B[2]), mrow[:, 2, :])

    @block.gpsimd
    def _(p):
        with p.Fori(0, DEPTH) as l:
            mixer1_pool(p, l)
        with p.Fori(0, DEPTH) as l:
            mixer2_pool(p, l)

    ctx.close()


def tables():
    f32 = np.float32
    i = np.arange(P)
    k, n = i[:, None], i[None, :]
    con = np.zeros((P, N1), f32)
    con[:, C_IDENT:C_IDENT + P] = k == n
    con[:, C_TRIU:C_TRIU + P] = k <= n
    con[:, C_ONES:C_ONES + P] = 1
    con[:, C_SU:C_SU + P] = k < n
    con[:, C_BLOCK:C_BLOCK + P] = k // 64 == n // 64
    for j in range(7):
        s = 1 << j
        con[:, C_MT + j * P:C_MT + (j + 1) * P] = (k // (2 * s) == n // (2 * s)) & (n // s % 2 == 1) & (k // s % 2 == 0)
    con[:, C_NEGM:C_NEGM + P] = np.where(n > k, NEG, 0)
    key = np.arange(SEQ)[None, :]
    negd = [np.where(key // 64 > (k + tile * P) // 64, NEG, 0) for tile in range(TILES)]
    con[:, C_NEGD:C_NEGD + 384] = np.concatenate([negd[0][:, :P], negd[1]], 1)
    con[:, C_SGN:C_SGN + 12] = [1] * 8 + [-1] * 4

    def angles(freq):
        a = np.arange(SEQ, dtype=f32)[:, None] * freq[None, :]
        return np.cos(a).astype(f32), np.sin(a).astype(f32)

    def tiled(a):
        return a.reshape(TILES, P, -1).transpose(1, 0, 2)

    c, s = angles((f32(10000.0) ** (-np.arange(0, 32, 2, dtype=f32) / f32(32))).astype(f32))
    con[:, C_ROPE:C_ROPE + 32] = tiled(c).reshape(P, -1)
    con[:, C_ROPE + 32:C_ROPE + 64] = tiled(s).reshape(P, -1)

    con2 = np.zeros((P, N2), f32)
    con2[:, C2_SL:C2_SL + P] = k > n
    tq = k + np.array([0, P])[:, None, None]
    dist = tq - key[None]
    cnt = sum(((dist >= 0) & (dist % dl == 0) & (dist <= w)).astype(f32)
              for w, dl in ((128, 1), (512, 4), (2048, 16)))
    cnt = np.concatenate([cnt[0][:, :P], cnt[1]], 1)
    con2[:, C2_CNT:C2_CNT + 384] = cnt
    con2[:, C2_NEGC:C2_NEGC + 384] = np.where(cnt > 0, 0, NEG)
    lg = np.log1p(-np.exp2(-5.0 - np.arange(H)))
    d0 = key - k
    dd = np.concatenate([d0, d0[:, :P]], 1)
    ret = np.where(dd >= 0, np.exp(lg[:, None, None] * np.maximum(dd, 0)), 0) * 64.0 ** -0.5
    con2[:, C2_RET:C2_RET + H * 384] = ret.transpose(1, 0, 2).reshape(P, -1)
    rf = (1.0 / f32(10000.0) ** np.linspace(0.0, 1.0, 32, dtype=f32)).astype(f32)
    pf = (1.0 / f32(10000.0) ** (np.arange(0, 64, 2, dtype=f32) / f32(64))).astype(f32)
    kinds = [angles(rf), angles(pf)]
    rot = np.stack([np.stack([tiled(kd[z]) for kd in kinds], 2) for z in range(2)], 1)
    con2[:, C2_ROT:C2_ROT + 256] = rot.reshape(P, -1)
    return con, con2


def column_tiles(w, width=FB):
    L_, k, n = w.shape
    return np.ascontiguousarray(w.reshape(L_, k // P, P, n // width, width).transpose(0, 3, 2, 1, 4)
                                .reshape(L_, n // width, P, -1))


def row_tiles(w):
    L_, k, n = w.shape
    return np.ascontiguousarray(w.reshape(L_, k // 256, 2, P, n).transpose(0, 1, 3, 2, 4).reshape(L_, k // 256, P, -1))


def layout(i):
    con, con2 = tables()
    a = {"x": i["x"][0], "con1": con, "con2": con2}
    for n, (s, sfx) in enumerate((("ffn1", ""), ("ffn2", ""), ("ffn1", "_2"), ("ffn2", "_2"))):
        a[f"g{n + 1}"] = column_tiles(i[f"{s}_w_gate{sfx}"])
        a[f"u{n + 1}"] = column_tiles(i[f"{s}_w_up{sfx}"])
        a[f"d{n + 1}"] = row_tiles(i[f"{s}_w_down{sfx}"])
    w = i["w_in"]
    big = [0, 256, 512, 2056, 2312, 2568, 2828, 3084, 768, 1032, 1288, 1544, 1800, 3340, 3596]
    a["w_in"] = column_tiles(np.concatenate([w[:, :, c:c + 256] for c in big], 2))
    ws = np.concatenate([w[:, :, 1024:1028], w[:, :, 3852:3856], w[:, :, 1028:1032], w[:, :, 2824:2828],
                         w[:, :, 3856:3860]], 2)
    a["w_small"] = column_tiles(ws, SMALL)[:, 0]
    a["w_out"] = row_tiles(i["w_out"])
    w = i["w_in_2"]
    a["w_in_2"] = column_tiles(np.concatenate([w[:, :, c:c + 256] for c in
                                               (0, 256, 1536, 1792, 2304, 2560, 512, 768, 1024, 1280, 2048, 2816)], 2))
    a["w_out_2"] = row_tiles(i["w_out_2"])
    ada = i["w_ada_2"].reshape(DEPTH, KT, P, 3, 3 * D).transpose(0, 3, 1, 2, 4).reshape(DEPTH * 3, KT, P, 3 * D)
    a["w_ada"] = np.concatenate([ada, ada[-1:]])
    bias = i["b_ada_2"].reshape(DEPTH * 3, 3 * D)
    a["b_ada"] = np.concatenate([bias, bias[-1:]])
    a["c"] = np.ascontiguousarray(i["c_2"].reshape(KT, P).T)
    r1 = np.stack([np.stack([i[f"{s}_pre_g"], i[f"{s}_post_g"]], 1) for s in ("ffn1", "mix", "ffn2")], 1)
    r2 = np.stack([i["ln_gain_2"], i["ln_bias_2"]], 2)
    a["rows"] = np.concatenate([r1, r2]).reshape(4 * 3, 2 * D)
    zeros = np.zeros((DEPTH, H), np.float32)
    li = np.array([[0.8 - 0.6 * np.exp(-0.3 * l)] for l in range(DEPTH)])
    one_less = (1.0 - li).astype(np.float32)
    tile4 = lambda v: np.concatenate([v] * H, 1)
    a["par"] = np.concatenate([
        i["gdn_dt_bias"], i["ssd_dt_bias"], i["mlstm_f_bias"], i["gdn_a_log"], i["ssd_a_log"], zeros,
        i["mlstm_i_bias"], i["ssd_d"], i["diff_lam_q1"], i["diff_lam_k1"], i["diff_lam_q2"], i["diff_lam_k2"],
        li.astype(np.float32), one_less,
        tile4(i["gdn_norm_g"]), tile4(i["diff_norm_g"]), i["ssd_norm_g"], i["mlstm_norm_g"]], 1)
    taps = np.concatenate([i["gdn_conv_w"], i["ssd_conv_w"]], 2).reshape(DEPTH, 4, 12, P).transpose(0, 3, 2, 1)
    a["fpar"] = np.concatenate([taps.reshape(DEPTH, P, 48), i["ssd_conv_b"].reshape(DEPTH, 6, P).transpose(0, 2, 1)], 2)
    return {k: np.ascontiguousarray(v, dtype=np.float32) for k, v in a.items()}


def kernel(**inputs):
    import concourse.bacc as _bacc
    from concourse.bass_utils import run_bass_kernel_spmd as _run

    arrays = layout({k: np.asarray(v) for k, v in inputs.items()})
    nc = _bacc.Bacc("TRN2", target_bir_lowering=False, num_devices=1)
    t = {k: nc.dram_tensor(f"in_{k}", v.shape, F32, kind="ExternalInput").ap() for k, v in arrays.items()}
    out = nc.dram_tensor("out", (SEQ, D), F32, kind="ExternalOutput").ap()
    build(nc, t, out)
    r = _run(nc, [{f"in_{k}": v for k, v in arrays.items()}], core_ids=[0])
    return r.results[0]["out"].reshape(1, SEQ, D)
```

```python
from contextlib import ExitStack

import numpy as np

import concourse.bass as bass
from concourse import mybir

F32 = mybir.dt.float32
F32R = mybir.dt.float32r
BF16 = mybir.dt.bfloat16
ALU = mybir.AluOpType
ACT = mybir.ActivationFunctionType
AX = mybir.AxisListType.X

P = 128
SEQ = 256
TILES = SEQ // P
D = 1024
KT = D // P
DFF = 2816
FB = 256
NF = DFF // FB
DEPTH = 2
H = 4
NEG = -1.0e30
EPS = 1e-6
LN_EPS = 1e-5
ALPHA = (2.0 * DEPTH) ** 0.25
SLOTS = 4
UNIT = 1024
UBUF = 3
CREDIT = 8
IN1 = 16
IN2 = 12
WO = 4
SMALL = 20
SMALL_AT = 2
NADA = 9
LEVELS = 6
PAD = 3
FU = 6 * NF
ENDS1 = [2 * n + 2 - (n >= SMALL_AT) for n in range(IN1 + WO)]
ENDS2 = [2 * n + 2 for n in range(IN2 + WO)]
LU1 = 2 * FU + ENDS1[-1]
LU2 = 2 * FU + ENDS2[-1]
LOADS1 = 2 * NF + (IN1 + WO) // SLOTS
LOADS2 = 2 * NF + (IN2 + WO) // SLOTS

C_IDENT, C_TRIU, C_ONES, C_SU, C_BLOCK = 0, 128, 256, 384, 512
C_MT = 640
C_NEGM = C_MT + 7 * 128
C_NEGD = C_NEGM + 128
C_SGN = C_NEGD + 384
C_ROPE = C_SGN + 12
N1 = C_ROPE + 64
C2_SL, C2_NEGC, C2_CNT, C2_RET, C2_ROT = 0, 128, 512, 896, 896 + 4 * 384
N2 = C2_ROT + 2 * 2 * 2 * 32
NBASE = C_BLOCK

R_SPB, R_ALOG, R_IB, R_DSK, R_LAM, R_LI, R_GAIN = 0, 12, 24, 28, 32, 160, 162
NR = R_GAIN + D
F_CONV, F_CB = 0, 48
NFP = 54
ARENA = 23700


class Steps:

    def __init__(self, sem, names):
        self.sem, self.names, self.turn = sem, names.split(), 0
        assert len(set(self.names)) == len(self.names)

    def at(self, name, use):
        return use * len(self.names) + (self.names.index(name) + 1)

    def done(self, name):
        assert self.names[self.turn] == name, (self.names[self.turn], name)
        self.turn = (self.turn + 1) % len(self.names)
        return self.sem


def over(ap, shape, *dims):
    for d in dims:
        ap = ap.unsqueeze(d)
    return ap.to_broadcast(shape)


def build(nc, t, out):
    ctx = ExitStack()

    def sb(name, shape, dt=F32):
        return ctx.enter_context(nc.sbuf_tensor(name, shape, dt))

    def sem(name):
        return ctx.enter_context(nc.semaphore(name))

    def steps(name, names):
        return Steps(sem(name), names)

    ps = ctx.enter_context(nc.psum_tensor("ps", [P, 8, 512], F32))
    x = sb("x", [P, TILES, D])
    tok = sb("tok", [P, TILES, D])
    hT_hi = sb("hT_hi", [P, KT, SEQ], F32R)
    hT_lo = sb("hT_lo", [P, KT, SEQ], F32R)
    raw = sb("raw", [P, SLOTS, KT * FB])
    w_hi = sb("w_hi", [P, UBUF, UNIT], F32R)
    w_lo = sb("w_lo", [P, UBUF, UNIT], F32R)
    hidden = sb("hidden", [P, 2, 2 * SEQ])
    silu_g, act = hidden[:, 0, :], hidden[:, 1, :]
    act_hi = sb("act_hi", [P, FB // P, SEQ], F32R)
    act_lo = sb("act_lo", [P, FB // P, SEQ], F32R)
    rows = sb("rows", [P, 2, 2, D])
    arena = sb("arena", [P, ARENA])
    base = sb("base", [P, NBASE])
    zero = sb("zero", [P, 512], BF16)
    stat = sb("stat", [P, 8])
    bn = sb("bn", [P, TILES, 2, 6])
    mv = sb("mv", [P, TILES, 2])
    IDENT, TRIU = base[:, C_IDENT:C_IDENT + P], base[:, C_TRIU:C_TRIU + P]
    ONES, SU = base[:, C_ONES:C_ONES + P], base[:, C_SU:C_SU + P]
    TU = base[:, C_TRIU:C_TRIU + SEQ]

    x_ready = sem("x_ready")
    base_in = sem("base_in")
    settled = sem("settled")
    rows_in = [sem("rows_in0"), sem("rows_in1")]
    zero_set = sem("zero_set")
    raw_in = [sem(f"raw_in{i}") for i in range(SLOTS)]
    unit_hi, unit_lo = sem("unit_hi"), sem("unit_lo")
    unit_done = sem("unit_done")
    silu_done, act_ready = sem("silu_done"), sem("act_ready")
    act_split, act_rest = sem("act_split"), sem("act_rest")
    proj_evac = sem("proj_evac")
    pre_t = steps("pre_t", "trans0 trans1")
    pre_a = steps("pre_a", "ssq root hi0 hi1")
    pre_v = steps("pre_v", "mean rstd tok0 tok1 lo0 lo1")
    post_a = steps("post_a", "ssq0 ssq1 root")
    post_v = steps("post_v", "gained1 gained0 mean stats rstd")
    bn_done, ln_r = sem("bn_done"), sem("ln_r")
    mod_a = steps("mod_a", "shift scale rows")
    ln_v = steps("ln_v", "gated mixed stats var centred")
    ln_a = steps("ln_a", "root")

    def settle(eng):
        eng.sem_inc(settled, 1)

    def acc(tile):
        return ps[:, 2 * tile:2 * tile + 2, :]

    def hi_unit(a, B, j, buf, slot, loads, half, width=UNIT):
        if half == 0:
            a.wait_ge(raw_in[slot], loads * 16)
        a.wait_ge(unit_done, B + (j - UBUF + 1 + CREDIT if not isinstance(j, tuple) else j[0] + (j[1] - UBUF + 1 + CREDIT)))
        nc.scalar.activation(w_hi[:, buf, 0:width], raw[:, slot, half * UNIT:half * UNIT + width],
                             ACT.Copy).then_inc(unit_hi, 1)

    def lo_unit(v, B, j, buf, slot, half, width=UNIT):
        v.wait_ge(unit_hi, B + (j + 1 if not isinstance(j, tuple) else j[0] + (j[1] + 1)))
        nc.vector.tensor_tensor(w_lo[:, buf, 0:width], raw[:, slot, half * UNIT:half * UNIT + width],
                                w_hi[:, buf, 0:width].bitcast(F32), ALU.subtract).then_inc(unit_lo, 1)

    def unit_ready(pe, which, B, j):
        n = 1 + (CREDIT if which is unit_lo else 0)
        pe.wait_ge(which, B + (j + n if not isinstance(j, tuple) else j[0] + (j[1] + n)))

    def feature_unit(pe, B, j, buf, bank, half):
        h_, l_ = (w[:, buf, :].rearrange("p (k n) -> p k n", k=4) for w in (w_hi, w_lo))
        unit_ready(pe, unit_hi, B, j)
        for s in range(2):
            o, c = ps[:, bank, s * SEQ:(s + 1) * SEQ], slice(s * P, (s + 1) * P)
            for k in range(4):
                nc.tensor.matmul(o, h_[:, k, c], hT_hi[:, 4 * half + k, :], start=(half == s == k == 0), stop=False)
                nc.tensor.matmul(o, h_[:, k, c], hT_lo[:, 4 * half + k, :], start=False, stop=False)
        unit_ready(pe, unit_lo, B, j)
        for s in range(2):
            o, c = ps[:, bank, s * SEQ:(s + 1) * SEQ], slice(s * P, (s + 1) * P)
            for k in range(4):
                last = nc.tensor.matmul(o, l_[:, k, c], hT_hi[:, 4 * half + k, :], start=False,
                                        stop=(half == s == 1 and k == 3))
        last.then_inc(unit_done, 1)

    def token_unit(pe, B, j, buf, bank, half, width=FB, chunks=4):
        h_, l_ = (w[:, buf, 0:chunks * width].rearrange("p (k n) -> p k n", k=chunks) for w in (w_hi, w_lo))
        end = half == 1 or chunks == KT
        unit_ready(pe, unit_hi, B, j)
        for tile in range(TILES):
            o, c = ps[:, bank, tile * width:(tile + 1) * width], slice(tile * P, (tile + 1) * P)
            for k in range(chunks):
                nc.tensor.matmul(o, hT_hi[:, 4 * half + k, c], h_[:, k, :], start=(half == tile == k == 0), stop=False)
                nc.tensor.matmul(o, hT_lo[:, 4 * half + k, c], h_[:, k, :], start=False, stop=False)
        unit_ready(pe, unit_lo, B, j)
        for tile in range(TILES):
            o, c = ps[:, bank, tile * width:(tile + 1) * width], slice(tile * P, (tile + 1) * P)
            for k in range(chunks):
                last = nc.tensor.matmul(o, hT_hi[:, 4 * half + k, c], l_[:, k, :], start=False,
                                        stop=(end and tile == 1 and k == chunks - 1))
        last.then_inc(unit_done, 1)

    def row_unit(pe, B, j, buf, left, start, stop):
        unit_ready(pe, unit_hi, B, j)
        for tile in range(TILES):
            c = slice(tile * P, (tile + 1) * P)
            for i, part in enumerate(left):
                for half in range(2):
                    nc.tensor.matmul(ps[:, 2 * tile + half, :], part[:, c], w_hi[:, buf, half * 512:(half + 1) * 512],
                                     start=start and i == 0, stop=False)
        unit_ready(pe, unit_lo, B, j)
        for tile in range(TILES):
            c = slice(tile * P, (tile + 1) * P)
            for half in range(2):
                last = nc.tensor.matmul(ps[:, 2 * tile + half, :], left[0][:, c],
                                        w_lo[:, buf, half * 512:(half + 1) * 512], start=False, stop=stop)
        last.then_inc(unit_done, 1)

    def ffn_sp(sp, B, loads, l, wg, wu, wd, between=None):
        def load(slot, w, i):
            sp.dma_start(raw[:, slot, :], w[bass.ds(l, 1), i, :, :].rearrange("l i p n -> p (l i n)")).then_inc(
                raw_in[slot], 16)

        sp.wait_ge(unit_lo, B + (CREDIT - 6))
        load(0, wg, slice(0, 1))
        sp.wait_ge(unit_lo, B + (CREDIT - 4))
        load(1, wu, slice(0, 1))
        if between:
            between[0]()
        for first, end in ((1, 9), (9, NF)):
            with sp.Fori(first, end) as i:
                sp.wait_ge(unit_lo, B + i * 6 + (CREDIT - 4))
                load(0, wg, bass.ds(i, 1))
                sp.wait_ge(unit_lo, B + i * 6 + (CREDIT - 2))
                load(1, wu, bass.ds(i, 1))
                load(2, wd, bass.ds(i - 1, 1))
                if between and first == 1:
                    between[1](i - 1)
        sp.wait_ge(unit_lo, B + (6 * NF - 2 + CREDIT))
        load(2, wd, slice(NF - 1, NF))

    def ffn_pe(pe, B, f, g):
        pe.wait_ge(zero_set, 1)
        for b in range(4):
            nc.tensor.matmul(ps[:, b, :], zero[:, 0:P], zero[:], start=True, stop=False)
        pre_done(pe, g)
        left = lambda kk: (act_hi[:, kk, :], act_lo[:, kk, :])

        def gate_up(n, j):
            pe.wait_ge(silu_done, n + 1)
            feature_unit(pe, B, j(0), (j(0) if not isinstance(j(0), tuple) else j(0)[1]) % UBUF, 4, 0)
            feature_unit(pe, B, j(1), (j(1) if not isinstance(j(1), tuple) else j(1)[1]) % UBUF, 4, 1)
            pe.wait_ge(act_ready, n + 1)
            feature_unit(pe, B, j(2), (j(2) if not isinstance(j(2), tuple) else j(2)[1]) % UBUF, 5, 0)
            feature_unit(pe, B, j(3), (j(3) if not isinstance(j(3), tuple) else j(3)[1]) % UBUF, 5, 1)

        gate_up(f * NF, lambda r: r)
        with pe.Fori(1, NF) as i:
            gate_up(f * NF + i, lambda r: (i * 6, r - 2))
            pe.wait_ge(act_split, f * NF + i)
            pe.wait_ge(act_rest, f * NF + i)
            row_unit(pe, B, (i * 6, 2), 2, left(0), False, False)
            row_unit(pe, B, (i * 6, 3), 0, left(1), False, False)
        pe.wait_ge(act_split, f * NF + NF)
        pe.wait_ge(act_rest, f * NF + NF)
        row_unit(pe, B, 6 * NF - 2, (6 * NF - 2) % UBUF, left(0), False, False)
        row_unit(pe, B, 6 * NF - 1, (6 * NF - 1) % UBUF, left(1), False, True)

    def ffn_act(a, B, loads, f):
        def split_act(n, done):
            a.wait_ge(act_ready, n + 2)
            a.wait_ge(unit_done, done)
            nc.scalar.activation(act_hi[:].rearrange("p s t -> p (s t)"), act, ACT.Copy).then_inc(act_split, 1)

        def silu(n, done):
            a.wait_ge(unit_done, done)
            a.wait_ge(act_ready, n + 1)
            nc.scalar.activation(silu_g, ps[:, 4, :], ACT.Silu).then_inc(silu_done, 1)

        for r in range(4):
            hi_unit(a, B, r if r >= UBUF - 1 else UBUF - 1, r % UBUF, r // 2, loads + 1, r % 2)
        silu(f * NF, B + (2 + CREDIT))
        with a.Fori(1, NF) as i:
            for r in range(2):
                hi_unit(a, B, (i * 6, r - 2), (r - 2) % UBUF, 0, loads + i + 1, r)
            split_act(f * NF + i - 1, B + i * 6 + (CREDIT - 2))
            for r in range(2, 4):
                hi_unit(a, B, (i * 6, r - 2), (r - 2) % UBUF, 1, loads + i + 1, r - 2)
            silu(f * NF + i, B + i * 6 + CREDIT)
            for r in range(4, 6):
                hi_unit(a, B, (i * 6, r - 2), (r - 2) % UBUF, 2, loads + i, r - 4)
        split_act(f * NF + (NF - 1), B + (NF * 6 - 2 + CREDIT))
        for r in range(2):
            hi_unit(a, B, 6 * NF - 2 + r, (6 * NF - 2 + r) % UBUF, 2, loads + NF, r)

    def ffn_dve(v, B, f, between=None):
        def rest_act(n):
            v.wait_ge(act_split, n + 1)
            nc.vector.tensor_tensor(act_lo[:].rearrange("p s t -> p (s t)"), act,
                                    act_hi[:].rearrange("p s t -> p (s t)").bitcast(F32), ALU.subtract).then_inc(act_rest, 1)

        def product(n, done):
            v.wait_ge(silu_done, n + 2)
            v.wait_ge(unit_done, done)
            nc.vector.tensor_tensor(act, silu_g, ps[:, 5, :], ALU.mult).then_inc(act_ready, 1)

        for r in range(4):
            lo_unit(v, B, r, r % UBUF, r // 2, r % 2)
        product(f * NF, B + (4 + CREDIT))
        for first, end in ((1, 9), (9, NF)):
            with v.Fori(first, end) as i:
                for r in range(2):
                    lo_unit(v, B, (i * 6, r - 2), (r - 2) % UBUF, 0, r)
                rest_act(f * NF + i - 1)
                for r in range(2, 6):
                    lo_unit(v, B, (i * 6, r - 2), (r - 2) % UBUF, r // 2, r % 2)
                if between and first == 1:
                    between(i - 1)
                v.wait_ge(act_rest, f * NF + i)
                product(f * NF + i, B + i * 6 + (2 + CREDIT))
        rest_act(f * NF + (NF - 1))
        for r in range(2):
            lo_unit(v, B, 6 * NF - 2 + r, (6 * NF - 2 + r) % UBUF, 2, r)

    def ffn_end(B):
        return unit_done, B + (6 * NF + CREDIT)

    def transposes_pe(tile):
        for k in range(KT):
            c = (k % 2) * SEQ + tile * P
            last = nc.tensor.transpose(ps[:, 4 + k // 2, c:c + P], tok[:, tile, k * P:(k + 1) * P], IDENT)
        return last

    def hT_half(w, i):
        return w[:, 4 * i:4 * i + 4, :].rearrange("p (b k) t -> p b (k t)", b=2)

    def split_hi(a, i, A):
        nc.scalar.activation(hT_half(hT_hi, i), ps[:, 4 + 2 * i:6 + 2 * i, :], ACT.Copy).then_inc(A.done(f"hi{i}"), 1)

    def split_lo(v, i, A, use, V):
        v.wait_ge(A.sem, A.at(f"hi{i}", use))
        nc.vector.tensor_tensor(hT_half(hT_lo, i), ps[:, 4 + 2 * i:6 + 2 * i, :], hT_half(hT_hi, i).bitcast(F32),
                                ALU.subtract).then_inc(V.done(f"lo{i}"), 1)

    def pre_done(pe, g):
        pe.wait_ge(pre_v.sem, pre_v.at("lo1", g))

    def tile_bank(tile):
        return ps[:, 4 + 2 * tile:6 + 2 * tile, :].rearrange("p b (k t) -> p b k t", k=4)

    def tile_of(w, tile):
        return w[:, :, tile * P:(tile + 1) * P].rearrange("p (b k) t -> p b k t", b=2)

    def pre_pe(pe, g):
        for tile in range(TILES):
            pe.wait_ge(pre_v.sem, pre_v.at(f"tok{tile}", g))
            for k in range(KT):
                last = nc.tensor.transpose(tile_bank(tile)[:, k // 4, k % 4, :], tok[:, tile, k * P:(k + 1) * P], IDENT)
            last.then_inc(pre_t.done(f"trans{tile}"), 1)

    def pre_act(a, g, normed):
        a.wait_ge(x_ready, g * 16 + 16)
        if normed:
            for tile in range(TILES):
                last = nc.scalar.activation(tok[:, tile, :], x[:, tile, :], ACT.Square,
                                            accum_out=stat[:, tile:tile + 1])
            last.then_inc(pre_a.done("ssq"), 1)
            a.wait_ge(pre_v.sem, pre_v.at("mean", g))
            nc.scalar.activation(stat[:, 2:4], stat[:, 2:4], ACT.Sqrt).then_inc(pre_a.done("root"), 1)
        else:
            nc.scalar.activation(stat[:, 6:7], x[:, 0, 0:1], ACT.Copy).then_inc(pre_a.done("ssq"), 1)
            nc.scalar.activation(stat[:, 7:8], x[:, 0, 0:1], ACT.Copy).then_inc(pre_a.done("root"), 1)
        for tile in range(TILES):
            a.wait_ge(pre_t.sem, pre_t.at(f"trans{tile}", g))
            nc.scalar.activation(tile_of(hT_hi, tile), tile_bank(tile), ACT.Copy).then_inc(pre_a.done(f"hi{tile}"), 1)

    def rows_wait(v, L, pos):
        if pos == 1:
            v.wait_ge(rows_in[1], L * 16 + 16)
        else:
            v.wait_ge(rows_in[0], L * 32 + (16 if pos == 0 else 32))

    def pre_dve(v, L, pos, normed):
        g = L * 3 + pos
        rows_wait(v, L, pos)
        v.wait_ge(x_ready, g * 16 + 16)
        if normed:
            v.wait_ge(pre_a.sem, pre_a.at("ssq", g))
            nc.vector.tensor_scalar(stat[:, 2:4], stat[:, 0:2], 1.0 / D, EPS, ALU.mult,
                                    ALU.add).then_inc(pre_v.done("mean"), 1)
            v.wait_ge(pre_a.sem, pre_a.at("root", g))
            nc.vector.reciprocal(stat[:, 4:6], stat[:, 2:4]).then_inc(pre_v.done("rstd"), 1)
            v.wait_ge(pre_v.sem, pre_v.at("rstd", g))
            for tile in range(TILES):
                nc.vector.scalar_tensor_tensor(tok[:, tile, :], x[:, tile, :], stat[:, 4 + tile:5 + tile],
                                               rows[:, pos % 2, 0, :], ALU.mult, ALU.mult).then_inc(
                                                   pre_v.done(f"tok{tile}"), 1)
        else:
            shift, scale1 = mrow[:, 0, :], mrow[:, 1, :]
            v.wait_ge(mod_a.sem, mod_a.at("rows", g - 6))
            nc.vector.tensor_tensor(tok[:], x[:], over(scale1, [P, TILES, D], 1),
                                    ALU.mult).then_inc(pre_v.done("mean"), 1)
            nc.vector.memset(stat[:, 5:6], 0.0).then_inc(pre_v.done("rstd"), 1)
            v.wait_ge(pre_v.sem, pre_v.at("mean", g))
            for tile in range(TILES):
                nc.vector.tensor_tensor(tok[:, tile, :], tok[:, tile, :], shift, ALU.add).then_inc(
                    pre_v.done(f"tok{tile}"), 1)
        for tile in range(TILES):
            v.wait_ge(pre_a.sem, pre_a.at(f"hi{tile}", g))
            nc.vector.tensor_tensor(tile_of(hT_lo, tile), tile_bank(tile), tile_of(hT_hi, tile).bitcast(F32),
                                    ALU.subtract).then_inc(pre_v.done(f"lo{tile}"), 1)

    def post_act(a, g, ready):
        a.wait_ge(*ready)
        for tile in range(TILES):
            if tile == 1:
                a.wait_ge(post_v.sem, post_v.at("gained1", g))
                a.wait_ge(post_a.sem, post_a.at("ssq0", g))
            nc.scalar.activation(hidden[:], acc(tile), ACT.Square,
                                 accum_out=stat[:, tile:tile + 1]).then_inc(post_a.done(f"ssq{tile}"), 1)
        a.wait_ge(post_v.sem, post_v.at("mean", g))
        nc.scalar.activation(stat[:, 2:4], stat[:, 2:4], ACT.Sqrt).then_inc(post_a.done("root"), 1)

    def post_dve(v, g, pos, weight, ready):
        v.wait_ge(*ready)
        for tile in (1, 0):
            if tile == 0:
                v.wait_ge(post_a.sem, post_a.at("ssq0", g))
            nc.vector.tensor_tensor(tok[:, tile, :].rearrange("p (b n) -> p b n", b=2), acc(tile),
                                    rows[:, pos % 2, 1, :].rearrange("p (b n) -> p b n", b=2),
                                    ALU.mult).then_inc(post_v.done(f"gained{tile}"), 1)
        v.wait_ge(post_a.sem, post_a.at("ssq1", g))
        nc.vector.tensor_scalar(stat[:, 2:4], stat[:, 0:2], 1.0 / D, EPS, ALU.mult,
                                ALU.add).then_inc(post_v.done("mean"), 1)
        v.wait_ge(post_a.sem, post_a.at("root", g))
        nc.vector.reciprocal(stat[:, 4:6], stat[:, 2:4]).then_inc(post_v.done("stats"), 1)
        v.wait_ge(post_v.sem, post_v.at("stats", g))
        nc.vector.tensor_scalar(stat[:, 6:8], stat[:, 4:6], weight, None, ALU.mult).then_inc(post_v.done("rstd"), 1)
        v.wait_ge(post_v.sem, post_v.at("rstd", g))
        for tile in range(TILES):
            last = nc.vector.scalar_tensor_tensor(x[:, tile, :], tok[:, tile, :], stat[:, 6 + tile:7 + tile],
                                                  x[:, tile, :], ALU.mult, ALU.add)
        last.then_inc(x_ready, 16)

    def ln_act(a, h):
        a.wait_ge(ln_v.sem, ln_v.at("var", h))
        nc.scalar.activation(stat[:, 2:4], stat[:, 0:2], ACT.Sqrt).then_inc(ln_a.done("root"), 1)

    def ln_dve(v, h, pos, ready, gate):
        v.wait_ge(*ready)
        for tile in range(TILES):
            last = nc.vector.tensor_tensor(tok[:, tile, :].rearrange("p (b n) -> p b n", b=2), acc(tile),
                                           gate.rearrange("p (b n) -> p b n", b=2), ALU.mult)
        last.then_inc(ln_v.done("gated"), 1)
        v.wait_ge(ln_v.sem, ln_v.at("gated", h))
        nc.vector.scalar_tensor_tensor(tok[:], x[:], ALPHA, tok[:], ALU.mult, ALU.add).then_inc(ln_v.done("mixed"), 1)
        v.wait_ge(ln_v.sem, ln_v.at("mixed", h))
        for tile in range(TILES):
            for half in range(2):
                last = nc.vector.bn_stats(bn[:, tile, half, :], tok[:, tile, half * 512:(half + 1) * 512])
        last.then_inc(ln_v.done("stats"), 1)
        v.wait_ge(ln_v.sem, ln_v.at("stats", h))
        settle(v)
        for tile in range(TILES):
            last = nc.vector.bn_aggr(mv[:, tile, :], bn[:, tile, :, :].rearrange("p a b -> p (a b)"))
        last.then_inc(bn_done, 1)
        v.wait_ge(bn_done, h + 1)
        nc.vector.tensor_scalar(stat[:, 0:2], mv[:, :, 1], LN_EPS, None, ALU.add).then_inc(ln_v.done("var"), 1)
        for tile in range(TILES):
            last = nc.vector.scalar_tensor_tensor(tok[:, tile, :], tok[:, tile, :], mv[:, tile, 0:1],
                                                  rows[:, pos % 2, 0, :], ALU.subtract, ALU.mult)
        last.then_inc(ln_v.done("centred"), 1)
        v.wait_ge(ln_a.sem, ln_a.at("root", h))
        nc.vector.reciprocal(stat[:, 4:6], stat[:, 2:4]).then_inc(ln_r, 1)
        v.wait_ge(ln_r, h + 1)
        for tile in range(TILES):
            last = nc.vector.scalar_tensor_tensor(x[:, tile, :], tok[:, tile, :], stat[:, 4 + tile:5 + tile],
                                                  rows[:, pos % 2, 1, :], ALU.mult, ALU.add)
        last.then_inc(x_ready, 16)


    def mixer_load(sp, B, ends, n, src, width=KT * FB):
        sp.wait_ge(unit_lo, B + (CREDIT + (ends[n - SLOTS] if n >= SLOTS else (-4, -2, 0, 0)[n])))
        sp.dma_start(raw[:, n % SLOTS, 0:width], src).then_inc(raw_in[n % SLOTS], 16)

    def mixer_units(ends, n):
        first = ends[n - 1] if n else 0
        return [(j, j - first) for j in range(first, ends[n])]

    def mixer_hi(a, B, ends, n, loads):
        for j, half in mixer_units(ends, n):
            width = UNIT if ends[n] - (ends[n - 1] if n else 0) == 2 else KT * SMALL
            hi_unit(a, B, max(j, UBUF - 1), j % UBUF, n % SLOTS, loads[n % SLOTS] + (n // SLOTS + 1), half, width)

    def mixer_lo(v, B, ends, n):
        for j, half in mixer_units(ends, n):
            width = UNIT if ends[n] - (ends[n - 1] if n else 0) == 2 else KT * SMALL
            lo_unit(v, B, j, j % UBUF, n % SLOTS, half, width)

    def out_product(pe, B, ends, first):
        for n in range(first, first + WO):
            for j, half in mixer_units(ends, n):
                k = 2 * (n - first) + half
                row_unit(pe, B, j, j % UBUF, (hT_hi[:, k, :], hT_lo[:, k, :]), k == 0, k == KT - 1)

    def scores_T(bank, kT_s, qT_t, h):
        nc.tensor.matmul(ps[:, bank, 0:SEQ], kT_s[:, 0:P], qT_t[:, 0:SEQ], start=True, stop=True)
        return nc.tensor.matmul(ps[:, bank, SEQ:SEQ + P], kT_s[:, P:SEQ], qT_t[:, P:SEQ], start=True, stop=True)

    def weighted_values(out0, out1, pT, v0, v1):
        nc.tensor.matmul(out0, pT[:, 0:P], v0, start=True, stop=True)
        nc.tensor.matmul(out1, pT[:, P:SEQ], v0, start=True, stop=False)
        return nc.tensor.matmul(out1, pT[:, SEQ:SEQ + P], v1, start=False, stop=True)

    def row_of(out, col):
        return nc.tensor.matmul(out, col.to_broadcast([P, P]), IDENT, start=True, stop=True)

    def prefix_row(bank, off, col0, col1):
        nc.tensor.matmul(ps[:, bank, off:off + SEQ], col0.to_broadcast([P, P]), TU, start=True, stop=False)
        return nc.tensor.matmul(ps[:, bank, off + P:off + SEQ], col1.to_broadcast([P, P]), TRIU, start=False, stop=True)

    def diag(buf):
        return buf[:].rearrange("p h (b n) -> p h b n", b=3)[:, :, 0:3:2, :]


    class Arena:

        def __init__(self):
            self.at = 0

        def take(self, *shape):
            n = int(np.prod(shape))
            piece = arena[:, self.at:self.at + n]
            self.at += n
            assert self.at <= ARENA, (self.at, ARENA)
            if len(shape) == 2:
                piece = piece.rearrange("p (a b) -> p a b", a=shape[0])
            if len(shape) == 3:
                piece = piece.rearrange("p (a b c) -> p a b c", a=shape[0], b=shape[1])
            if len(shape) == 4:
                piece = piece.rearrange("p (a b c d) -> p a b c d", a=shape[0], b=shape[1], c=shape[2])
            return piece

    m = Arena()
    con = m.take(N1 - NBASE)
    par = m.take(NR)
    fp = m.take(NFP)
    u = m.take(12, PAD + SEQ)
    cv = m.take(12, SEQ)
    qk_m = m.take(4, SEQ)
    small = m.take(TILES, SMALL)
    gate_g = m.take(TILES, SEQ)
    rope_in = m.take(TILES, 512)
    v_d = m.take(TILES, SEQ)
    v_m = m.take(TILES, H, 65)
    sp_x, sp_e, sp_u, sp_l, sp_c = (m.take(TILES, 12) for _ in range(5))
    ld = m.take(TILES, 12)
    ea = m.take(12)
    gc = m.take(TILES, 12)
    beta = m.take(TILES, H)
    dt = m.take(TILES, H)
    acol, mcol, negm, em, den = (m.take(TILES, H) for _ in range(5))
    md = m.take(H, TILES)
    mfull = m.take(H)
    coef = m.take(TILES, 8)
    rmax = m.take(TILES, 8)
    lamb = m.take(8)
    lamp = m.take(2, 32)
    ms = m.take(TILES, 16)
    rn = m.take(TILES, 8)
    gsum = m.take(TILES, 2)
    uflat = u.rearrange("p a b -> p (a b)")
    dT2 = uflat[:, 0:1536].rearrange("p (a b) -> p a b", a=H)
    xs = uflat[:, 1536:2048].rearrange("p (a b) -> p a b", a=TILES)
    xdt = uflat[:, 2048:2560].rearrange("p (a b) -> p a b", a=TILES)
    o_m = uflat[:, 2560:3072].rearrange("p (a b) -> p a b", a=TILES)
    kb = uflat[:, 0:512].rearrange("p (a b) -> p a b", a=2)
    vb, uu, z_s = cv[:, 0:2, :], cv[:, 2:4, :], cv[:, 6:8, :]
    sq_m = cv.rearrange("p a b -> p (a b)")[:, 8 * SEQ:12 * SEQ].rearrange("p (a b) -> p a b", a=8)
    dT = m.take(H, 384)
    lT = m.take(H, 384)
    X = m.take(2, 2, 4 * P)
    xflat = X.rearrange("p g z n -> p (g z n)")
    rnx = xflat[:, 0:1024].rearrange("p (t h d) -> p t h d", t=TILES, h=8)
    bk = xflat[:, 1024:1536].rearrange("p (t h d) -> p t h d", t=TILES, h=H)
    r2 = m.take(SEQ)
    pm = hidden[:].rearrange("p a (i n) -> p (a i) n", i=4)
    pm_sq = hidden[:].rearrange("p a (i n) -> p (a i) n", i=2)
    dS = m.take(8, 384)
    pD = m.take(H, 384)
    pT = pD
    qkr = dS.rearrange("p a b -> p (a b)")[:, 0:TILES * 512].rearrange("p (a b) -> p a b", a=TILES)
    dqk = rope_in.rearrange("p a (i n) -> p (a i) n", i=2)
    rt = pD.rearrange("p a b -> p (a b)")[:, 0:512].rearrange("p (a b) -> p a b", a=2)
    sq = dS.rearrange("p a b -> p (a b)")[:, 0:TILES * D].rearrange("p (a b) -> p a b", a=TILES)
    mix = tok

    def K(c, n=P):
        return con[:, c - NBASE:c - NBASE + n]

    BLOCKS, NEGM, NEGD = K(C_BLOCK), K(C_NEGM), K(C_NEGD, 384)
    COS = K(C_ROPE, 32).rearrange("p (t n) -> p t n", t=2)
    SIN = K(C_ROPE + 32, 32).rearrange("p (t n) -> p t n", t=2)
    con_in, par_in = sem("con_in"), sem("par_in")
    pads = sem("pads")
    ones_set = sem("ones_set")
    inv_p, inv_c, inv_r, inv_x = (sem(f"inv_{c}") for c in "pcrx")

    T1 = steps("mix1_t", "sums rows_n kk_even kk qk_even qk x0 rows_s xt_s cb o_s rope_t map00 map01 map02 map03 map10 map11 "
                         "map12 map13 rows_a vt rows_m trans_d qk_m_even qk_m o_d o_m u1 l21 u2 o_g trans1 trans0")
    A1 = steps("mix1_a", "silu_qk sq sp_e ea eb sp_l gc root dec_g silu_v xi silu_s dec_s xs dqk exp_d0 exp_d1 lam dec_m em pT "
                         "o_d den u1 u2 sq1 root1 o_g sq0 root0 hi1 hi0")
    V1 = steps("mix1_v", "cq0 cq1 cq2 conv_qk sp_in sp_sgn sp_abs sp_u sp_um sp_em sp_ru sp_corr sp_max sp_l sp dt ld eb1 beta "
                         "rs dec_g rn rnx bk cv0 cv1 cv2 conv_v kb qn lT mt1 xT aT cs0 cs1 cs2 conv_s dec_s xdt ra1 rb1 rc1 "
                         "rd1 re1 rf1 w_s ra2 rb2 rc2 rd2 re2 rf2 skip o_s ai acol mask_d0 max_d0 nmax_d0 mask_d1 max_d1 "
                         "nmax_d1 tmp_m md mf m0 m1 mt negm lam0 lam1 vb rec_d lam2 coef scale_d add_d dec_m gl gg w_m denm "
                         "rden o_m r2 pre_gate sums1 pair0 pair1 mean1 rstd1 norm1 gain1 sums0 mean0 rstd0 norm0 gain0 lo1 lo0")
    G1 = steps("mix1_g", "dec_g dec_s dec_m")

    def x_of(i, transposed):
        return X[:, i // 4, transposed, (i % 4) * P:(i % 4 + 1) * P]

    def blocks(buf):
        return buf.rearrange("p h (b n) -> p h b n", b=3)

    def bank_blocks(first):
        return ps[:, first:first + 3, :].rearrange("p b (h n) -> p h b n", h=H)

    def mixer1_sp(sp, B, l):
        at = 0
        for n in range(IN1 + WO):
            if n == SMALL_AT:
                mixer_load(sp, B, ENDS1, n, t["w_small"][bass.ds(l, 1), :, :].rearrange("l p n -> p (l n)"), KT * SMALL)
            elif n < IN1:
                mixer_load(sp, B, ENDS1, n, t["w_in"][bass.ds(l, 1), at:at + 1, :, :].rearrange("l i p n -> p (l i n)"))
                at += 1
            else:
                mixer_load(sp, B, ENDS1, n,
                           t["w_out"][bass.ds(l, 1), n - IN1:n - IN1 + 1, :, :].rearrange("l i p n -> p (l i n)"))

    def mixer1_pe(pe, B, l, g):
        def after(S, name):
            pe.wait_ge(S.sem, S.at(name, l))

        def project(n):
            pe.wait_ge(proj_evac, l * IN1 + n + 3)
            for j, half in mixer_units(ENDS1, n):
                if n == SMALL_AT:
                    token_unit(pe, B, j, j % UBUF, 6 + n % 2, 0, SMALL, KT)
                elif n < 7 or n in (10, 11):
                    feature_unit(pe, B, j, j % UBUF, 6 + n % 2, half)
                else:
                    token_unit(pe, B, j, j % UBUF, 6 + n % 2, half)

        def head(h):
            return slice(64 * (h % 2), 64 * (h % 2) + 64)

        def head_scores(name, first, kT, qT):
            for odd in range(2):
                if odd:
                    after(T1, name + "_even")
                for h in (odd, odd + 2):
                    k_, q_ = kT[head(h), h // 2, :], qT[head(h), h // 2, :]
                    for b, (s_, t_) in enumerate(((0, 0), (0, 1), (1, 1))):
                        last = nc.tensor.matmul(ps[:, first + b, h * P:(h + 1) * P], k_[:, s_ * P:(s_ + 1) * P],
                                                q_[:, t_ * P:(t_ + 1) * P], start=True, stop=True)
                last.then_inc(T1.done(name + ("" if odd else "_even")), 1)

        def product(i):
            if i >= 2:
                pe.wait_ge(inv_x, l * 2 * LEVELS + (i - 1))
            if i:
                pe.wait_ge(inv_c, l * 2 * LEVELS + i)
            for q in range(4):
                m_ = 4 * (i % 2) + q
                c = 2 * P * (m_ % 2)
                last = nc.tensor.matmul(ps[:, 0, q * P:(q + 1) * P], lT[:, m_ // 2, c:c + P], x_of(m_, 0),
                                        start=True, stop=True)
            last.then_inc(inv_p, 1)

        def update(i):
            pe.wait_ge(inv_c, l * 2 * LEVELS + (i + 1))
            if i:
                pe.wait_ge(inv_x, l * 2 * LEVELS + i)
            for q in range(4):
                m_ = 4 * (i % 2) + q
                if i < 2 * LEVELS - 2:
                    nc.tensor.matmul(ps[:, 1, q * P:(q + 1) * P], x_of(m_, 1), pm[:, m_, :], start=True, stop=True)
                last = nc.tensor.matmul(ps[:, 2, q * P:(q + 1) * P], pm[:, m_, :], x_of(m_, 1), start=True, stop=True)
            last.then_inc(inv_r, 1)

        pe.wait_ge(ones_set, 1)
        pre_done(pe, g)
        for n in range(5):
            project(n)
        after(V1, "ld")
        nc.tensor.matmul(ps[:, 5, 0:12], TRIU, ld[:, 0, :], start=True, stop=True)
        nc.tensor.matmul(ps[:, 5, 12:24], ONES, ld[:, 0, :], start=True, stop=False)
        nc.tensor.matmul(ps[:, 5, 12:24], TRIU, ld[:, 1, :], start=False, stop=True)
        for h in range(H):
            prefix_row(3 + h // 2, (h % 2) * SEQ, ld[:, 0, h:h + 1], ld[:, 1, h:h + 1])
        after(A1, "sq")
        for c in range(4):
            for tile in range(TILES):
                o = 32 + tile * 8 + 2 * c
                last = nc.tensor.matmul(ps[:, 5, o:o + 2], pm_sq[:, c, tile * P:(tile + 1) * P], BLOCKS[:, 0:P:64],
                                        start=True, stop=True)
        last.then_inc(T1.done("sums"), 1)
        project(5)
        after(V1, "bk")
        for i, (cols, first) in enumerate(((rnx, 0), (rnx, 4), (bk, 0))):
            for c in range(2):
                for tile in range(TILES):
                    both = cols[:, tile, first + 2 * c:first + 2 * c + 2, :].rearrange("p h d -> p (h d)")
                    o = c * SEQ + tile * P
                    last = nc.tensor.matmul(ps[:, i, o:o + P], both, IDENT, start=True, stop=True)
        last.then_inc(T1.done("rows_n"), 1)
        project(6)
        after(V1, "qn")
        after(V1, "dec_g")
        after(A1, "gc")
        head_scores("kk", 3, cv[:, 2:4, :], kb)
        head_scores("qk", 0, cv[:, 2:4, :], cv[:, 0:2, :])
        project(7)
        after(V1, "xT")
        for i in range(8):
            last = nc.tensor.transpose(ps[:, 3 + i // 4, (i % 4) * P:(i % 4 + 1) * P], x_of(i, 1), IDENT)
        last.then_inc(T1.done("x0"), 1)
        project(8)
        after(A1, "xi")
        after(V1, "aT")
        product(0)
        project(9)
        update(0)
        product(1)
        for h in range(H):
            last = prefix_row(3 + h // 2, (h % 2) * SEQ, ld[:, 0, 4 + h:5 + h], ld[:, 1, 4 + h:5 + h])
        last.then_inc(T1.done("rows_s"), 1)
        project(10)
        update(1)
        product(2)
        after(A1, "silu_s")
        for c in range(2):
            for tile in range(TILES):
                o = tile * SEQ + c * P
                last = nc.tensor.transpose(ps[:, 5, o:o + P], cv[:, 6 + c, tile * P:(tile + 1) * P], IDENT)
        last.then_inc(T1.done("xt_s"), 1)
        project(11)
        update(2)
        product(3)
        after(V1, "dec_s")
        for grp in range(2):
            last = scores_T(3 + grp, cv[:, 8 + grp, :], cv[:, 10 + grp, :], grp)
        last.then_inc(T1.done("cb"), 1)
        project(12)
        update(3)
        product(4)
        after(V1, "w_s")
        after(V1, "xdt")
        for h in range(H):
            c = slice(h * 64, (h + 1) * 64)
            last = weighted_values(ps[:, 5, h * 64:(h + 1) * 64], ps[:, 5, SEQ + h * 64:SEQ + (h + 1) * 64],
                                   dT2[:, h, :], xdt[:, 0, c], xdt[:, 1, c])
        last.then_inc(T1.done("o_s"), 1)
        after(V1, "rf2")
        for c in range(4):
            for tile in range(TILES):
                o = (c % 2) * SEQ + tile * P
                last = nc.tensor.transpose(ps[:, 3 + c // 2, o:o + P], qkr[:, tile, c * P:(c + 1) * P], IDENT)
        last.then_inc(T1.done("rope_t"), 1)
        project(13)
        update(4)
        product(5)
        after(A1, "dqk")
        after(V1, "o_s")

        def maps(c):
            for j in range(4):
                part = slice(32 * j, 32 * j + 32)
                if j:
                    after(T1, f"map{c}{j - 1}")
                nc.tensor.matmul(ps[:, 3, j * P:(j + 1) * P], dqk[part, c, 0:P], dqk[part, 2 + c, 0:P],
                                 start=True, stop=True, tile_position=(32 * j, 0))
                last = nc.tensor.matmul(ps[:, 4 + j // 2, (j % 2) * SEQ:(j % 2 + 1) * SEQ], dqk[part, c, P:SEQ],
                                        dqk[part, 2 + c, :], start=True, stop=True, tile_position=(32 * j, 0))
                last.then_inc(T1.done(f"map{c}{j}"), 1)

        maps(0)
        project(14)
        update(5)
        product(6)
        after(V1, "mask_d0")
        maps(1)
        project(15)
        update(6)
        product(7)
        after(V1, "mask_d1")
        after(V1, "acol")
        for h in range(H):
            for tile in range(TILES):
                c = (h % 2) * SEQ + tile * P
                last = row_of(ps[:, 3 + h // 2, c:c + P], acol[:, tile, h:h + 1])
        last.then_inc(T1.done("rows_a"), 1)
        after(A1, "silu_v")
        for c in range(2):
            for tile in range(TILES):
                o = tile * SEQ + c * P
                last = nc.tensor.transpose(ps[:, 5, o:o + P], cv[:, 4 + c, tile * P:(tile + 1) * P], IDENT)
        last.then_inc(T1.done("vt"), 1)
        update(7)
        product(8)
        pe.wait_ge(proj_evac, l * IN1 + IN1 + 4)
        after(V1, "m1")
        for h in range(H):
            for tile in range(TILES):
                c = (h % 2) * SEQ + tile * P
                last = row_of(ps[:, 6 + h // 2, c:c + P], mcol[:, tile, h:h + 1])
        last.then_inc(T1.done("rows_m"), 1)
        update(8)
        product(9)
        after(V1, "add_d")
        after(V1, "vb")
        for h in range(H):
            for b in range(3):
                last = nc.tensor.transpose(ps[:, 3 + b, h * P:(h + 1) * P], pD[:, h, b * P:(b + 1) * P], IDENT)
        last.then_inc(T1.done("trans_d"), 1)
        update(9)
        product(10)
        after(A1, "pT")
        after(V1, "dec_m")
        head_scores("qk_m", 3, qk_m[:, 2:4, :], qk_m[:, 0:2, :])
        update(10)
        product(11)
        for h in range(H):
            c = slice(h * 64, (h + 1) * 64)
            last = weighted_values(ps[:, 6, h * 64:(h + 1) * 64], ps[:, 6, SEQ + h * 64:SEQ + (h + 1) * 64],
                                   pT[:, h, :], v_d[:, 0, c], v_d[:, 1, c])
        last.then_inc(T1.done("o_d"), 1)
        update(11)
        after(V1, "w_m")
        for h in range(H):
            last = weighted_values(ps[:, 3, h * 65:(h + 1) * 65], ps[:, 4, h * 65:(h + 1) * 65], dT2[:, h, :],
                                   v_m[:, 0, h, :], v_m[:, 1, h, :])
        last.then_inc(T1.done("o_m"), 1)
        pe.wait_ge(inv_x, l * 2 * LEVELS + 2 * LEVELS)
        for h in range(H):
            last = nc.tensor.matmul(ps[:, 1, h * 64:(h + 1) * 64], x_of(2 * h, 1), vb[:, 0, h * 64:(h + 1) * 64],
                                    start=True, stop=True)
        last.then_inc(T1.done("u1"), 1)
        after(A1, "u1")
        for h in range(H):
            last = nc.tensor.matmul(ps[:, 2, h * 64:(h + 1) * 64], lT[:, h, P:SEQ], uu[:, 0, h * 64:(h + 1) * 64],
                                    start=True, stop=True)
        last.then_inc(T1.done("l21"), 1)
        after(V1, "r2")
        for h in range(H):
            last = nc.tensor.matmul(ps[:, 0, h * 64:(h + 1) * 64], x_of(2 * h + 1, 1), r2[:, h * 64:(h + 1) * 64],
                                    start=True, stop=True)
        last.then_inc(T1.done("u2"), 1)
        after(A1, "u2")
        for h in range(H):
            c = slice(h * 64, (h + 1) * 64)
            last = weighted_values(ps[:, 1, h * 64:(h + 1) * 64], ps[:, 1, SEQ + h * 64:SEQ + (h + 1) * 64],
                                   dT[:, h, :], uu[:, 0, c], uu[:, 1, c])
        last.then_inc(T1.done("o_g"), 1)

        for i in (1, 0):
            after(V1, f"gain{i}")
            for k in range(4 * i, 4 * i + 4):
                for tile in range(TILES):
                    c = (k % 2) * SEQ + tile * P
                    last = nc.tensor.transpose(ps[:, 4 + k // 2, c:c + P], tok[:, tile, k * P:(k + 1) * P], IDENT)
            last.then_inc(T1.done(f"trans{i}"), 1)
        after(V1, "lo0")
        out_product(pe, B, ENDS1, IN1)

    def mixer1_act(a, B, loads, l):
        def after(S, name):
            a.wait_ge(S.sem, S.at(name, l))

        def two(bank):
            return ps[:, bank, :].rearrange("p (a b) -> p a b", a=2)

        feature_homes = {0: u[:, 0:2, PAD:], 1: u[:, 2:4, PAD:], 3: u[:, 4:6, PAD:], 4: u[:, 6:8, PAD:],
                         5: u[:, 8:10, PAD:], 6: u[:, 10:12, PAD:], 10: qk_m[:, 0:2, :], 11: qk_m[:, 2:4, :]}
        token_homes = {7: rope_in[:, :, 0:SEQ], 8: rope_in[:, :, SEQ:512], 9: v_d, 13: o_m, 14: z_s, 15: gate_g}

        def projection(n):
            mixer_hi(a, B, ENDS1, n + 1, loads)
            a.wait_ge(unit_done, B + (ENDS1[n] + CREDIT))
            bank = 6 + n % 2
            if n == SMALL_AT:
                last = nc.scalar.activation(small, ps[:, bank, 0:2 * SMALL].rearrange("p (a b) -> p a b", a=2), ACT.Copy)
            elif n in feature_homes:
                last = nc.scalar.activation(feature_homes[n], two(bank), ACT.Copy,
                                            scale=64.0 ** -0.5 if n == 11 else 1.0)
            elif n == 12:
                for tile in range(TILES):
                    last = nc.scalar.activation(v_m[:, tile, :, 0:64],
                                                two(bank)[:, tile, :].rearrange("p (h d) -> p h d", h=H), ACT.Copy)
            else:
                func = ACT.Sigmoid if n == 13 else ACT.Silu if n > 13 else ACT.Copy
                last = nc.scalar.activation(token_homes[n], two(bank), func)
            last.then_inc(proj_evac, 1)

        def softmax_exp(c):
            after(V1, f"nmax_d{c}")
            for j in range(4 * c, 4 * c + 4):
                for tile, part in enumerate((slice(0, P), slice(P, 384))):
                    last = nc.scalar.activation(dS[:, j, part], dS[:, j, part], ACT.Exp, scale=32.0 ** -0.5,
                                                bias=rmax[:, tile, j:j + 1], accum_out=coef[:, tile, j:j + 1])
            last.then_inc(A1.done(f"exp_d{c}"), 1)

        mixer_hi(a, B, ENDS1, 0, loads)
        for n in range(4):
            projection(n)
        after(V1, "conv_qk")
        nc.scalar.activation(cv[:, 0:4, :], cv[:, 0:4, :], ACT.Silu).then_inc(A1.done("silu_qk"), 1)
        after(A1, "silu_qk")
        nc.scalar.activation(pm_sq, cv[:, 0:4, :], ACT.Square).then_inc(A1.done("sq"), 1)
        a.wait_ge(par_in, l * 32 + 32)
        after(V1, "sp_abs")
        nc.scalar.activation(sp_e, sp_c, ACT.Exp, scale=-1.0).then_inc(A1.done("sp_e"), 1)
        nc.scalar.activation(ea, par[:, R_ALOG:R_ALOG + 12], ACT.Exp).then_inc(A1.done("ea"), 1)
        nc.scalar.activation(beta, small[:, :, 0:H], ACT.Exp, scale=-1.0).then_inc(A1.done("eb"), 1)
        after(V1, "sp_u")
        nc.scalar.activation(sp_l, sp_u, ACT.Ln).then_inc(A1.done("sp_l"), 1)
        projection(4)
        after(T1, "sums")
        nc.scalar.activation(gc, ps[:, 5, 0:24].rearrange("p (a b) -> p a b", a=2), ACT.Copy).then_inc(A1.done("gc"), 1)
        after(V1, "rs")
        nc.scalar.activation(rn, rn, ACT.Sqrt).then_inc(A1.done("root"), 1)
        projection(5)
        after(V1, "dec_g")
        nc.scalar.activation(dT, dT, ACT.Exp).then_inc(A1.done("dec_g"), 1)
        projection(6)
        after(V1, "conv_v")
        nc.scalar.activation(cv[:, 4:6, :], cv[:, 4:6, :], ACT.Silu).then_inc(A1.done("silu_v"), 1)
        projection(7)
        after(T1, "x0")
        nc.scalar.activation(X[:, :, 0, :], ps[:, 3:5, :], ACT.Copy).then_inc(A1.done("xi"), 1)
        projection(8)
        projection(9)
        after(V1, "conv_s")
        for c in range(6):
            last = nc.scalar.activation(cv[:, 6 + c, :], cv[:, 6 + c, :], ACT.Silu, bias=fp[:, F_CB + c:F_CB + c + 1])
        last.then_inc(A1.done("silu_s"), 1)
        projection(10)
        after(V1, "dec_s")
        nc.scalar.activation(dT2, dT2, ACT.Exp).then_inc(A1.done("dec_s"), 1)
        after(T1, "xt_s")
        nc.scalar.activation(xs, two(5), ACT.Copy).then_inc(A1.done("xs"), 1)
        projection(11)
        projection(12)
        after(T1, "rope_t")
        nc.scalar.activation(dqk.rearrange("p (a i) n -> p a (i n)", a=2), ps[:, 3:5, :], ACT.Copy).then_inc(A1.done("dqk"), 1)
        projection(13)
        projection(14)
        softmax_exp(0)
        projection(15)
        softmax_exp(1)
        after(V1, "lam1")
        nc.scalar.activation(lamb[:, 2:4], lamb[:, 0:2], ACT.Exp).then_inc(A1.done("lam"), 1)
        after(V1, "dec_m")
        nc.scalar.activation(dT2, dT2, ACT.Exp, scale=-1.0).then_inc(A1.done("dec_m"), 1)
        after(V1, "negm")
        nc.scalar.activation(em, negm, ACT.Exp).then_inc(A1.done("em"), 1)
        after(T1, "trans_d")
        nc.scalar.activation(blocks(pT), bank_blocks(3), ACT.Copy).then_inc(A1.done("pT"), 1)
        after(T1, "o_d")
        nc.scalar.activation(mix[:, :, SEQ:512], two(6), ACT.Copy).then_inc(A1.done("o_d"), 1)
        after(T1, "o_m")
        nc.scalar.activation(den, ps[:, 3:5, 0:H * 65].rearrange("p a (h d) -> p a h d", h=H)[:, :, :, 64],
                             ACT.Abs).then_inc(A1.done("den"), 1)
        after(T1, "u1")
        nc.scalar.activation(uu[:, 0, :], ps[:, 1, 0:SEQ], ACT.Copy).then_inc(A1.done("u1"), 1)
        after(T1, "u2")
        nc.scalar.activation(uu[:, 1, :], ps[:, 0, 0:SEQ], ACT.Copy).then_inc(A1.done("u2"), 1)
        after(V1, "pre_gate")
        nc.scalar.activation(sq[:, :, SEQ:D], mix[:, :, SEQ:D], ACT.Square).then_inc(A1.done("sq1"), 1)
        after(V1, "mean1")
        nc.scalar.activation(ms[:, :, 4:16], ms[:, :, 4:16], ACT.Sqrt).then_inc(A1.done("root1"), 1)
        after(T1, "o_g")
        nc.scalar.activation(mix[:, :, 0:SEQ], two(1), ACT.Copy).then_inc(A1.done("o_g"), 1)
        after(A1, "o_g")
        nc.scalar.activation(sq[:, :, 0:SEQ], mix[:, :, 0:SEQ], ACT.Square).then_inc(A1.done("sq0"), 1)
        after(V1, "mean0")
        nc.scalar.activation(ms[:, :, 0:4], ms[:, :, 0:4], ACT.Sqrt).then_inc(A1.done("root0"), 1)
        for i in (1, 0):
            after(T1, f"trans{i}")
            split_hi(a, i, A1)
        for n in range(IN1 + 1, IN1 + WO):
            mixer_hi(a, B, ENDS1, n, loads)

    def rotate(V, after, n, src, dst, cos, sin, half):
        na, nb, nc_, nd, ne, nf = (f"r{c}{n}" for c in "abcdef")
        x1, x2, y1, y2 = src[0], src[1], dst[0], dst[1]
        nc.vector.tensor_tensor(y1, x1, cos, ALU.mult).then_inc(V.done(na), 1)
        nc.vector.tensor_tensor(half, x2, sin, ALU.mult).then_inc(V.done(nb), 1)
        after(V, nb)
        nc.vector.tensor_tensor(y1, y1, half, ALU.subtract).then_inc(V.done(nc_), 1)
        nc.vector.tensor_tensor(y2, x1, sin, ALU.mult).then_inc(V.done(nd), 1)
        after(V, nc_)
        nc.vector.tensor_tensor(half, x2, cos, ALU.mult).then_inc(V.done(ne), 1)
        after(V, ne)
        nc.vector.tensor_tensor(y2, y2, half, ALU.add).then_inc(V.done(nf), 1)

    def decays(rows_bank, first, buf, col, op0, op1):
        for h in range(H):
            r = ps[:, rows_bank + h // 2, (h % 2) * SEQ:(h % 2) * SEQ + SEQ]
            nc.vector.tensor_scalar(buf[:, h, 0:SEQ], r, col[:, 0, first + h:first + h + 1], 0.0, op0, op1)
            last = nc.vector.tensor_scalar(buf[:, h, SEQ:384], r[:, P:SEQ], col[:, 1, first + h:first + h + 1], 0.0,
                                           op0, op1)
        return last

    def convolve(v, after, chunks, names, between=None):
        for c in chunks:
            last = nc.vector.tensor_scalar(cv[:, c, :], u[:, c, 0:SEQ], fp[:, F_CONV + 4 * c:F_CONV + 4 * c + 1],
                                           None, ALU.mult)
        last.then_inc(V1.done(names[0]), 1)
        for k in range(1, 4):
            if between:
                between(k)
            after(V1, names[k - 1])
            for c in chunks:
                last = nc.vector.scalar_tensor_tensor(cv[:, c, :], u[:, c, k:k + SEQ],
                                                      fp[:, F_CONV + 4 * c + k:F_CONV + 4 * c + k + 1], cv[:, c, :],
                                                      ALU.mult, ALU.add)
            last.then_inc(V1.done(names[k]), 1)

    def mixer1_dve(v, B, l):
        def after(S, name):
            v.wait_ge(S.sem, S.at(name, l))

        def lo(n):
            mixer_lo(v, B, ENDS1, n)

        def masked(i):
            v.wait_ge(inv_p, l * 2 * LEVELS + (i + 1))
            group, lev = slice(4 * (i % 2), 4 * (i % 2) + 4), K(C_MT + (i // 2 + 1) * P)
            nc.vector.tensor_tensor(pm[:, group, :], ps[:, 0, :].rearrange("p (i n) -> p i n", i=4),
                                    over(lev, [P, 4, P], 1), ALU.mult).then_inc(inv_c, 1)

        def rotate_d(tile):
            s_ = rope_in[:, tile, :].rearrange("p (h z n) -> p h z n", h=16, z=2)
            d_ = qkr[:, tile, :].rearrange("p (h z n) -> p h z n", h=16, z=2)
            rotate(V1, after, tile + 1, (s_[:, :, 0, :], s_[:, :, 1, :]), (d_[:, :, 0, :], d_[:, :, 1, :]),
                   over(COS[:, tile, :], [P, 16, 16], 1), over(SIN[:, tile, :], [P, 16, 16], 1),
                   rt[:, tile, :].rearrange("p (h n) -> p h n", h=16))

        def subtracted(i):
            v.wait_ge(inv_r, l * 2 * LEVELS + (i + 1))
            z = 0 if i < 2 * LEVELS - 2 else 1
            nc.vector.tensor_tensor(X[:, i % 2, z:2, :], X[:, i % 2, z:2, :], ps[:, 1 + z:3, :],
                                    ALU.subtract).then_inc(inv_x, 1)

        v.wait_ge(par_in, l * 32 + 32)
        v.wait_ge(con_in, 16)
        nc.vector.memset(u[:, :, 0:PAD], 0.0).then_inc(pads, 1)
        for n in range(3):
            lo(n)
        v.wait_ge(pads, l + 1)
        v.wait_ge(proj_evac, l * IN1 + 2 + 4)
        convolve(v, after, range(0, 4), ("cq0", "cq1", "cq2", "conv_qk"), lambda k: lo(3) if k == 1 else None)
        v.wait_ge(proj_evac, l * IN1 + SMALL_AT + 1 + 4)
        nc.vector.tensor_tensor(sp_x, small[:, :, 8:SMALL], over(par[:, R_SPB:R_SPB + 12], [P, TILES, 12], 1),
                                ALU.add).then_inc(V1.done("sp_in"), 1)
        after(V1, "sp_in")
        nc.vector.tensor_tensor(sp_x, sp_x, over(K(C_SGN, 12), [P, TILES, 12], 1), ALU.mult).then_inc(V1.done("sp_sgn"), 1)
        after(V1, "sp_sgn")
        nc.vector.scalar_tensor_tensor(sp_c, sp_x, -1.0, sp_x, ALU.mult, ALU.max).then_inc(V1.done("sp_abs"), 1)
        lo(4)
        after(A1, "sp_e")
        nc.vector.tensor_scalar(sp_u, sp_e, 1.0, None, ALU.add).then_inc(V1.done("sp_u"), 1)
        after(V1, "sp_u")
        nc.vector.tensor_scalar(sp_c, sp_u, -1.0, None, ALU.add).then_inc(V1.done("sp_um"), 1)
        after(V1, "sp_um")
        nc.vector.tensor_tensor(sp_e, sp_e, sp_c, ALU.subtract).then_inc(V1.done("sp_em"), 1)
        after(V1, "sp_em")
        nc.vector.reciprocal(sp_c, sp_u).then_inc(V1.done("sp_ru"), 1)
        after(V1, "sp_ru")
        nc.vector.tensor_tensor(sp_e, sp_e, sp_c, ALU.mult).then_inc(V1.done("sp_corr"), 1)
        nc.vector.tensor_scalar(sp_x, sp_x, 0.0, None, ALU.max).then_inc(V1.done("sp_max"), 1)
        after(A1, "sp_l")
        after(V1, "sp_max")
        nc.vector.tensor_tensor(sp_x, sp_x, sp_l, ALU.add).then_inc(V1.done("sp_l"), 1)
        after(V1, "sp_l")
        nc.vector.tensor_tensor(sp_x, sp_x, sp_e, ALU.add).then_inc(V1.done("sp"), 1)
        after(V1, "sp")
        nc.vector.tensor_copy(dt, sp_x[:, :, 4:8]).then_inc(V1.done("dt"), 1)
        after(A1, "ea")
        nc.vector.scalar_tensor_tensor(ld, sp_x, -1.0, over(ea, [P, TILES, 12], 1), ALU.mult,
                                       ALU.mult).then_inc(V1.done("ld"), 1)
        after(A1, "eb")
        nc.vector.tensor_scalar(negm, beta, 1.0, None, ALU.add).then_inc(V1.done("eb1"), 1)
        after(V1, "eb1")
        nc.vector.reciprocal(beta, negm).then_inc(V1.done("beta"), 1)
        lo(5)
        after(T1, "sums")
        after(A1, "gc")
        nc.vector.tensor_scalar(rn.rearrange("p a b -> p (a b)"), ps[:, 5, 32:48], EPS, None,
                                ALU.add).then_inc(V1.done("rs"), 1)
        decays(3, 0, dT, gc, ALU.subtract, ALU.min).then_inc(V1.done("dec_g"), 1)
        after(A1, "root")
        nc.vector.reciprocal(rn, rn).then_inc(V1.done("rn"), 1)
        after(V1, "rn")
        nc.vector.tensor_copy(rnx, over(rn, [P, TILES, 8, 64], 3)).then_inc(V1.done("rnx"), 1)
        after(V1, "rnx")
        nc.vector.tensor_tensor(bk, rnx[:, :, 4:8, :], over(beta, [P, TILES, H, 64], 3), ALU.mult).then_inc(V1.done("bk"), 1)
        lo(6)
        v.wait_ge(proj_evac, l * IN1 + 4 + 4)
        convolve(v, after, range(4, 6), ("cv0", "cv1", "cv2", "conv_v"))
        after(T1, "rows_n")
        pair = lambda bank: ps[:, bank, :].rearrange("p (c n) -> p c n", c=2)
        nc.vector.tensor_tensor(kb, cv[:, 2:4, :], pair(2), ALU.mult).then_inc(V1.done("kb"), 1)
        after(V1, "kb")
        nc.vector.tensor_tensor(cv[:, 2:4, :], cv[:, 2:4, :], pair(1), ALU.mult)
        nc.vector.scalar_tensor_tensor(cv[:, 0:2, :], cv[:, 0:2, :], 64.0 ** -0.5, pair(0), ALU.mult,
                                       ALU.mult).then_inc(V1.done("qn"), 1)
        lo(7)
        after(G1, "dec_g")
        after(T1, "kk")
        nc.vector.tensor_tensor(blocks(lT), bank_blocks(3), blocks(dT), ALU.mult).then_inc(V1.done("lT"), 1)
        after(V1, "lT")
        for g_ in range(2):
            last = nc.vector.tensor_tensor(X[:, g_, 1, :].rearrange("p (h b n) -> p h b n", h=2, b=2),
                                           diag(lT)[:, 2 * g_:2 * g_ + 2, :, :], over(K(C_MT), [P, 2, 2, P], 1, 1), ALU.mult)
        last.then_inc(V1.done("mt1"), 1)
        after(V1, "mt1")
        for g_ in range(2):
            x4 = X[:, g_, 1, :].rearrange("p (i n) -> p i n", i=4)
            last = nc.vector.scalar_tensor_tensor(x4, x4, -1.0, over(IDENT, [P, 4, P], 1), ALU.mult, ALU.add)
        last.then_inc(V1.done("xT"), 1)
        lo(8)
        after(T1, "qk")
        nc.vector.tensor_tensor(blocks(dT), bank_blocks(0), blocks(dT), ALU.mult).then_inc(V1.done("aT"), 1)
        v.wait_ge(proj_evac, l * IN1 + 7 + 4)
        convolve(v, after, range(6, 12), ("cs0", "cs1", "cs2", "conv_s"),
                 lambda k: lo(9) if k == 1 else lo(10) if k == 3 else None)
        masked(0)
        subtracted(0)
        masked(1)
        lo(11)
        after(T1, "rows_s")
        decays(3, 4, dT2, gc, ALU.subtract, ALU.min).then_inc(V1.done("dec_s"), 1)
        subtracted(1)
        masked(2)
        lo(12)
        after(A1, "xs")
        nc.vector.tensor_tensor(xdt.rearrange("p a (h d) -> p (a h) d", h=H),
                                xs.rearrange("p a (h d) -> p (a h) d", h=H),
                                over(dt.rearrange("p a h -> p (a h)"), [P, 8, 64], 2), ALU.mult).then_inc(V1.done("xdt"), 1)
        v.wait_ge(proj_evac, l * IN1 + 9 + 4)
        rotate_d(0)
        subtracted(2)
        masked(3)
        lo(13)
        after(G1, "dec_s")
        after(T1, "cb")
        for grp in range(2):
            last = nc.vector.tensor_tensor(dT2[:, 2 * grp:2 * grp + 2, :], over(ps[:, 3 + grp, 0:384], [P, 2, 384], 1),
                                           dT2[:, 2 * grp:2 * grp + 2, :], ALU.mult)
        last.then_inc(V1.done("w_s"), 1)
        rotate_d(1)
        subtracted(3)
        masked(4)
        lo(14)
        nc.vector.tensor_tensor(xs.rearrange("p a (h d) -> p a h d", h=H), xs.rearrange("p a (h d) -> p a h d", h=H),
                                over(par[:, R_DSK:R_DSK + H], [P, TILES, H, 64], 1, 3), ALU.mult).then_inc(V1.done("skip"), 1)
        after(V1, "skip")
        after(T1, "o_s")
        nc.vector.tensor_tensor(mix[:, :, 512:768], xs, ps[:, 5, :].rearrange("p (a b) -> p a b", a=2),
                                ALU.add).then_inc(V1.done("o_s"), 1)
        nc.vector.tensor_tensor(negm, small[:, :, 4:8], over(par[:, R_IB:R_IB + H], [P, TILES, H], 1),
                                ALU.add).then_inc(V1.done("ai"), 1)
        after(V1, "ai")
        nc.vector.tensor_tensor(acol, negm, gc[:, :, 8:12], ALU.subtract).then_inc(V1.done("acol"), 1)
        subtracted(4)
        masked(5)
        lo(15)

        def masked_maps(c):
            after(T1, f"map{c}3")
            mine = slice(4 * c, 4 * c + 4)
            nc.vector.tensor_tensor(dS[:, mine, 0:P], ps[:, 3, :].rearrange("p (j n) -> p j n", j=4),
                                    over(NEGD[:, 0:P], [P, 4, P], 1), ALU.add)
            nc.vector.tensor_tensor(dS[:, mine, P:384].rearrange("p (b j) n -> p b j n", b=2),
                                    ps[:, 4:6, :].rearrange("p b (j n) -> p b j n", j=2),
                                    over(NEGD[:, P:384], [P, 2, 2, SEQ], 1, 1), ALU.add).then_inc(V1.done(f"mask_d{c}"), 1)
            after(V1, f"mask_d{c}")
            for tile, part in enumerate((slice(0, P), slice(P, 384))):
                last = nc.vector.reduce_max(rmax[:, tile, mine], dS[:, mine, part], AX)
            last.then_inc(V1.done(f"max_d{c}"), 1)
            after(V1, f"max_d{c}")
            nc.vector.tensor_scalar(rmax[:, :, mine], rmax[:, :, mine], -(32.0 ** -0.5), None,
                                    ALU.mult).then_inc(V1.done(f"nmax_d{c}"), 1)

        masked_maps(0)
        subtracted(5)
        masked(6)
        lo(16)
        masked_maps(1)
        subtracted(6)
        masked(7)
        after(T1, "rows_a")
        for h in range(H):
            last = nc.vector.tensor_tensor(sq_m[:, 2 * h:2 * h + 2, :],
                                           ps[:, 3 + h // 2, (h % 2) * SEQ:(h % 2 + 1) * SEQ].rearrange("p (a n) -> p a n", a=2),
                                           over(NEGM, [P, 2, P], 1), ALU.add)
        last.then_inc(V1.done("tmp_m"), 1)
        after(V1, "tmp_m")
        nc.vector.reduce_max(md.rearrange("p h t -> p (h t)"), sq_m, AX).then_inc(V1.done("md"), 1)
        nc.vector.reduce_max(mfull.rearrange("p (a b) -> p a b", a=2),
                             ps[:, 3:5, :].rearrange("p a (b n) -> p a b n", b=2)[:, :, :, 0:P],
                             AX).then_inc(V1.done("mf"), 1)
        subtracted(7)
        masked(8)
        after(V1, "mf")
        nc.vector.tensor_scalar(mcol[:, 0, :], md[:, :, 0], 0.0, None, ALU.max).then_inc(V1.done("m0"), 1)
        nc.vector.scalar_tensor_tensor(mcol[:, 1, :], md[:, :, 1], 0.0, mfull, ALU.max, ALU.max).then_inc(V1.done("m1"), 1)
        after(V1, "m1")
        nc.vector.tensor_tensor(negm, mcol, gc[:, :, 8:12], ALU.add).then_inc(V1.done("mt"), 1)
        after(V1, "mt")
        nc.vector.tensor_scalar(negm, negm, -1.0, 85.0, ALU.mult, ALU.min).then_inc(V1.done("negm"), 1)
        lam4 = par[:, R_LAM:R_LAM + 128].rearrange("p (a b n) -> p a b n", a=2, b=2)
        nc.vector.tensor_tensor(lamp, lam4[:, :, 0, :], lam4[:, :, 1, :], ALU.mult).then_inc(V1.done("lam0"), 1)
        after(V1, "lam0")
        nc.vector.reduce_sum(lamb[:, 0:2], lamp, AX).then_inc(V1.done("lam1"), 1)
        after(T1, "vt")
        nc.vector.tensor_tensor(vb.rearrange("p a (h d) -> p (a h) d", h=H),
                                ps[:, 5, :].rearrange("p (i d) -> p i d", d=64),
                                over(beta.rearrange("p a h -> p (a h)"), [P, 8, 64], 2), ALU.mult).then_inc(V1.done("vb"), 1)
        subtracted(8)
        masked(9)
        after(A1, "exp_d0")
        after(A1, "exp_d1")
        nc.vector.reciprocal(coef, coef).then_inc(V1.done("rec_d"), 1)
        after(A1, "lam")
        nc.vector.scalar_tensor_tensor(lamb[:, 4:5], lamb[:, 3:4], par[:, R_LI:R_LI + 1], lamb[:, 2:3], ALU.subtract,
                                       ALU.subtract).then_inc(V1.done("lam2"), 1)
        after(V1, "lam2")
        second = coef.rearrange("p a (j c) -> p (a j) c", c=2)[:, :, 1]
        nc.vector.tensor_scalar(second, second, lamb[:, 4:5], None, ALU.mult).then_inc(V1.done("coef"), 1)
        after(V1, "coef")
        dS2 = dS.rearrange("p (h c) n -> p h c n", c=2)
        for tile, part in enumerate((slice(0, P), slice(P, 384))):
            w = part.stop - part.start
            last = nc.vector.tensor_tensor(pD[:, :, part], dS2[:, :, 0, part], over(coef[:, tile, 0:8:2], [P, H, w], 2),
                                           ALU.mult)
            last = nc.vector.tensor_tensor(dS2[:, :, 1, part], dS2[:, :, 1, part], over(coef[:, tile, 1:8:2], [P, H, w], 2),
                                           ALU.mult)
        last.then_inc(V1.done("scale_d"), 1)
        after(V1, "scale_d")
        nc.vector.tensor_tensor(pD, pD, dS2[:, :, 1, :], ALU.add).then_inc(V1.done("add_d"), 1)
        after(T1, "rows_m")
        decays(6, 0, dT2, acol, ALU.subtract, ALU.max).then_inc(V1.done("dec_m"), 1)
        subtracted(9)
        masked(10)
        gain = par[:, R_GAIN:R_GAIN + D]
        nc.vector.tensor_scalar(gain[:, SEQ:512], gain[:, SEQ:512], par[:, R_LI + 1:R_LI + 2], None,
                                ALU.mult).then_inc(V1.done("gl"), 1)
        v.wait_ge(proj_evac, l * IN1 + IN1 + 4)
        nc.vector.tensor_tensor(gate_g, gate_g, over(gain[:, 0:SEQ], [P, TILES, SEQ], 1),
                                ALU.mult).then_inc(V1.done("gg"), 1)
        subtracted(10)
        masked(11)
        after(G1, "dec_m")
        after(T1, "qk_m")
        nc.vector.tensor_tensor(blocks(dT2), bank_blocks(3), blocks(dT2), ALU.mult).then_inc(V1.done("w_m"), 1)
        subtracted(11)
        after(T1, "o_m")
        o65 = ps[:, 3:5, 0:H * 65].rearrange("p a (h d) -> p a h d", h=H)
        after(A1, "den")
        nc.vector.tensor_tensor(den, den, em, ALU.max).then_inc(V1.done("denm"), 1)
        after(V1, "denm")
        nc.vector.reciprocal(den, den).then_inc(V1.done("rden"), 1)
        after(V1, "rden")
        nc.vector.tensor_tensor(mix[:, :, 768:D].rearrange("p a (h d) -> p a h d", h=H), o65[:, :, :, 0:64],
                                over(den, [P, TILES, H, 64], 3), ALU.mult).then_inc(V1.done("o_m"), 1)
        after(T1, "l21")
        nc.vector.tensor_tensor(r2, vb[:, 1, :], ps[:, 2, 0:SEQ], ALU.subtract).then_inc(V1.done("r2"), 1)
        after(V1, "o_m")
        nc.vector.tensor_tensor(mix[:, :, 512:768], mix[:, :, 512:768], z_s, ALU.mult)
        nc.vector.tensor_tensor(mix[:, :, 768:D], mix[:, :, 768:D], o_m, ALU.mult).then_inc(V1.done("pre_gate"), 1)

        def norms(i, c, gains):
            h_ = slice(c.start // 64, c.stop // 64)
            n_ = h_.stop - h_.start
            after(A1, f"sq{i}")
            for tile in range(TILES):
                last = nc.vector.reduce_sum(ms[:, tile, h_], sq[:, tile, c].rearrange("p (h d) -> p h d", d=64), AX)
            last.then_inc(V1.done(f"sums{i}"), 1)
            after(V1, f"sums{i}")
            if i:
                pairs = ms[:, :, 8:12].rearrange("p a (g c) -> p a g c", c=2)
                nc.vector.tensor_tensor(gsum, pairs[:, :, :, 0], pairs[:, :, :, 1], ALU.add).then_inc(V1.done("pair0"), 1)
                after(V1, "pair0")
                nc.vector.tensor_scalar(pairs, over(gsum, [P, TILES, 2, 2], 3), 0.5, None, ALU.mult).then_inc(V1.done("pair1"), 1)
                after(V1, "pair1")
            nc.vector.tensor_scalar(ms[:, :, h_], ms[:, :, h_], 1.0 / 64, EPS, ALU.mult, ALU.add).then_inc(V1.done(f"mean{i}"), 1)
            after(A1, f"root{i}")
            nc.vector.reciprocal(ms[:, :, h_], ms[:, :, h_]).then_inc(V1.done(f"rstd{i}"), 1)
            after(V1, f"rstd{i}")
            mine = mix[:, :, c].rearrange("p a (h d) -> p a h d", d=64)
            nc.vector.tensor_tensor(mine, mine, over(ms[:, :, h_], [P, TILES, n_, 64], 3),
                                    ALU.mult).then_inc(V1.done(f"norm{i}"), 1)
            after(V1, f"norm{i}")
            nc.vector.tensor_tensor(mix[:, :, c], mix[:, :, c], gains, ALU.mult).then_inc(V1.done(f"gain{i}"), 1)

        norms(1, slice(SEQ, D), over(gain[:, SEQ:D], [P, TILES, D - SEQ], 1))
        norms(0, slice(0, SEQ), gate_g)
        for i in (1, 0):
            split_lo(v, i, A1, l, V1)
        for n in range(IN1 + 1, IN1 + WO):
            lo(n)

    def mixer1_pool(p, l):
        def after(S, name):
            p.wait_ge(S.sem, S.at(name, l))

        def mask(buf):
            d_ = diag(buf)
            return nc.gpsimd.tensor_tensor(d_, d_, over(TRIU, [P, H, 2, P], 1, 1), ALU.mult)

        for name, buf in (("dec_g", dT), ("dec_s", dT2), ("dec_m", dT2)):
            after(A1, name)
            mask(buf).then_inc(G1.done(name), 1)

    m2 = Arena()
    con2 = m2.take(N2)
    m2.at = max(m2.at, N1 - NBASE + NR + NFP)
    ada = m2.take(3 * D)
    ada_w = m2.take(3 * D)
    mrow = m2.take(3, D)
    mark2 = m2.at
    rot_in = m2.take(TILES, 4 * SEQ)
    rot = m2.take(TILES, 4 * SEQ)
    half = m2.take(TILES, 512)
    m2.at = mark2
    b1, b2, b3 = (m2.take(H, 384) for _ in range(3))
    m2.at = mark2 + 5 * 1024
    rqk = m2.take(8, SEQ)
    b4 = rqk.rearrange("p a b -> p (a b)")[:, 0:H * 384].rearrange("p (a b) -> p a b", a=H)
    sqk = m2.take(4, SEQ)
    v_r, g_r = m2.take(TILES, 512), m2.take(TILES, 512)
    v_2, v_b = m2.take(TILES, SEQ), m2.take(TILES, SEQ)
    bn8 = m2.take(8, 6)
    mv8 = m2.take(8, 2)
    rstd8 = m2.take(8)
    max2 = m2.take(TILES, H)
    sum2 = m2.take(TILES, H)
    SL, NEGC, CNT = con2[:, C2_SL:C2_SL + P], con2[:, C2_NEGC:C2_NEGC + 384], con2[:, C2_CNT:C2_CNT + 384]
    RET = con2[:, C2_RET:C2_RET + H * 384].rearrange("p (h n) -> p h n", h=H)
    ROT = con2[:, C2_ROT:C2_ROT + 256].rearrange("p (z t k n) -> p z t k n", z=2, t=2, k=2)
    c_in, cond_done = sem("c_in"), sem("cond_done")
    ada_acc = sem("ada_acc")
    ada_in = sem("ada_in")
    ada_zero, bias_in, mod_t = sem("ada_zero"), sem("bias_in"), sem("mod_t")
    T2 = steps("mix2_t", "qkt sc_r zt sc_d o_r between trans_d o_d o_b trans")
    A2 = steps("mix2_a", "rqk abs_b e_b l_b exp_d root_r pT exp_b o_b hi0 hi1")
    V2 = steps("mix2_v", "ra1 rb1 rc1 rd1 re1 rf1 ra2 rb2 rc2 rd2 re2 rf2 w_r mask_d max_d sub_d stats_r aggr_r var_r sp_b t_b "
                         "rstd_r norm_r cnt_d sum_d rec_d exp_arg gated o_d lo0 lo1")
    G2 = steps("mix2_g", "keep a")

    def bias_sp(sp, n, h):
        sp.wait_ge(ada_zero, n + 1)
        settle(sp)
        sp.dma_start(ada[0:1, :], t["b_ada"][h, :]).then_inc(bias_in, 16)

    def chunk_sp(sp, n, h, k):
        sp.wait_ge(ada_acc, n * KT + k + 1)
        settle(sp)
        sp.dma_start(ada_w, t["w_ada"][h, bass.ds(k, 1) if not isinstance(k, int) else slice(k, k + 1), :, :]
                     .rearrange("h k p n -> p (h k n)")).then_inc(ada_in, 16)

    def zero_pool(p):
        settle(p)
        nc.gpsimd.memset(ada, 0.0).then_inc(ada_zero, 1)

    def chunk_dve(v, n, k):
        v.wait_ge(bias_in, n * 16 + 16)
        c = cond[:, k:k + 1] if isinstance(k, int) else cond[:, bass.ds(k, 1)]
        v.wait_ge(ada_in, n * (KT * 16) + k * 16 + 16)
        v.wait_ge(ada_acc, n * KT + k + 1)
        nc.vector.scalar_tensor_tensor(ada, ada_w, c, ada, ALU.mult, ALU.add).then_inc(ada_acc, 1)

    def mod_act(a, h, half):
        a.wait_ge(mod_t, h + 1)
        two = "p (b n) -> p b n"
        nc.scalar.activation(mrow[:, 0, :].rearrange(two, b=2), ps[:, 0:2, :], ACT.Copy).then_inc(mod_a.done("shift"), 1)
        nc.scalar.activation(mrow[:, 1, :].rearrange(two, b=2), ps[:, 2:4, :], ACT.Identity,
                             bias=one[:]).then_inc(mod_a.done("scale"), 1)
        nc.scalar.activation(mrow[:, 2, :].rearrange(two, b=2), ps[:, 4:6, :], ACT.Identity, scale=0.5 if half else 1.0,
                             bias=first[:, 7:8] if half else one[:]).then_inc(mod_a.done("rows"), 1)

    def mod_pe(pe, h):
        pe.wait_ge(ada_acc, h * KT + (2 * KT + 1))
        if isinstance(h, int):
            pe.wait_ge(x_ready, 6 * 16 + 16)
        else:
            pe.wait_ge(ln_v.sem, ln_v.at("gated", h - 1))
        for b in range(6):
            last = nc.tensor.matmul(ps[:, b, :], ONES, ada[:, b * 512:(b + 1) * 512], start=True, stop=True)
        last.then_inc(mod_t, 1)

    def mixer2_sp(sp, B, l):
        bias_sp(sp, l * 3 + 3, bass.ds(l * 3 + 2, 1))
        for n in range(IN2 + WO):
            name, i = ("w_in_2", n) if n < IN2 else ("w_out_2", n - IN2)
            mixer_load(sp, B, ENDS2, n, t[name][bass.ds(l, 1), i:i + 1, :, :].rearrange("l i p n -> p (l i n)"))
            if n < KT:
                chunk_sp(sp, l * 3 + 3, bass.ds(l * 3 + 2, 1), n)

    def mixer2_pe(pe, B, l, g):
        def after(S, name):
            pe.wait_ge(S.sem, S.at(name, l))

        pre_done(pe, g)
        for n in range(IN2):
            pe.wait_ge(proj_evac, l * IN2 + (DEPTH * IN1 + n + 1))
            for j, half_ in mixer_units(ENDS2, n):
                (feature_unit if n in (4, 5) else token_unit)(pe, B, j, j % UBUF, 4 + n % 4, half_)
            if n == 10:
                after(V2, "rf2")
                for c in range(8):
                    for tile in range(TILES):
                        o = (c % 2) * SEQ + tile * P
                        last = nc.tensor.transpose(ps[:, c // 2, o:o + P], rot[:, tile, c * P:(c + 1) * P], IDENT)
                last.then_inc(T2.done("qkt"), 1)

        def head(h):
            return slice(64 * (h % 2), 64 * (h % 2) + 64)

        after(A2, "rqk")
        for h in range(H):
            last = scores_T(h, rqk[head(h), 2 + h // 2, :], rqk[head(h), h // 2, :], h)
        last.then_inc(T2.done("sc_r"), 1)
        pe.wait_ge(proj_evac, l * IN2 + (DEPTH * IN1 + IN2 + 4))
        for h in range(H):
            last = scores_T(4 + h, sqk[head(h), 2 + h // 2, :], sqk[head(h), h // 2, :], h)
        last.then_inc(T2.done("zt"), 1)
        after(V2, "w_r")
        for h in range(H):
            q_, k_ = rqk[head(h), 4 + h // 2, :], rqk[head(h), 6 + h // 2, :]
            nc.tensor.matmul(ps[:, h, 0:P], q_[:, 0:P], k_[:, 0:P], start=True, stop=True)
            last = nc.tensor.matmul(ps[:, h, P:384], q_[:, P:SEQ], k_, start=True, stop=True)
        last.then_inc(T2.done("sc_d"), 1)
        after(V2, "mask_d")
        for h in range(H):
            c = slice(h * P, (h + 1) * P)
            last = weighted_values(ps[:, 0, c], ps[:, 1, c], b1[:, h, :], v_r[:, 0, c], v_r[:, 1, c])
        last.then_inc(T2.done("o_r"), 1)
        after(G2, "keep")
        after(V2, "t_b")
        for h in range(H):
            nc.tensor.matmul(ps[:, 4 + h, 0:384], SL, b3[:, h, :], start=True, stop=False)
            last = nc.tensor.matmul(ps[:, 4 + h, P:SEQ], ONES, b3[:, h, SEQ:384], start=False, stop=True)
        last.then_inc(T2.done("between"), 1)
        after(V2, "norm_r")
        after(V2, "cnt_d")
        for h in range(H):
            for b in range(3):
                last = nc.tensor.transpose(ps[:, h, b * P:(b + 1) * P], b2[:, h, b * P:(b + 1) * P], IDENT)
        last.then_inc(T2.done("trans_d"), 1)
        after(A2, "pT")
        for h in range(H):
            c = slice(h * 64, (h + 1) * 64)
            last = weighted_values(ps[:, 0, c], ps[:, 0, SEQ + h * 64:SEQ + (h + 1) * 64], b1[:, h, :],
                                   v_2[:, 0, c], v_2[:, 1, c])
        last.then_inc(T2.done("o_d"), 1)
        after(G2, "a")
        for h in range(H):
            c = slice(h * 64, (h + 1) * 64)
            last = weighted_values(ps[:, 5, c], ps[:, 5, SEQ + h * 64:SEQ + (h + 1) * 64], b4[:, h, :],
                                   v_b[:, 0, c], v_b[:, 1, c])
        last.then_inc(T2.done("o_b"), 1)
        after(V2, "o_d")
        after(A2, "o_b")
        after(V2, "gated")
        transposes_pe(0)
        transposes_pe(1).then_inc(T2.done("trans"), 1)
        after(V2, "lo1")
        out_product(pe, B, ENDS2, IN2)

    def mixer2_act(a, B, loads, l):
        def after(S, name):
            a.wait_ge(S.sem, S.at(name, l))

        for n in range(IN2):
            if n == 0:
                mixer_hi(a, B, ENDS2, 0, loads)
            mixer_hi(a, B, ENDS2, n + 1, loads)
            a.wait_ge(unit_done, B + (ENDS2[n] + CREDIT))
            two = ps[:, 4 + n % 4, :].rearrange("p (a b) -> p a b", a=2)
            if n < 4:
                last = nc.scalar.activation(rot_in[:, :, n * SEQ:(n + 1) * SEQ], two, ACT.Copy)
            elif n < 6:
                last = nc.scalar.activation(sqk[:, 2 * (n - 4):2 * (n - 4) + 2, :], two, ACT.Copy,
                                            scale=64.0 ** -0.5 if n == 4 else 1.0)
            elif n < 8:
                last = nc.scalar.activation(v_r[:, :, (n - 6) * SEQ:(n - 5) * SEQ], two, ACT.Copy)
            elif n < 10:
                last = nc.scalar.activation(g_r[:, :, (n - 8) * SEQ:(n - 7) * SEQ], two, ACT.Silu)
            else:
                last = nc.scalar.activation(v_2 if n == 10 else v_b, two, ACT.Copy)
            last.then_inc(proj_evac, 1)
            if n == 10:
                after(T2, "qkt")
                nc.scalar.activation(rqk.rearrange("p (a i) n -> p a (i n)", a=4), ps[:, 0:4, :],
                                     ACT.Copy).then_inc(A2.done("rqk"), 1)
        after(T2, "zt")
        nc.scalar.activation(b3, ps[:, 4:8, 0:384], ACT.Abs).then_inc(A2.done("abs_b"), 1)
        after(A2, "abs_b")
        nc.scalar.activation(b3, b3, ACT.Exp, scale=-1.0).then_inc(A2.done("e_b"), 1)
        after(A2, "e_b")
        nc.scalar.activation(b3, b3, ACT.Ln, bias=one[:, 0:1]).then_inc(A2.done("l_b"), 1)
        after(V2, "sub_d")
        nc.scalar.activation(b2, b2, ACT.Exp, scale=64.0 ** -0.5).then_inc(A2.done("exp_d"), 1)
        after(V2, "var_r")
        nc.scalar.activation(rstd8, rstd8, ACT.Sqrt).then_inc(A2.done("root_r"), 1)
        after(T2, "trans_d")
        nc.scalar.activation(b1, ps[:, 0:4, 0:384], ACT.Copy).then_inc(A2.done("pT"), 1)
        after(V2, "exp_arg")
        nc.scalar.activation(b4, b4, ACT.Exp).then_inc(A2.done("exp_b"), 1)
        after(T2, "o_b")
        nc.scalar.activation(mix[:, :, 768:D], ps[:, 5, :].rearrange("p (a b) -> p a b", a=2),
                             ACT.Copy).then_inc(A2.done("o_b"), 1)
        after(T2, "trans")
        for i in range(2):
            split_hi(a, i, A2)
        for n in range(IN2 + 1, IN2 + WO):
            mixer_hi(a, B, ENDS2, n, loads)

    def mixer2_dve(v, B, l):
        def after(S, name):
            v.wait_ge(S.sem, S.at(name, l))

        def rotate_q_k(tile):
            s_ = rot_in[:, tile, :].rearrange("p (k h z n) -> p k h z n", k=2, h=8, z=2)
            d_ = rot[:, tile, :].rearrange("p (k h z n) -> p k h z n", k=2, h=8, z=2)
            rotate(V2, after, tile + 1, (s_[:, :, :, 0, :], s_[:, :, :, 1, :]), (d_[:, :, :, 0, :], d_[:, :, :, 1, :]),
                   over(ROT[:, 0, tile, :, :], [P, 2, 8, 32], 2), over(ROT[:, 1, tile, :, :], [P, 2, 8, 32], 2),
                   half[:, tile, :].rearrange("p (k h n) -> p k h n", k=2, h=8))

        mixer_lo(v, B, ENDS2, 0)
        for n in range(IN2):
            mixer_lo(v, B, ENDS2, n + 1)
            if n < KT:
                chunk_dve(v, l * 3 + 3, n)
            if n in (8, 9):
                v.wait_ge(proj_evac, l * IN2 + (DEPTH * IN1 + 4 + 4))
                rotate_q_k(n - 8)
        after(T2, "sc_r")
        nc.vector.tensor_tensor(b1, ps[:, 0:4, 0:384], RET, ALU.mult).then_inc(V2.done("w_r"), 1)
        part = (slice(0, P), slice(P, 384))
        after(T2, "sc_d")
        nc.vector.tensor_tensor(b2, ps[:, 0:4, 0:384], over(NEGC, [P, H, 384], 1), ALU.add).then_inc(V2.done("mask_d"), 1)
        after(V2, "mask_d")
        for tile in range(TILES):
            last = nc.vector.reduce_max(max2[:, tile, :], b2[:, :, part[tile]], AX)
        last.then_inc(V2.done("max_d"), 1)
        after(V2, "max_d")
        for tile in range(TILES):
            w = P if tile == 0 else SEQ
            last = nc.vector.tensor_tensor(b2[:, :, part[tile]], b2[:, :, part[tile]],
                                           over(max2[:, tile, :], [P, H, w], 2), ALU.subtract)
        last.then_inc(V2.done("sub_d"), 1)
        after(T2, "o_r")
        for i in range(8):
            last = nc.vector.bn_stats(bn8[:, i, :], ps[:, i // 4, (i % 4) * P:(i % 4 + 1) * P])
        last.then_inc(V2.done("stats_r"), 1)
        after(V2, "stats_r")
        settle(v)
        for i in range(8):
            last = nc.vector.bn_aggr(mv8[:, i, :], bn8[:, i, :])
        last.then_inc(V2.done("aggr_r"), 1)
        after(V2, "aggr_r")
        nc.vector.tensor_scalar(rstd8, mv8[:, :, 1], EPS, None, ALU.add).then_inc(V2.done("var_r"), 1)
        after(A2, "l_b")
        nc.vector.scalar_tensor_tensor(b3, ps[:, 4:8, 0:384], 0.0, b3, ALU.max, ALU.add).then_inc(V2.done("sp_b"), 1)
        after(V2, "sp_b")
        nc.vector.tensor_tensor(b4, ps[:, 4:8, 0:384], b3, ALU.subtract).then_inc(V2.done("t_b"), 1)
        after(A2, "root_r")
        nc.vector.reciprocal(rstd8, rstd8).then_inc(V2.done("rstd_r"), 1)
        after(V2, "rstd_r")
        for i in range(8):
            last = nc.vector.tensor_scalar(mix[:, i // 4, (i % 4) * P:(i % 4 + 1) * P],
                                           ps[:, i // 4, (i % 4) * P:(i % 4 + 1) * P], mv8[:, i, 0:1],
                                           rstd8[:, i:i + 1], ALU.subtract, ALU.mult)
        last.then_inc(V2.done("norm_r"), 1)
        after(A2, "exp_d")
        nc.vector.tensor_tensor(b2, b2, over(CNT, [P, H, 384], 1), ALU.mult).then_inc(V2.done("cnt_d"), 1)
        after(V2, "cnt_d")
        for tile in range(TILES):
            last = nc.vector.reduce_sum(sum2[:, tile, :], b2[:, :, part[tile]], AX)
        last.then_inc(V2.done("sum_d"), 1)
        after(V2, "sum_d")
        nc.vector.reciprocal(sum2, sum2).then_inc(V2.done("rec_d"), 1)
        after(T2, "between")
        nc.vector.tensor_tensor(b4, b4, ps[:, 4:8, 0:384], ALU.subtract).then_inc(V2.done("exp_arg"), 1)
        nc.vector.tensor_tensor(mix[:, :, 0:512], mix[:, :, 0:512], g_r, ALU.mult).then_inc(V2.done("gated"), 1)
        after(V2, "rec_d")
        after(T2, "o_d")
        nc.vector.tensor_tensor(mix[:, :, 512:768].rearrange("p a (h d) -> p a h d", h=H),
                                ps[:, 0, :].rearrange("p (a h d) -> p a h d", a=2, h=H),
                                over(sum2, [P, TILES, H, 64], 3), ALU.mult).then_inc(V2.done("o_d"), 1)
        for i in range(2):
            split_lo(v, i, A2, l, V2)
        for n in range(IN2 + 1, IN2 + WO):
            mixer_lo(v, B, ENDS2, n)

    def mixer2_pool(p, l):
        def after(S, name):
            p.wait_ge(S.sem, S.at(name, l))

        after(V2, "t_b")
        d_ = diag(b3)
        nc.gpsimd.tensor_tensor(d_, d_, over(SU, [P, H, 2, P], 1, 1), ALU.mult).then_inc(G2.done("keep"), 1)
        after(A2, "exp_b")
        d_ = diag(b4)
        nc.gpsimd.tensor_tensor(d_, d_, over(SU, [P, H, 2, P], 1, 1), ALU.mult).then_inc(G2.done("a"), 1)

    one = sb("one", [P, 1])
    cond = sb("cond", [P, KT])
    first = sb("first", [P, 8])
    one_set = sem("one_set")
    out_sent = sem("out_sent")

    def rows_load(sp, L, pos):
        sp.dma_start(rows[:, pos % 2, :, :].rearrange("p a b -> p (a b)"),
                     t["rows"][bass.ds(L * 3 + pos, 1), :].to_broadcast([P, 2 * D])).then_inc(rows_in[pos % 2], 16)

    block = ctx.enter_context(nc.Block())

    def units1(l):
        B = l * LU1
        return B, B + FU, B + (FU + ENDS1[-1])

    def units2(l):
        B = l * LU2 + DEPTH * LU1
        return B, B + FU, B + (FU + ENDS2[-1])

    def loads1(l):
        n = l * LOADS1
        m_ = (IN1 + WO) // SLOTS
        return n, [n + NF] * 3 + [l * m_], n + (NF + m_)

    def loads2(l):
        n = l * LOADS2 + DEPTH * LOADS1
        m_ = (IN2 + WO) // SLOTS
        return n, [n + NF] * 3 + [l * m_ + DEPTH * (IN1 + WO) // SLOTS], n + (NF + m_)

    def ada_sp(sp, n, h):
        return (lambda: bias_sp(sp, n, h), lambda k: chunk_sp(sp, n, h, k))

    @block.sync
    def _(sp):
        sp.dma_start(x[:], t["x"].rearrange("(a p) d -> p a d", p=P)).then_inc(x_ready, 16)
        sp.dma_start(base[:], t["con1"][:, 0:NBASE]).then_inc(base_in, 16)
        sp.dma_start(con, t["con1"][:, NBASE:N1]).then_inc(con_in, 16)
        sp.dma_start(cond[:], t["c"][:, :]).then_inc(c_in, 16)
        with sp.Fori(0, DEPTH) as l:
            B, n = units1(l), loads1(l)
            sp.wait_ge(x_ready, l * 48 + 16)
            rows_load(sp, l, 0)
            rows_load(sp, l, 1)
            sp.dma_start(par, t["par"][bass.ds(l, 1), :].to_broadcast([P, NR])).then_inc(par_in, 16)
            sp.dma_start(fp, t["fpar"][bass.ds(l, 1), :, :].rearrange("l p n -> p (l n)")).then_inc(par_in, 16)
            ffn_sp(sp, B[0], n[0], l, t["g1"], t["u1"], t["d1"])
            mixer1_sp(sp, B[1], l)
            sp.wait_ge(x_ready, l * 48 + 32)
            rows_load(sp, l, 2)
            ffn_sp(sp, B[2], n[2], l, t["g2"], t["u2"], t["d2"], ada_sp(sp, l, slice(0, 1)))
        sp.wait_ge(x_ready, DEPTH * 48 + 16)
        sp.dma_start(con2, t["con2"][:, :]).then_inc(con_in, 16)
        with sp.Fori(0, DEPTH) as l:
            L = l + DEPTH
            B, n = units2(l), loads2(l)
            sp.wait_ge(x_ready, L * 48 + 16)
            rows_load(sp, L, 0)
            rows_load(sp, L, 1)
            ffn_sp(sp, B[0], n[0], l, t["g3"], t["u3"], t["d3"], ada_sp(sp, l * 3 + 2, bass.ds(l * 3 + 1, 1)))
            mixer2_sp(sp, B[1], l)
            sp.wait_ge(x_ready, L * 48 + 32)
            rows_load(sp, L, 2)
            ffn_sp(sp, B[2], n[2], l, t["g4"], t["u4"], t["d4"], ada_sp(sp, l * 3 + 4, bass.ds(l * 3 + 3, 1)))
        sp.wait_ge(x_ready, 12 * 16 + 16)
        sp.dma_start(out.rearrange("(a p) d -> p a d", p=P), x[:]).then_inc(out_sent, 16)
        sp.wait_ge(out_sent, 16)

    @block.tensor
    def _(pe):
        pe.wait_ge(base_in, 16)
        with pe.Fori(0, DEPTH) as l:
            g = l * 3
            B = units1(l)
            pre_pe(pe, g)
            ffn_pe(pe, B[0], l * 2, g)
            pre_pe(pe, g + 1)
            mixer1_pe(pe, B[1], l, g + 1)
            pre_pe(pe, g + 2)
            ffn_pe(pe, B[2], l * 2 + 1, g + 2)
        mod_pe(pe, 0)
        with pe.Fori(0, DEPTH) as l:
            g, h = l * 3 + 6, l * 3
            B = units2(l)
            pre_pe(pe, g)
            ffn_pe(pe, B[0], l * 2 + 4, g)
            mod_pe(pe, h + 1)
            pre_pe(pe, g + 1)
            mixer2_pe(pe, B[1], l, g + 1)
            mod_pe(pe, h + 2)
            pre_pe(pe, g + 2)
            ffn_pe(pe, B[2], l * 2 + 5, g + 2)
            mod_pe(pe, h + 3)

    @block.scalar
    def _(a):
        a.wait_ge(one_set, 2)
        a.wait_ge(c_in, 16)
        nc.scalar.activation(cond[:], cond[:], ACT.Silu).then_inc(cond_done, 1)
        with a.Fori(0, DEPTH) as l:
            g = l * 3
            B, n = units1(l), loads1(l)
            pre_act(a, g, True)
            ffn_act(a, B[0], n[0], l * 2)
            post_act(a, g, ffn_end(B[0]))
            pre_act(a, g + 1, True)
            mixer1_act(a, B[1], n[1], l)
            post_act(a, g + 1, (unit_done, B[2] + CREDIT))
            pre_act(a, g + 2, True)
            ffn_act(a, B[2], n[2], l * 2 + 1)
            post_act(a, g + 2, ffn_end(B[2]))
        mod_act(a, 0, True)
        with a.Fori(0, DEPTH) as l:
            g, h = l * 3 + 6, l * 3
            B, n = units2(l), loads2(l)
            pre_act(a, g, False)
            ffn_act(a, B[0], n[0], l * 2 + 4)
            ln_act(a, h)
            mod_act(a, h + 1, False)
            pre_act(a, g + 1, False)
            mixer2_act(a, B[1], n[1], l)
            ln_act(a, h + 1)
            mod_act(a, h + 2, True)
            pre_act(a, g + 2, False)
            ffn_act(a, B[2], n[2], l * 2 + 5)
            ln_act(a, h + 2)
            mod_act(a, h + 3, True)

    @block.vector
    def _(v):
        nc.vector.memset(zero[:], 0.0).then_inc(zero_set, 1)
        nc.vector.memset(one[:], 1.0).then_inc(one_set, 1)
        nc.vector.memset(first[:, 7:8], 0.5).then_inc(one_set, 1)
        nc.vector.memset(v_m[:, :, :, 64:65], 1.0).then_inc(ones_set, 1)
        for i, (credit, n) in enumerate(((unit_lo, CREDIT), (unit_done, CREDIT), (silu_done, 1), (act_ready, 1),
                                         (proj_evac, 4), (ada_acc, 1))):
            nc.vector.memset(first[:, i:i + 1], 0.0).then_inc(credit, n)
        v.wait_ge(cond_done, 1)
        with v.Fori(0, DEPTH) as l:
            g = l * 3
            B = units1(l)
            pre_dve(v, l, 0, True)
            ffn_dve(v, B[0], l * 2)
            post_dve(v, g, 0, 0.5, ffn_end(B[0]))
            pre_dve(v, l, 1, True)
            mixer1_dve(v, B[1], l)
            post_dve(v, g + 1, 1, 1.0, (unit_done, B[2] + CREDIT))
            pre_dve(v, l, 2, True)
            ffn_dve(v, B[2], l * 2 + 1, lambda k: chunk_dve(v, l, k))
            post_dve(v, g + 2, 2, 0.5, ffn_end(B[2]))
        v.wait_ge(con_in, 32)
        with v.Fori(0, DEPTH) as l:
            L = l + DEPTH
            h = l * 3
            B = units2(l)
            pre_dve(v, L, 0, False)
            ffn_dve(v, B[0], l * 2 + 4, lambda k: chunk_dve(v, h + 2, k))
            ln_dve(v, h, 0, ffn_end(B[0]), mrow[:, 2, :])
            pre_dve(v, L, 1, False)
            mixer2_dve(v, B[1], l)
            ln_dve(v, h + 1, 1, (unit_done, B[2] + CREDIT), mrow[:, 2, :])
            pre_dve(v, L, 2, False)
            ffn_dve(v, B[2], l * 2 + 5, lambda k: chunk_dve(v, h + 4, k))
            ln_dve(v, h + 2, 2, ffn_end(B[2]), mrow[:, 2, :])

    @block.gpsimd
    def _(p):
        with p.Fori(0, DEPTH) as l:
            mixer1_pool(p, l)
            p.wait_ge(x_ready, l * 48 + 48)
            zero_pool(p)
        with p.Fori(0, DEPTH) as l:
            h = l * 3
            p.wait_ge(mod_t, h + 1)
            zero_pool(p)
            p.wait_ge(mod_t, h + 2)
            zero_pool(p)
            mixer2_pool(p, l)
            p.wait_ge(mod_t, h + 3)
            zero_pool(p)

    ctx.close()


def tables():
    f32 = np.float32
    i = np.arange(P)
    k, n = i[:, None], i[None, :]
    con = np.zeros((P, N1), f32)
    con[:, C_IDENT:C_IDENT + P] = k == n
    con[:, C_TRIU:C_TRIU + P] = k <= n
    con[:, C_ONES:C_ONES + P] = 1
    con[:, C_SU:C_SU + P] = k < n
    con[:, C_BLOCK:C_BLOCK + P] = k // 64 == n // 64
    for j in range(7):
        s = 1 << j
        pair = (k // (2 * s) == n // (2 * s)) & (n // s % 2 == 1) & (k // s % 2 == 0)
        con[:, C_MT + j * P:C_MT + (j + 1) * P] = pair if j == 0 else pair.T
    con[:, C_NEGM:C_NEGM + P] = np.where(n > k, NEG, 0)
    key = np.arange(SEQ)[None, :]
    negd = [np.where(key // 64 > (k + tile * P) // 64, NEG, 0) for tile in range(TILES)]
    con[:, C_NEGD:C_NEGD + 384] = np.concatenate([negd[0][:, :P], negd[1]], 1)
    con[:, C_SGN:C_SGN + 12] = [1] * 8 + [-1] * 4

    def angles(freq):
        a = np.arange(SEQ, dtype=f32)[:, None] * freq[None, :]
        return np.cos(a).astype(f32), np.sin(a).astype(f32)

    def tiled(a):
        return a.reshape(TILES, P, -1).transpose(1, 0, 2)

    c, s = angles((f32(10000.0) ** (-np.arange(0, 32, 2, dtype=f32) / f32(32))).astype(f32))
    con[:, C_ROPE:C_ROPE + 32] = tiled(c).reshape(P, -1)
    con[:, C_ROPE + 32:C_ROPE + 64] = tiled(s).reshape(P, -1)

    con2 = np.zeros((P, N2), f32)
    con2[:, C2_SL:C2_SL + P] = k > n
    tq = k + np.array([0, P])[:, None, None]
    dist = tq - key[None]
    cnt = sum(((dist >= 0) & (dist % dl == 0) & (dist <= w)).astype(f32)
              for w, dl in ((128, 1), (512, 4), (2048, 16)))
    cnt = np.concatenate([cnt[0][:, :P], cnt[1]], 1)
    con2[:, C2_CNT:C2_CNT + 384] = cnt
    con2[:, C2_NEGC:C2_NEGC + 384] = np.where(cnt > 0, 0, NEG)
    lg = np.log1p(-np.exp2(-5.0 - np.arange(H)))
    d0 = key - k
    dd = np.concatenate([d0, d0[:, :P]], 1)
    ret = np.where(dd >= 0, np.exp(lg[:, None, None] * np.maximum(dd, 0)), 0) * 64.0 ** -0.5
    con2[:, C2_RET:C2_RET + H * 384] = ret.transpose(1, 0, 2).reshape(P, -1)
    rf = (1.0 / f32(10000.0) ** np.linspace(0.0, 1.0, 32, dtype=f32)).astype(f32)
    pf = (1.0 / f32(10000.0) ** (np.arange(0, 64, 2, dtype=f32) / f32(64))).astype(f32)
    kinds = [angles(rf), angles(pf)]
    rot = np.stack([np.stack([tiled(kd[z]) for kd in kinds], 2) for z in range(2)], 1)
    con2[:, C2_ROT:C2_ROT + 256] = rot.reshape(P, -1)
    return con, con2


def column_tiles(w, width=FB):
    L_, k, n = w.shape
    return np.ascontiguousarray(w.reshape(L_, k // P, P, n // width, width).transpose(0, 3, 2, 1, 4)
                                .reshape(L_, n // width, P, -1))


def row_tiles(w):
    L_, k, n = w.shape
    return np.ascontiguousarray(w.reshape(L_, k // 256, 2, P, n).transpose(0, 1, 3, 2, 4).reshape(L_, k // 256, P, -1))


def layout(i):
    con, con2 = tables()
    a = {"x": i["x"][0], "con1": con, "con2": con2}
    for n, (s, sfx) in enumerate((("ffn1", ""), ("ffn2", ""), ("ffn1", "_2"), ("ffn2", "_2"))):
        a[f"g{n + 1}"] = column_tiles(i[f"{s}_w_gate{sfx}"])
        a[f"u{n + 1}"] = column_tiles(i[f"{s}_w_up{sfx}"])
        a[f"d{n + 1}"] = row_tiles(i[f"{s}_w_down{sfx}"])
    w = i["w_in"]
    big = [0, 256, 512, 2056, 2312, 2568, 1032, 1288, 1544, 2828, 3084, 3340, 3596, 1800, 768]
    a["w_in"] = column_tiles(np.concatenate([w[:, :, c:c + 256] for c in big], 2))
    ws = np.concatenate([w[:, :, 1024:1028], w[:, :, 3852:3856], w[:, :, 1028:1032], w[:, :, 2824:2828],
                         w[:, :, 3856:3860]], 2)
    a["w_small"] = column_tiles(ws, SMALL)[:, 0]
    a["w_out"] = row_tiles(i["w_out"])
    w = i["w_in_2"]
    a["w_in_2"] = column_tiles(np.concatenate([w[:, :, c:c + 256] for c in
                                               (0, 256, 1536, 1792, 2304, 2560, 512, 768, 1024, 1280, 2048, 2816)], 2))
    a["w_out_2"] = row_tiles(i["w_out_2"])
    ada = i["w_ada_2"].reshape(DEPTH, KT, P, 3, 3 * D).transpose(0, 3, 1, 2, 4).reshape(DEPTH * 3, KT, P, 3 * D)
    a["w_ada"] = np.concatenate([ada, ada[-1:]])
    bias = i["b_ada_2"].reshape(DEPTH * 3, 3 * D)
    a["b_ada"] = np.concatenate([bias, bias[-1:]])
    a["c"] = np.ascontiguousarray(i["c_2"].reshape(KT, P).T)
    r1 = np.stack([np.stack([i[f"{s}_pre_g"], i[f"{s}_post_g"]], 1) for s in ("ffn1", "mix", "ffn2")], 1)
    r2 = np.stack([i["ln_gain_2"], i["ln_bias_2"]], 2)
    a["rows"] = np.concatenate([r1, r2]).reshape(4 * 3, 2 * D)
    zeros = np.zeros((DEPTH, H), np.float32)
    li = np.array([[0.8 - 0.6 * np.exp(-0.3 * l)] for l in range(DEPTH)])
    one_less = (1.0 - li).astype(np.float32)
    tile4 = lambda v: np.concatenate([v] * H, 1)
    a["par"] = np.concatenate([
        i["gdn_dt_bias"], i["ssd_dt_bias"], i["mlstm_f_bias"], i["gdn_a_log"], i["ssd_a_log"], zeros,
        i["mlstm_i_bias"], i["ssd_d"], i["diff_lam_q1"], i["diff_lam_k1"], i["diff_lam_q2"], i["diff_lam_k2"],
        li.astype(np.float32), one_less,
        tile4(i["gdn_norm_g"]), tile4(i["diff_norm_g"]), i["ssd_norm_g"], i["mlstm_norm_g"]], 1)
    taps = np.concatenate([i["gdn_conv_w"], i["ssd_conv_w"]], 2).reshape(DEPTH, 4, 12, P).transpose(0, 3, 2, 1)
    a["fpar"] = np.concatenate([taps.reshape(DEPTH, P, 48), i["ssd_conv_b"].reshape(DEPTH, 6, P).transpose(0, 2, 1)], 2)
    return {k: np.ascontiguousarray(v, dtype=np.float32) for k, v in a.items()}


def kernel(**inputs):
    import concourse.bacc as _bacc
    from concourse.bass_utils import run_bass_kernel_spmd as _run

    arrays = layout({k: np.asarray(v) for k, v in inputs.items()})
    nc = _bacc.Bacc("TRN2", target_bir_lowering=False, num_devices=1)
    t = {k: nc.dram_tensor(f"in_{k}", v.shape, F32, kind="ExternalInput").ap() for k, v in arrays.items()}
    out = nc.dram_tensor("out", (SEQ, D), F32, kind="ExternalOutput").ap()
    build(nc, t, out)
    r = _run(nc, [{f"in_{k}": v for k, v in arrays.items()}], core_ids=[0])
    return r.results[0]["out"].reshape(1, SEQ, D)
```
